# Optimizing a Trainium2 kernel written in Bass

```python
import jax, jax.numpy as jnp
from jax import lax
import numpy as np
import math

D_MODEL = 1024
BATCH = 1
SEQ = 2048
DEPTH = 1

N_META = 16
GRID_W = 64
HEAD_DIM = 64
N_Q_HEADS = 8
N_KV_HEADS = 2
GQA_GROUP = N_Q_HEADS // N_KV_HEADS
ATTN_WIDTH = N_Q_HEADS * HEAD_DIM
KV_WIDTH = N_KV_HEADS * HEAD_DIM
FOURIER_GROUPS = 8
FOURIER_GROUP_DIM = 64
FOURIER_WIDTH = FOURIER_GROUPS * FOURIER_GROUP_DIM
MIX_WIDTH = FOURIER_WIDTH + ATTN_WIDTH
IN_WIDTH = 2 * FOURIER_WIDTH + ATTN_WIDTH + 2 * KV_WIDTH + ATTN_WIDTH
SPLIT_POINTS = (FOURIER_WIDTH, 2 * FOURIER_WIDTH, 2 * FOURIER_WIDTH + ATTN_WIDTH,
                2 * FOURIER_WIDTH + ATTN_WIDTH + KV_WIDTH,
                2 * FOURIER_WIDTH + ATTN_WIDTH + 2 * KV_WIDTH)
Q_BLOCK = 128
ROPE_THETA = 10000.0
AXIS_ROT_DIM = HEAD_DIM // 2
AXIS_N_FREQ = AXIS_ROT_DIM // 2
EPS = 1e-6


def rmsnorm(x, g):
    xf = x.astype(jnp.float32)
    y = xf * lax.rsqrt(jnp.mean(xf * xf, axis=-1, keepdims=True) + EPS)
    return (y * g.astype(jnp.float32)).astype(x.dtype)

def axial_rope_tables(n_tok):
    rows = n_tok // GRID_W
    j = jnp.arange(n_tok, dtype=jnp.int32)
    row = (j // GRID_W - rows // 2).astype(jnp.float32)
    col = (j % GRID_W - GRID_W // 2).astype(jnp.float32)
    freqs = 1.0 / (ROPE_THETA ** (jnp.arange(AXIS_N_FREQ, dtype=jnp.float32) * 2.0 / AXIS_ROT_DIM))
    ang = jnp.concatenate([row[:, None] * freqs, col[:, None] * freqs], axis=-1)
    ang = jnp.concatenate([jnp.zeros((N_META, HEAD_DIM // 2), jnp.float32), ang], axis=0)
    return jnp.cos(ang), jnp.sin(ang)

def apply_rope(x, cos, sin):
    b, h, l, d = x.shape
    xf = x.astype(jnp.float32).reshape(b, h, l, d // 2, 2)
    x0, x1 = xf[..., 0], xf[..., 1]
    out = jnp.stack([x0 * cos - x1 * sin, x0 * sin + x1 * cos], axis=-1)
    return out.reshape(b, h, l, d).astype(x.dtype)

def gqa_block(q_blk, k, v):
    s = jnp.einsum('bkgqd,bksd->bkgqs', q_blk, k).astype(jnp.float32) * (HEAD_DIM ** -0.5)
    p = jax.nn.softmax(s, axis=-1)
    return jnp.einsum('bkgqs,bksd->bkgqd', p.astype(v.dtype), v)

def fourier_branch(f_in, w_fmix, b_fmix):
    b, l, _ = f_in.shape
    f = f_in.reshape(b, l, FOURIER_GROUPS, FOURIER_GROUP_DIM).astype(jnp.float32)
    fr = jnp.real(jnp.fft.fftn(f, axes=(1, 3), norm='ortho')).astype(f_in.dtype)
    out = jnp.einsum('blgc,gcd->blgd', fr, w_fmix) + b_fmix
    return out.reshape(b, l, FOURIER_WIDTH)

def attention_branch(q, k, v, q_g, k_g, cos, sin, n_tok):
    b, l, _ = q.shape
    q = q.reshape(b, l, N_Q_HEADS, HEAD_DIM).transpose(0, 2, 1, 3)
    k = k.reshape(b, l, N_KV_HEADS, HEAD_DIM).transpose(0, 2, 1, 3)
    v = v.reshape(b, l, N_KV_HEADS, HEAD_DIM).transpose(0, 2, 1, 3)
    q = apply_rope(rmsnorm(q, q_g), cos, sin)
    k = apply_rope(rmsnorm(k, k_g), cos, sin)
    q = q.reshape(b, N_KV_HEADS, GQA_GROUP, l, HEAD_DIM)
    out_meta = gqa_block(q[:, :, :, :N_META], k, v)
    n_blk = n_tok // Q_BLOCK
    q_real = q[:, :, :, N_META:].reshape(b, N_KV_HEADS, GQA_GROUP, n_blk, Q_BLOCK, HEAD_DIM)
    q_real = q_real.transpose(3, 0, 1, 2, 4, 5)
    out_real = lax.map(lambda qb: gqa_block(qb, k, v), q_real)
    out_real = out_real.transpose(1, 2, 3, 0, 4, 5).reshape(b, N_KV_HEADS, GQA_GROUP, n_tok, HEAD_DIM)
    out = jnp.concatenate([out_meta, out_real], axis=3).reshape(b, N_Q_HEADS, l, HEAD_DIM)
    return out.transpose(0, 2, 1, 3).reshape(b, l, ATTN_WIDTH)

def first_inputs(seed: int = 0) -> dict:
    key = jax.random.key(seed)
    ks = jax.random.split(key, 10)
    f32 = jnp.float32
    x = jax.random.normal(ks[0], (BATCH, SEQ, D_MODEL), f32)
    meta_tokens = jax.random.normal(ks[1], (N_META, D_MODEL), f32)
    norm_g = 1.0 + 0.05 * jax.random.normal(ks[2], (DEPTH, D_MODEL), f32)
    w_in = jax.random.normal(ks[3], (DEPTH, D_MODEL, IN_WIDTH), f32) * D_MODEL ** -0.5
    w_fmix = jax.random.normal(ks[4], (DEPTH, FOURIER_GROUPS, FOURIER_GROUP_DIM, FOURIER_GROUP_DIM), f32) * FOURIER_GROUP_DIM ** -0.5
    b_fmix = 0.02 * jax.random.normal(ks[5], (DEPTH, FOURIER_GROUPS, FOURIER_GROUP_DIM), f32)
    q_norm_g = 1.0 + 0.05 * jax.random.normal(ks[6], (DEPTH, HEAD_DIM), f32)
    k_norm_g = 1.0 + 0.05 * jax.random.normal(ks[7], (DEPTH, HEAD_DIM), f32)
    w_out = jax.random.normal(ks[8], (DEPTH, MIX_WIDTH, D_MODEL), f32) * MIX_WIDTH ** -0.5
    final_g = 1.0 + 0.05 * jax.random.normal(ks[9], (D_MODEL,), f32)
    return {"x": x, "meta_tokens": meta_tokens, "norm_g": norm_g, "w_in": w_in,
            "w_fmix": w_fmix, "b_fmix": b_fmix, "q_norm_g": q_norm_g, "k_norm_g": k_norm_g,
            "w_out": w_out, "final_g": final_g}

def first_block(x, meta_tokens, norm_g, w_in, w_fmix, b_fmix, q_norm_g, k_norm_g, w_out, final_g):
    b, n_tok, d = x.shape
    cos, sin = axial_rope_tables(n_tok)
    meta = jnp.broadcast_to(meta_tokens.astype(x.dtype)[None], (b, N_META, d))
    h = jnp.concatenate([meta, x], axis=1)
    for i in range(DEPTH):
        u = rmsnorm(h, norm_g[i])
        proj = jnp.einsum('bld,de->ble', u, w_in[i])
        f_in, f_gate, q, k, v, a_gate = jnp.split(proj, SPLIT_POINTS, axis=-1)
        f_out = fourier_branch(f_in, w_fmix[i], b_fmix[i]) * jax.nn.silu(f_gate)
        a_out = attention_branch(q, k, v, q_norm_g[i], k_norm_g[i], cos, sin, n_tok) * jax.nn.silu(a_gate)
        mixed = jnp.concatenate([f_out, a_out], axis=-1)
        h = h + jnp.einsum('ble,ed->bld', mixed, w_out[i])
    h = rmsnorm(h, final_g)
    return h[:, N_META:]


CHUNK = 64
QBLK = 128
P_DIM = 256
MLA_HEADS = 8
Q_LORA = 256
KV_LORA = 128
NOPE_D = 64
ROPE_D = 32
V_D = 64
ML_HEADS = 4
ML_HD = 128
ML_W = ML_HEADS * ML_HD
CONV_K = 4
MIX_W = MLA_HEADS * V_D + ML_W
IN_W = Q_LORA + KV_LORA + ROPE_D + ML_W + ML_W + ML_HEADS + ML_HEADS
N_GROUPS = 4
EXPERTS_PER_GROUP = 8
N_EXPERTS = N_GROUPS * EXPERTS_PER_GROUP
TOP_K = 2
D_EXPERT = 256
MOE_BLK = 128


def _rmsnorm(x, g):
    xf = x.astype(jnp.float32)
    r = lax.rsqrt(jnp.mean(xf * xf, axis=-1, keepdims=True) + EPS)
    return (xf * r * g.astype(jnp.float32)).astype(x.dtype)

def _split_in(proj):
    sizes = (Q_LORA, KV_LORA, ROPE_D, ML_W, ML_W, ML_HEADS, ML_HEADS)
    offs = np.cumsum(sizes)[:-1].tolist()
    return jnp.split(proj, offs, axis=-1)

def _rope_cs(positions):
    inv = 1.0 / (ROPE_THETA ** (jnp.arange(0, ROPE_D, 2, dtype=jnp.float32) / ROPE_D))
    ang = positions.astype(jnp.float32)[..., None] * inv
    return jnp.cos(ang), jnp.sin(ang)

def _apply_rope(x, cos, sin):
    xf = x.astype(jnp.float32)
    x1, x2 = xf[..., :ROPE_D // 2], xf[..., ROPE_D // 2:]
    return jnp.concatenate([x1 * cos - x2 * sin, x1 * sin + x2 * cos], axis=-1).astype(x.dtype)

def _mla_attention(q_nope, q_rope, k_nope, k_rope, v):
    B, S = q_nope.shape[:2]
    nq = S // QBLK
    scale = 1.0 / math.sqrt(NOPE_D + ROPE_D)
    k_chunk = jnp.arange(S) // CHUNK

    def blocks(t):
        return t.reshape(B, nq, QBLK, MLA_HEADS, t.shape[-1]).transpose(1, 0, 3, 2, 4)

    def one(args):
        qn, qr, blk = args
        s = (jnp.einsum('bhqd,bkhd->bhqk', qn, k_nope)
             + jnp.einsum('bhqr,bkr->bhqk', qr, k_rope)).astype(jnp.float32) * scale
        q_chunk = (blk * QBLK + jnp.arange(QBLK)) // CHUNK
        mask = k_chunk[None, :] <= q_chunk[:, None]
        s = jnp.where(mask, s, -1e30)
        pr = jax.nn.softmax(s, axis=-1).astype(v.dtype)
        return jnp.einsum('bhqk,bkhv->bhqv', pr, v)

    o = lax.map(one, (blocks(q_nope), blocks(q_rope), jnp.arange(nq)))
    return o.transpose(1, 0, 3, 2, 4).reshape(B, S, MLA_HEADS * V_D)

def _causal_conv(x, w, b):
    S = x.shape[1]
    xp = jnp.pad(x, ((0, 0), (CONV_K - 1, 0), (0, 0)))
    return sum(xp[:, k:k + S] * w[k] for k in range(CONV_K)) + b

def _mlstm_chunkwise(q, k, v, i_pre, f_pre):
    B, H, S, dk = q.shape
    dv = v.shape[-1]
    L = CHUNK
    nc = S // L

    def chunks(t):
        return t.reshape(B, H, nc, L, t.shape[-1]).transpose(2, 0, 1, 3, 4).astype(jnp.float32)

    qc, kc, vc = chunks(q), chunks(k), chunks(v)
    ic = i_pre.astype(jnp.float32).reshape(B, H, nc, L).transpose(2, 0, 1, 3)
    logf = jax.nn.log_sigmoid(f_pre.astype(jnp.float32)).reshape(B, H, nc, L).transpose(2, 0, 1, 3)
    bc = jnp.cumsum(logf, axis=-1)
    tril = jnp.tril(jnp.ones((L, L), dtype=bool))

    def step(carry, inp):
        C, n, m = carry
        q_, k_, v_, i_, b_ = inp
        D = b_[..., :, None] - b_[..., None, :] + i_[..., None, :]
        D = jnp.where(tril, D, -jnp.inf)
        inter = b_ + m[..., None]
        m_t = jnp.maximum(jnp.max(D, axis=-1), inter)
        w_intra = jnp.exp(D - m_t[..., None])
        w_inter = jnp.exp(inter - m_t)
        qk = jnp.einsum('bhtd,bhsd->bhts', q_, k_) * w_intra
        num = jnp.einsum('bhts,bhsv->bhtv', qk, v_) + w_inter[..., None] * jnp.einsum('bhtd,bhdv->bhtv', q_, C)
        den = jnp.sum(qk, axis=-1) + w_inter * jnp.einsum('bhtd,bhd->bht', q_, n)
        den = jnp.maximum(jnp.abs(den), jnp.exp(-m_t))
        h = num / den[..., None]
        bL = b_[..., -1]
        w_s = bL[..., None] - b_ + i_
        m_new = jnp.maximum(bL + m, jnp.max(w_s, axis=-1))
        ws = jnp.exp(w_s - m_new[..., None])
        decay = jnp.exp(bL + m - m_new)
        C_new = decay[..., None, None] * C + jnp.einsum('bhs,bhsd,bhsv->bhdv', ws, k_, v_)
        n_new = decay[..., None] * n + jnp.einsum('bhs,bhsd->bhd', ws, k_)
        return (C_new, n_new, m_new), h

    init = (jnp.zeros((B, H, dk, dv), jnp.float32), jnp.zeros((B, H, dk), jnp.float32),
            jnp.zeros((B, H), jnp.float32))
    _, hs = lax.scan(step, init, (qc, kc, vc, ic, bc))
    return hs.transpose(1, 2, 0, 3, 4).reshape(B, H, S, dv)

def _hier_moe(h, w_rg, b_rg, w_re, b_re, w_g, w_u, w_d):
    B, S, D = h.shape
    T = B * S
    hf = h.reshape(T, D)
    g_prob = jax.nn.softmax((hf @ w_rg).astype(jnp.float32) + b_rg.astype(jnp.float32), axis=-1)
    g_top, g_idx = lax.top_k(g_prob, 1)
    e_logits = ((hf @ w_re).astype(jnp.float32) + b_re.astype(jnp.float32)).reshape(T, N_GROUPS, EXPERTS_PER_GROUP)
    e_in = jnp.take_along_axis(e_logits, g_idx[:, :, None], axis=1)[:, 0]
    e_top, e_idx = lax.top_k(jax.nn.softmax(e_in, axis=-1), TOP_K)
    wts = g_top * e_top / jnp.sum(e_top, axis=-1, keepdims=True)
    eid = g_idx * EXPERTS_PER_GROUP + e_idx
    M = T * TOP_K
    P = M + N_EXPERTS * MOE_BLK
    nb = P // MOE_BLK
    flat_e = eid.reshape(M).astype(jnp.int32)
    flat_w = wts.reshape(M)
    flat_tok = jnp.repeat(jnp.arange(T, dtype=jnp.int32), TOP_K)
    order = jnp.argsort(flat_e)
    sorted_e = flat_e[order]
    counts = jnp.zeros((N_EXPERTS,), jnp.int32).at[flat_e].add(1)
    starts = jnp.cumsum(counts) - counts
    padded = (counts + MOE_BLK - 1) // MOE_BLK * MOE_BLK
    pad_ends = jnp.cumsum(padded)
    pad_starts = pad_ends - padded
    dest = pad_starts[sorted_e] + (jnp.arange(M, dtype=jnp.int32) - starts[sorted_e])
    row_tok = jnp.full((P,), T, jnp.int32).at[dest].set(flat_tok[order])
    row_w = jnp.zeros((P,), jnp.float32).at[dest].set(flat_w[order])
    block_e = jnp.minimum(jnp.searchsorted(pad_ends, jnp.arange(nb, dtype=jnp.int32) * MOE_BLK, side='right'),
                          N_EXPERTS - 1)
    x_pad = jnp.concatenate([hf, jnp.zeros((1, D), hf.dtype)], axis=0)
    x_rows = x_pad[row_tok].reshape(nb, MOE_BLK, D)

    def expert(args):
        xb, e = args
        return (jax.nn.silu(xb @ w_g[e]) * (xb @ w_u[e])) @ w_d[e]

    y = lax.map(expert, (x_rows, block_e)).reshape(P, D)
    out = jnp.zeros((T + 1, D), jnp.float32).at[row_tok].add(y.astype(jnp.float32) * row_w[:, None])[:T]
    return out.reshape(B, S, D).astype(h.dtype)

def second_inputs(seed: int = 0) -> dict:
    key = jax.random.key(seed)
    ks = jax.random.split(key, 40)
    f32 = jnp.float32

    def nrm(k, shape, fan_in):
        return jax.random.normal(k, shape, f32) * (fan_in ** -0.5)

    def gain(k, shape):
        return 1.0 + 0.05 * jax.random.normal(k, shape, f32)

    x = jax.random.normal(ks[0], (BATCH, SEQ, D_MODEL), f32)
    p = jax.random.normal(ks[1], (DEPTH, BATCH, SEQ, P_DIM), f32)
    positions = (jax.random.randint(ks[2], (BATCH, 1), 0, 4096, dtype=jnp.int32)
                 + jnp.arange(SEQ, dtype=jnp.int32)[None, :])
    return {
        'x': x,
        'p': p,
        'positions': positions,
        'norm_mix_g': gain(ks[3], (DEPTH, D_MODEL)),
        'w_in': nrm(ks[4], (DEPTH, D_MODEL, IN_W), D_MODEL),
        'q_norm_g': gain(ks[5], (DEPTH, Q_LORA)),
        'w_uq': nrm(ks[6], (DEPTH, Q_LORA, MLA_HEADS * (NOPE_D + ROPE_D)), Q_LORA),
        'kv_norm_g': gain(ks[7], (DEPTH, KV_LORA)),
        'w_ukv': nrm(ks[8], (DEPTH, KV_LORA, MLA_HEADS * (NOPE_D + V_D)), KV_LORA),
        'conv_w': nrm(ks[9], (DEPTH, CONV_K, ML_W), CONV_K),
        'conv_b': 0.02 * jax.random.normal(ks[10], (DEPTH, ML_W), f32),
        'w_mq': nrm(ks[11], (DEPTH, ML_HEADS, ML_HD, ML_HD), ML_HD),
        'w_mk': nrm(ks[12], (DEPTH, ML_HEADS, ML_HD, ML_HD), ML_HD),
        'w_mv': nrm(ks[13], (DEPTH, ML_HEADS, ML_HD, ML_HD), ML_HD),
        'b_igate': 0.1 * jax.random.normal(ks[14], (DEPTH, ML_HEADS), f32),
        'b_fgate': jnp.linspace(3.0, 6.0, ML_HEADS, dtype=f32)[None, :] + 0.1 * jax.random.normal(ks[15], (DEPTH, ML_HEADS), f32),
        'mh_norm_g': gain(ks[16], (DEPTH, ML_W)),
        'ml_skip': gain(ks[17], (DEPTH, ML_W)),
        'w_o': nrm(ks[18], (DEPTH, MIX_W, D_MODEL), MIX_W),
        'norm_ffn_g': gain(ks[19], (DEPTH, D_MODEL)),
        'w_router_group': nrm(ks[20], (DEPTH, D_MODEL, N_GROUPS), D_MODEL),
        'b_router_group': 0.01 * jax.random.normal(ks[21], (DEPTH, N_GROUPS), f32),
        'w_router_expert': nrm(ks[22], (DEPTH, D_MODEL, N_EXPERTS), D_MODEL),
        'b_router_expert': 0.01 * jax.random.normal(ks[23], (DEPTH, N_EXPERTS), f32),
        'w_gate_e': nrm(ks[24], (DEPTH, N_EXPERTS, D_MODEL, D_EXPERT), D_MODEL),
        'w_up_e': nrm(ks[25], (DEPTH, N_EXPERTS, D_MODEL, D_EXPERT), D_MODEL),
        'w_down_e': nrm(ks[26], (DEPTH, N_EXPERTS, D_EXPERT, D_MODEL), D_EXPERT),
        'norm_ple_g': gain(ks[27], (DEPTH, D_MODEL)),
        'w_ple': nrm(ks[28], (DEPTH, P_DIM, D_MODEL), P_DIM),
        'w_ple_gate': nrm(ks[29], (DEPTH, D_MODEL, D_MODEL), D_MODEL),
        'final_norm_g': gain(ks[30], (D_MODEL,)),
    }

def second_block(x, p, positions, norm_mix_g, w_in, q_norm_g, w_uq, kv_norm_g, w_ukv, conv_w, conv_b,
              w_mq, w_mk, w_mv, b_igate, b_fgate, mh_norm_g, ml_skip, w_o, norm_ffn_g,
              w_router_group, b_router_group, w_router_expert, b_router_expert,
              w_gate_e, w_up_e, w_down_e, norm_ple_g, w_ple, w_ple_gate, final_norm_g):
    B, S, _ = x.shape
    cos, sin = _rope_cs(positions)
    for i in range(DEPTH):
        h = _rmsnorm(x, norm_mix_g[i])
        c_q, c_kv, k_r, x_m, z, i_pre, f_pre = _split_in(h @ w_in[i])
        q = (_rmsnorm(c_q, q_norm_g[i]) @ w_uq[i]).reshape(B, S, MLA_HEADS, NOPE_D + ROPE_D)
        kv = (_rmsnorm(c_kv, kv_norm_g[i]) @ w_ukv[i]).reshape(B, S, MLA_HEADS, NOPE_D + V_D)
        q_nope, q_rope = q[..., :NOPE_D], _apply_rope(q[..., NOPE_D:], cos[:, :, None], sin[:, :, None])
        k_nope, v = kv[..., :NOPE_D], kv[..., NOPE_D:]
        k_rope = _apply_rope(k_r, cos, sin)
        attn_out = _mla_attention(q_nope, q_rope, k_nope, k_rope, v)
        xc = jax.nn.silu(_causal_conv(x_m, conv_w[i], conv_b[i]))
        xch = xc.reshape(B, S, ML_HEADS, ML_HD)
        xmh = x_m.reshape(B, S, ML_HEADS, ML_HD)
        mq = jnp.einsum('bshd,hde->bhse', xch, w_mq[i])
        mk = jnp.einsum('bshd,hde->bhse', xch, w_mk[i]) * (ML_HD ** -0.5)
        mv = jnp.einsum('bshd,hde->bhse', xmh, w_mv[i])
        ig = (i_pre + b_igate[i]).transpose(0, 2, 1)
        fg = (f_pre + b_fgate[i]).transpose(0, 2, 1)
        hm = _mlstm_chunkwise(mq, mk, mv, ig, fg).transpose(0, 2, 1, 3)
        mu = jnp.mean(hm, axis=-1, keepdims=True)
        var = jnp.mean(jnp.square(hm - mu), axis=-1, keepdims=True)
        hm = ((hm - mu) * lax.rsqrt(var + EPS)).reshape(B, S, ML_W) * mh_norm_g[i].astype(jnp.float32)
        ml_out = ((hm.astype(x.dtype) + ml_skip[i] * xc) * jax.nn.silu(z)).astype(x.dtype)
        x = x + jnp.concatenate([attn_out, ml_out], axis=-1) @ w_o[i]
        x = x + _hier_moe(_rmsnorm(x, norm_ffn_g[i]), w_router_group[i], b_router_group[i],
                          w_router_expert[i], b_router_expert[i], w_gate_e[i], w_up_e[i], w_down_e[i])
        hp = _rmsnorm(x, norm_ple_g[i])
        x = x + (p[i] @ w_ple[i]) * jax.nn.sigmoid(hp @ w_ple_gate[i])
    return _rmsnorm(x, final_norm_g)


def setup_inputs(seed=0):
    out = dict(first_inputs(seed))
    for name, value in second_inputs(seed + 1).items():
        if name != "x":
            out[name + "_2"] = value
    return out


def reference(
    x, meta_tokens, norm_g, w_in, w_fmix, b_fmix, q_norm_g, k_norm_g, w_out, final_g, p_2,
    positions_2, norm_mix_g_2, w_in_2, q_norm_g_2, w_uq_2, kv_norm_g_2, w_ukv_2, conv_w_2,
    conv_b_2, w_mq_2, w_mk_2, w_mv_2, b_igate_2, b_fgate_2, mh_norm_g_2, ml_skip_2, w_o_2,
    norm_ffn_g_2, w_router_group_2, b_router_group_2, w_router_expert_2, b_router_expert_2,
    w_gate_e_2, w_up_e_2, w_down_e_2, norm_ple_g_2, w_ple_2, w_ple_gate_2, final_norm_g_2,
):
    x = first_block(
        x, meta_tokens, norm_g, w_in, w_fmix, b_fmix, q_norm_g, k_norm_g, w_out, final_g,
    )
    return second_block(
        x, p_2, positions_2, norm_mix_g_2, w_in_2, q_norm_g_2, w_uq_2, kv_norm_g_2, w_ukv_2,
        conv_w_2, conv_b_2, w_mq_2, w_mk_2, w_mv_2, b_igate_2, b_fgate_2, mh_norm_g_2,
        ml_skip_2, w_o_2, norm_ffn_g_2, w_router_group_2, b_router_group_2, w_router_expert_2,
        b_router_expert_2, w_gate_e_2, w_up_e_2, w_down_e_2, norm_ple_g_2, w_ple_2,
        w_ple_gate_2, final_norm_g_2,
    )


_drawn_inputs = setup_inputs


def setup_inputs(seed=0):
    import zlib

    import numpy as np

    out = dict(_drawn_inputs(seed))
    spreads = {}
    factors = {'b_fmix': 3.063,
     'q_norm_g': 8.0,
     'k_norm_g': 8.0,
     'q_norm_g_2': 5.097,
     'kv_norm_g_2': 4.708,
     'b_igate_2': 64.0,
     'ml_skip_2': 12.637,
     'b_router_group_2': 55.755,
     'b_router_expert_2': 23.401,
     'norm_ple_g_2': 38.911,
     'conv_b_2': 6.967,
     'mh_norm_g_2': 6.497,
     'norm_ffn_g_2': 3.478}
    for name, (base, spread) in spreads.items():
        noise = np.random.default_rng([zlib.crc32(name.encode()), seed]).standard_normal(out[name].shape)
        drawn = base * np.exp(spread * noise) if base else spread * noise
        out[name] = __import__('jax').numpy.asarray(drawn.astype(out[name].dtype))
    for name, factor in factors.items():
        out[name] = (out[name] * factor).astype(out[name].dtype)
    return out
```

```python
from contextlib import ExitStack

import numpy as np

import concourse.bass as bass
from concourse import mybir

F32 = mybir.dt.float32
BF16 = mybir.dt.bfloat16
I32 = mybir.dt.int32
U32 = mybir.dt.uint32
ALU = mybir.AluOpType
ACT = mybir.ActivationFunctionType
AX_X = mybir.AxisListType.X

P = 128
D = 1024
KD = D // P
S = 2048
NT = S // P
META = 16
L = S + META
EPS = 1e-6
HD = 64
NQ, NKV = 8, 2
NH = NQ + NKV
FW = 512
W1 = 2 * FW + NQ * HD + 2 * NKV * HD + NQ * HD
LF = L // 2
KC = 344
NC = LF // KC

QL, KVL, RD, ND, VD = 256, 128, 32, 64, 64
MH = 8
QD = ND + RD
MLH, MLD = 4, 128
ML = MLH * MLD
CONV = 4
GRP, NE, DE = 4, 32, 256
NBLK = 2 * S // P + NE
PD = 256
W2 = QL + KVL + RD + 2 * ML + 2 * MLH


class Chain:

    def __init__(self, eng, sem, base=0):
        self.eng, self.sem, self.base, self.n = eng, sem, base, 0

    def link(self, ins):
        self.n += 1
        ins.then_inc(self.sem, 1)
        self.eng.wait_ge(self.sem, self.base + self.n)

    def at(self, base):
        self.base, self.n = base, 0


class Stage:

    def __init__(self, nc, name, stack):
        self.nc, self.name, self.stack, self.sems = nc, name, stack, []
        stack.callback(self.give_back)

    def give_back(self):
        self.nc.clear_and_free_semaphores(self.sems)
        self.nc.all_engine_barrier()

    def sb(self, name, shape, dt=F32):
        return self.stack.enter_context(self.nc.sbuf_tensor(f"{self.name}_{name}", shape, dt))

    def ps(self, name, shape, dt=F32):
        return self.stack.enter_context(self.nc.psum_tensor(f"{self.name}_{name}", shape, dt))

    def sem(self, name):
        self.sems.append(self.nc.alloc_semaphore(f"{self.name}_{name}"))
        return self.sems[-1]


def rows_of(n):
    return bass.ds(n * P, P)


def ahead(eng, *values):
    return [v if isinstance(v, int) else eng.snap(eng.to_reg(v)) for v in values]


def to_all(row, *repeats):
    width = row.shape[-1]
    return bass.AP(tensor=row.tensor, offset=row.offset, ap=[[0, P], *[[0, r] for r in repeats], [1, width]])


def stage_project1(nc, d):
    with ExitStack() as stack:
        st = Stage(nc, "A", stack)
        w = st.sb("w", [P, KD, W1])
        gain = st.sb("gain", [P, KD])
        ident = st.sb("ident", [P, P])
        eps = st.sb("eps", [P, 1])
        hgain = st.sb("hgain", [P, NH, HD])
        cs = st.sb("cs", [P, 2, 2, HD // 2])
        x = st.sb("x", [P, 2, D])
        sq = st.sb("sq", [P, D])
        stat = st.sb("stat", [P, 2, 4])
        u = st.sb("u", [P, 2, D])
        uT = st.sb("uT", [P, 2, KD, P])
        hsq = st.sb("hsq", [P, NH, HD])
        hstat = st.sb("hstat", [P, 3, NH])
        hn = st.sb("hn", [P, NH, HD])
        rt = st.sb("rt", [P, 4, NH, HD // 2])
        hr = st.sb("hr", [P, NH, HD])
        hT = st.sb("hT", [P, 2, NH // 2, P])
        fin = st.sb("fin", [P, 2, FW])
        v = st.sb("v", [P, 2, NKV * HD])
        ge = st.sb("ge", [P, 2, FW])
        gs = st.sb("gs", [P, 2, 2 * FW])
        psT = st.ps("psT", [P, KD, P])
        psG = [st.ps(f"psG{g}", [P, 512]) for g in range(5)]
        FIN, FG, Q, KV, AG = range(5)
        cols = {FIN: (0, FW), FG: (FW, FW), Q: (2 * FW, FW), KV: (3 * FW, 256), AG: (3 * FW + 256, FW)}
        order = (Q, KV, FIN, FG, AG)

        w_loaded = st.sem("w_loaded")
        c_loaded = st.sem("c_loaded")
        w_scaled = st.sem("w_scaled")
        eps_set = st.sem("eps_set")
        x_loaded = [st.sem(f"x_loaded{k}") for k in range(2)]
        cs_loaded = [st.sem(f"cs_loaded{k}") for k in range(2)]
        cs_free = st.sem("cs_free")
        x_free = st.sem("x_free")
        act_step = st.sem("act_step")
        r_ready = st.sem("r_ready")
        u_ready = st.sem("u_ready")
        t_done = st.sem("t_done")
        uT_a = st.sem("uT_a")
        uT_v = st.sem("uT_v")
        g_done = [st.sem(f"g_done{g}") for g in range(5)]
        g_free = [st.sem(f"g_free{g}") for g in range(5)]
        hsq_ready = st.sem("hsq_ready")
        hss_ready = st.sem("hss_ready")
        hr_stat = st.sem("hr_stat")
        ge_ready = st.sem("ge_ready")
        ge_used = st.sem("ge_used")
        rot_ready = st.sem("rot_ready")
        hT_done = st.sem("hT_done")
        hT_ready = st.sem("hT_ready")
        fv_ready = st.sem("fv_ready")
        gs_ready = st.sem("gs_ready")
        dve_step = st.sem("dve_step")
        f_stored = [st.sem(f"f_stored{k}") for k in range(2)]
        h_stored = [st.sem(f"h_stored{k}") for k in range(2)]
        u_free = st.sem("u_free")
        g_stored = [st.sem(f"g_stored{k}") for k in range(2)]

        w_dram = d["w_in"].rearrange("a (k p) n -> p (a k) n", p=P)
        x_dram = d["x"].rearrange("a s m -> (a s) m")

        with nc.Block() as block:

            @block.sync
            def _(sp):
                sp.dma_start(ident[:], d["ident"]).then_inc(c_loaded, 16)
                sp.dma_start(gain[:], d["norm_g"].rearrange("a (k p) -> p (a k)", p=P), allow_slow_non_contiguous=True).then_inc(c_loaded, 16)
                sp.dma_start(hgain[:, 0:NQ, :], to_all(d["q_norm_g"], NQ)).then_inc(c_loaded, 16)
                sp.dma_start(hgain[:, NQ:NH, :], to_all(d["k_norm_g"], NKV)).then_inc(c_loaded, 16)
                for kd in range(KD):
                    sp.dma_start(w[:, kd], w_dram[:, kd]).then_inc(w_loaded, 16)

                def load(n, k):
                    sp.wait_ge(x_free, n + 1)
                    if isinstance(n, int) and n == NT:
                        sp.dma_start(x[0:META, k], d["meta_tokens"]).then_inc(x_loaded[k], 16)
                    else:
                        sp.dma_start(x[:, k], x_dram[rows_of(n)]).then_inc(x_loaded[k], 16)
                    sp.wait_ge(cs_free, n + 1)
                    if isinstance(n, int) and n == NT:
                        sp.dma_start(cs[0:META, k], d["rope_meta"]).then_inc(cs_loaded[k], 16)
                    else:
                        sp.dma_start(cs[:, k], d["rope"][rows_of(n)]).then_inc(cs_loaded[k], 16)

                def store(n, k, meta=False):
                    rows = META if meta else P
                    hT_count, = ahead(sp, n + 2)
                    sp.wait_ge(fv_ready, n + 1)
                    at = slice(0, META) if meta else bass.ds(n * P + META, P)
                    sp.dma_start(d["fin"][at], fin[0:rows, k]).then_inc(f_stored[k], 16)
                    at = slice(S, L) if meta else rows_of(n)
                    sp.dma_start(d["v"][at], v[0:rows, k]).then_inc(f_stored[k], 16)
                    if not meta:
                        sp.wait_ge(gs_ready, 2 * n + 2)
                    sp.wait_ge(hT_ready, hT_count)
                    if not meta:
                        sp.dma_start(d["gates"][rows_of(n)], gs[:, k]).then_inc(g_stored[k], 16)
                    sp.dma_start(d["hT"][:, at].rearrange("(j p) s -> p j s", p=P),
                                 hT[:, k, :, 0:rows]).then_inc(h_stored[k], 16)

                for n in range(2):
                    load(n, n)
                with sp.Fori(0, NT // 2 - 1) as i:
                    for k in range(2):
                        store(2 * i + k, k)
                        load(2 * i + k + 2, k)
                store(NT - 2, 0)
                load(NT, 0)
                store(NT - 1, 1)
                store(NT, 0, meta=True)
                for k in range(2):
                    sp.wait_ge(f_stored[k], 32 * (NT // 2 + 2 - k))
                    sp.wait_ge(h_stored[k], 16 * (NT // 2 + 2 - k))
                    sp.wait_ge(g_stored[k], 16 * (NT // 2 + 1))

            @block.scalar
            def _(act):
                nc.scalar.preload_act_table_set("natural_log_exp_and_others")
                chain = Chain(act, act_step)
                for k in range(2):
                    act.sem_inc(f_stored[k], 32)
                act.wait_ge(eps_set, 1)

                def stats(n, k, m):
                    act.wait_ge(x_loaded[k], 16 * m)
                    chain.link(nc.scalar.activation(sq[:], x[:, k], ACT.Square, accum_out=stat[:, k, 0:1]))
                    chain.link(nc.scalar.activation(stat[:, k, 1:2], stat[:, k, 0:1], ACT.Ln, scale=1.0 / D, bias=eps[:, 0:1]))
                    nc.scalar.activation(stat[:, k, 2:3], stat[:, k, 1:2], ACT.Exp, scale=-0.5).then_inc(r_ready, 1)

                def tile(n, k, m, m_next, meta):
                    if not meta:
                        stats(n + 1, 1 - k, m_next)
                    act.wait_ge(t_done, n + 1)
                    nc.scalar.copy(uT[:, k, KD // 2:KD], psT[:, KD // 2:KD]).then_inc(uT_a, 1)
                    act.wait_ge(g_done[KV], n + 1)
                    if not meta:
                        nc.scalar.activation(hsq[:, 0:NQ].rearrange("p h c -> p (h c)"), psG[Q][:, 0:NQ * HD], ACT.Square)
                    nc.scalar.activation(hsq[:, NQ:NH].rearrange("p h c -> p (h c)"), psG[KV][:, 0:NKV * HD],
                                         ACT.Square).then_inc(hsq_ready, 1)
                    act.wait_ge(f_stored[k], 32 * m)
                    nc.scalar.copy(v[:, k], psG[KV][:, NKV * HD:2 * NKV * HD])
                    act.wait_ge(hss_ready, n + 1)
                    chain.link(nc.scalar.activation(hstat[:, 1], hstat[:, 0], ACT.Ln, scale=1.0 / HD, bias=eps[:, 0:1]))
                    nc.scalar.activation(hstat[:, 2], hstat[:, 1], ACT.Exp, scale=-0.5).then_inc(hr_stat, 1)
                    act.wait_ge(g_done[FIN], n + 1)
                    nc.scalar.copy(fin[:, k], psG[FIN][:]).then_inc(fv_ready, 1)
                    if not meta:
                        act.wait_ge(g_done[FG], n + 1)
                        act.wait_ge(ge_used, n + 1)
                        nc.scalar.activation(ge[:, 0], psG[FG][:], ACT.Exp, scale=-1.0).then_inc(ge_ready, 1)
                        act.wait_ge(g_done[AG], n + 1)
                        nc.scalar.activation(ge[:, 1], psG[AG][:], ACT.Exp, scale=-1.0).then_inc(ge_ready, 1)

                stats(0, 0, 1)
                with act.Fori(0, NT // 2) as i:
                    for k in range(2):
                        if k == 0:
                            chain.at(i * 6 + 2)
                        tile(2 * i + k, k, i + 1, i + 1 + k, False)
                chain.at(3 * NT + 2)
                tile(NT, 0, NT // 2 + 1, 0, True)

            @block.gpsimd
            def _(pool):
                pool.sem_inc(x_free, 2)

                def tile(n, k):
                    pool.wait_ge(r_ready, n + 1)
                    pool.wait_ge(u_free, n + 1)
                    nc.gpsimd.tensor_tensor(u[:, k], x[:, k], stat[:, k, 2:3].to_broadcast([P, D]), ALU.mult).then_inc(u_ready, 1)
                    pool.wait_ge(u_ready, n + 1)
                    pool.sem_inc(x_free, 1)

                with pool.Fori(0, NT // 2) as i:
                    for k in range(2):
                        tile(2 * i + k, k)
                tile(NT, 0)

            @block.tensor
            def _(pe):
                pe.wait_ge(c_loaded, 64)
                pe.sem_inc(u_free, 2)

                def tile(n, k, meta):
                    first = isinstance(n, int) and n == 0
                    pe.wait_ge(u_ready, n + 1)
                    pe.wait_ge(hT_ready, n + 1)
                    for kd in range(KD):
                        t = nc.tensor.transpose(psT[:, kd], u[:, k, kd * P:(kd + 1) * P], ident[:])
                    t.then_inc(t_done, 1)
                    pe.wait_ge(t_done, n + 1)
                    pe.sem_inc(u_free, 1)
                    pe.wait_ge(uT_a, n + 1)
                    pe.wait_ge(uT_v, n + 1)
                    for g in (KV, FIN) if meta else order:
                        c0, width = cols[g]
                        pe.wait_ge(g_free[g], n + 1)
                        for kd in range(KD):
                            m = nc.tensor.matmul(psG[g][:, 0:width], uT[:, k, kd], w[:, kd, c0:c0 + width],
                                                 start=(kd == 0), stop=(kd == KD - 1))
                        m.then_inc(g_done[g], 1)
                    pe.wait_ge(rot_ready, n + 1)
                    for j in range(NH // 2):
                        t = nc.tensor.transpose(psT[:, j], hr[:, 2 * j:2 * j + 2].rearrange("p h c -> p (h c)"), ident[:])
                    t.then_inc(hT_done, 1)

                pe.wait_ge(w_scaled, KD)
                with pe.Fori(0, NT // 2) as i:
                    for k in range(2):
                        tile(2 * i + k, k, False)
                tile(NT, 0, True)

            @block.vector
            def _(dve):
                chain = Chain(dve, dve_step)
                for k in range(2):
                    dve.sem_inc(h_stored[k], 16)
                    dve.sem_inc(g_stored[k], 16)
                nc.vector.memset(eps[:], EPS).then_inc(eps_set, 1)
                nc.vector.memset(hsq[:], 0.0)
                dve.sem_inc(cs_free, 2)
                dve.sem_inc(hT_ready, 1)
                dve.sem_inc(ge_used, 1)
                for g in range(5):
                    dve.sem_inc(g_free[g], 1)
                dve.wait_ge(c_loaded, 64)
                nc.vector.tensor_scalar(hgain[:, 0:NQ], hgain[:, 0:NQ], HD ** -0.5, None, ALU.mult)
                dve.wait_ge(w_loaded, 16 * KD)
                for kd in range(KD):
                    nc.vector.tensor_scalar(w[:, kd], w[:, kd], gain[:, kd:kd + 1], None, ALU.mult).then_inc(w_scaled, 1)

                def tile(n, k, m, meta):
                    dve.wait_ge(t_done, n + 1)
                    nc.vector.tensor_copy(uT[:, k, 0:KD // 2], psT[:, 0:KD // 2]).then_inc(uT_v, 1)
                    dve.wait_ge(hsq_ready, n + 1)
                    nc.vector.reduce_sum(hstat[:, 0], hsq[:], AX_X).then_inc(hss_ready, 1)
                    dve.wait_ge(hr_stat, n + 1)
                    if not meta:
                        nc.vector.tensor_tensor(hn[:, 0:NQ], psG[Q][:].rearrange("p (h c) -> p h c", c=HD),
                                                hstat[:, 2, 0:NQ].unsqueeze(2).to_broadcast([P, NQ, HD]),
                                                ALU.mult).then_inc(g_free[Q], 1)
                    chain.link(nc.vector.tensor_tensor(hn[:, NQ:NH], psG[KV][:, 0:NKV * HD].rearrange("p (h c) -> p h c", c=HD),
                                                       hstat[:, 2, NQ:NH].unsqueeze(2).to_broadcast([P, NKV, HD]), ALU.mult))
                    chain.link(nc.vector.tensor_tensor(hn[:], hn[:], hgain[:], ALU.mult))
                    dve.wait_ge(fv_ready, n + 1)
                    dve.sem_inc(g_free[KV], 1)
                    dve.sem_inc(g_free[FIN], 1)
                    dve.wait_ge(cs_loaded[k], 16 * m)
                    pairs = hn[:].rearrange("p h (c two) -> p h c two", two=2)
                    outs = hr[:].rearrange("p h (c two) -> p h c two", two=2)
                    cos = cs[:, k, 0].unsqueeze(1).to_broadcast([P, NH, HD // 2])
                    sin = cs[:, k, 1].unsqueeze(1).to_broadcast([P, NH, HD // 2])
                    nc.vector.tensor_tensor(rt[:, 0], pairs[:, :, :, 0], cos, ALU.mult)
                    nc.vector.tensor_tensor(rt[:, 1], pairs[:, :, :, 1], sin, ALU.mult)
                    nc.vector.tensor_tensor(rt[:, 2], pairs[:, :, :, 0], sin, ALU.mult)
                    chain.link(nc.vector.tensor_tensor(rt[:, 3], pairs[:, :, :, 1], cos, ALU.mult))
                    dve.sem_inc(cs_free, 1)
                    dve.wait_ge(hT_done, n) if not (isinstance(n, int) and n == 0) else None
                    nc.vector.tensor_tensor(outs[:, :, :, 0], rt[:, 0], rt[:, 1], ALU.subtract)
                    nc.vector.tensor_tensor(outs[:, :, :, 1], rt[:, 2], rt[:, 3], ALU.add).then_inc(rot_ready, 1)
                    if not meta:
                        dve.wait_ge(g_stored[k], 16 * m)
                        for j, g in enumerate((FG, AG)):
                            dve.wait_ge(ge_ready, 2 * n + j + 1)
                            chain.link(nc.vector.tensor_scalar(ge[:, j], ge[:, j], 1.0, None, ALU.add))
                            chain.link(nc.vector.reciprocal(ge[:, j], ge[:, j]))
                            nc.vector.tensor_tensor(gs[:, k, j * FW:(j + 1) * FW], psG[g][:], ge[:, j],
                                                    ALU.mult).then_inc(gs_ready, 1)
                        dve.wait_ge(gs_ready, 2 * n + 2)
                        dve.sem_inc(ge_used, 1)
                        dve.sem_inc(g_free[FG], 1)
                        dve.sem_inc(g_free[AG], 1)
                    dve.wait_ge(hT_done, n + 1)
                    dve.wait_ge(h_stored[k], 16 * m)
                    nc.vector.tensor_copy(hT[:, k], psT[:, 0:NH // 2]).then_inc(hT_ready, 1)

                LINKS = 7
                with dve.Fori(0, NT // 2) as i:
                    for k in range(2):
                        if k == 0:
                            chain.at(i * (2 * LINKS))
                        tile(2 * i + k, k, i + 1, False)
                    assert chain.n == 2 * LINKS
                chain.at(LINKS * NT)
                tile(NT, 0, NT // 2 + 1, True)


def stage_fourier(nc, d):
    JT = LF // P + 1
    LAST = LF + 1 - (JT - 1) * P
    GP = FW // P
    SUB = [(0, P), (P, P), (2 * P, KC - 2 * P)]
    with ExitStack() as stack:
        st = Stage(nc, "B", stack)
        f = st.sb("f", [P, JT, FW])
        fr = st.sb("fr", [P, JT, FW])
        e = st.sb("e", [P, JT, FW])
        o = st.sb("o", [P, JT, FW])
        tab = st.sb("tab", [P, 2, JT, LF])
        back_in = st.sb("back_in", [P, JT], I32)
        back_out = st.sb("back_out", [P, NC * len(SUB)], I32)
        cdsd = st.sb("cdsd", [P, 2, P])
        wf = st.sb("wf", [P, GP, P])
        mix = st.sb("mix", [P, 2, GP, P])
        bias = st.sb("bias", [1, FW])
        ones = st.sb("ones", [1, P])
        g = st.sb("g", [P, 2, GP, KC])
        osb = st.sb("osb", [P, 2, FW])
        lo = st.sb("lo", [P, 2, FW])
        hi = st.sb("hi", [P, 2, FW])
        psG = [[st.ps(f"psG{t}{c}", [P, 512]) for c in range(GP)] for t in range(2)]

        set_done = st.sem("set_done")
        f_loaded = st.sem("f_loaded")
        r_loaded = st.sem("r_loaded")
        i_loaded = st.sem("i_loaded")
        scattered = [st.sem(f"scattered{k}") for k in range(2)]
        c_loaded = st.sem("c_loaded")
        t_loaded = [st.sem(f"t_loaded{t}") for t in range(2)]
        folded = st.sem("folded")
        mix_done = st.sem("mix_done")
        mix_ready = st.sem("mix_ready")
        g_done = st.sem("g_done")
        g_ready = st.sem("g_ready")
        s_done = st.sem("s_done")
        o_ready = st.sem("o_ready")
        out_ready = st.sem("out_ready")
        stored = [st.sem(f"stored{k}") for k in range(2)]

        with nc.Block() as block:

            @block.sync
            def _(sp):
                sp.wait_ge(set_done, 1)
                for j in range(JT):
                    n = P if j < JT - 1 else LAST
                    sp.dma_start(f[0:n, j], d["fin"][j * P:j * P + n]).then_inc(f_loaded, 16)
                sp.dma_start(cdsd[:], d["cdsd"]).then_inc(c_loaded, 16)
                for c in range(GP):
                    for h in range(2):
                        sp.dma_start(wf[h * HD:(h + 1) * HD, c, h * HD:(h + 1) * HD],
                                     d["w_fmix"][0, 2 * c + h]).then_inc(c_loaded, 16)
                sp.dma_start(bias[:], d["b_fmix"].rearrange("a g c -> a (g c)")).then_inc(c_loaded, 16)
                for n in range(NC * len(SUB)):
                    c, (s0, w) = n // len(SUB), SUB[n % len(SUB)]
                    k0 = 1 + c * KC + s0
                    sp.wait_ge(out_ready, 2 * n + 2)
                    skip = max(0, META - k0)
                    sp.dma_start(d["four"][k0 + skip - META:k0 + w - META], lo[skip:w, n % 2]).then_inc(stored[n % 2], 16)
                sp.wait_ge(stored[0], 16 * 5)
                sp.wait_ge(stored[1], 16 * 4)

            @block.gpsimd
            def _(pool):
                pool.dma_start(back_in[:], d["fourier_back_in"]).then_inc(i_loaded, 16)
                pool.dma_start(back_out[:], d["fourier_back_out"]).then_inc(i_loaded, 16)
                pool.wait_ge(i_loaded, 32)
                for j in range(JT):
                    n = P if j < JT - 1 else LAST
                    pool.indirect_dma_start(fr[0:n, j], None, d["fin"],
                                            bass.IndirectOffsetOnAxis(back_in[0:n, j:j + 1], 0)).then_inc(r_loaded, 16)
                for t, table in enumerate(("dft_cos", "dft_sin")):
                    for j in range(JT):
                        n = P if j < JT - 1 else LAST
                        pool.dma_start(tab[0:n, t, j], d[table][j * P:j * P + n]).then_inc(t_loaded[t], 16)
                for n in range(NC * len(SUB)):
                    c, (s0, w) = n // len(SUB), SUB[n % len(SUB)]
                    m = w - (c * KC + s0 + w == LF)
                    pool.wait_ge(out_ready, 2 * n + 2)
                    pool.indirect_dma_start(d["four"], bass.IndirectOffsetOnAxis(back_out[0:m, n:n + 1], 0),
                                            hi[0:m, n % 2], None).then_inc(scattered[n % 2], 16)
                pool.wait_ge(scattered[0], 16 * 5)
                pool.wait_ge(scattered[1], 16 * 4)

            @block.vector
            def _(dve):
                nc.vector.memset(wf[:], 0.0)
                nc.vector.memset(ones[:], 1.0).then_inc(set_done, 1)
                dve.wait_ge(f_loaded, 16 * JT)
                dve.wait_ge(r_loaded, 16 * JT)
                nc.vector.memset(fr[0:1, 0], 0.0).then_inc(set_done, 1)
                dve.wait_ge(set_done, 2)
                for j in range(JT):
                    n = P if j < JT - 1 else LAST
                    nc.vector.tensor_tensor(e[0:n, j], f[0:n, j], fr[0:n, j], ALU.add)
                    nc.vector.tensor_tensor(o[0:n, j], f[0:n, j], fr[0:n, j], ALU.subtract).then_inc(folded, 1)
                dve.wait_ge(mix_done, 2)
                for t in range(2):
                    nc.vector.tensor_copy(mix[:, t], psG[t][0][:].rearrange("p (c n) -> p c n", n=P)).then_inc(mix_ready, 1)
                for c in range(NC):
                    dve.wait_ge(g_done, 2 * c + 2)
                    for t in range(2):
                        for h in range(2):
                            copy = nc.vector.tensor_copy(g[:, t, h], psG[t][h][:, 0:KC])
                    copy.then_inc(g_ready, 1)
                    for s, (s0, w) in enumerate(SUB):
                        n = c * len(SUB) + s
                        dve.wait_ge(o_ready, n + 1)
                        if n >= 2:
                            dve.wait_ge(stored[n % 2], 16 * (n // 2))
                            dve.wait_ge(scattered[n % 2], 16 * (n // 2))
                        ps = psG[n % 2][0]
                        nc.vector.tensor_tensor(lo[0:w, n % 2], ps[0:w], osb[0:w, n % 2], ALU.subtract).then_inc(out_ready, 1)
                        nc.vector.tensor_tensor(hi[0:w, n % 2], ps[0:w], osb[0:w, n % 2], ALU.add).then_inc(out_ready, 1)

            @block.scalar
            def _(act):
                for c in range(NC):
                    act.wait_ge(g_done, 2 * c + 2)
                    for t in range(2):
                        for h in range(2, GP):
                            copy = nc.scalar.copy(g[:, t, h], psG[t][h][:, 0:KC])
                    copy.then_inc(g_ready, 1)
                    for s, (s0, w) in enumerate(SUB):
                        n = c * len(SUB) + s
                        act.wait_ge(s_done, n + 1)
                        if n >= 2:
                            act.wait_ge(out_ready, 2 * n - 2)
                        nc.scalar.copy(osb[0:w, n % 2], psG[n % 2][1][0:w]).then_inc(o_ready, 1)

            @block.tensor
            def _(pe):
                pe.wait_ge(set_done, 1)
                pe.wait_ge(c_loaded, 16 * (2 + 2 * GP))
                for t in range(2):
                    for c in range(GP):
                        mm = nc.tensor.matmul(psG[t][0][:, c * P:(c + 1) * P], cdsd[:, t], wf[:, c], start=(c == 0),
                                              stop=True, skip_group_check=True)
                    mm.then_inc(mix_done, 1)
                pe.wait_ge(mix_ready, 2)
                for c in range(NC):
                    if c:
                        pe.wait_ge(out_ready, 2 * len(SUB) * c)
                    for t, src in enumerate((e, o)):
                        if c == 0:
                            pe.wait_ge(t_loaded[t], 16 * JT)
                        for j in range(JT):
                            n = P if j < JT - 1 else LAST
                            if c == 0 and t == 0:
                                pe.wait_ge(folded, j + 1)
                            for h in range(GP):
                                mm = nc.tensor.matmul(psG[t][h][:, 0:KC], src[0:n, j, h * P:(h + 1) * P],
                                                      tab[0:n, t, j, c * KC:(c + 1) * KC], start=(j == 0), stop=(j == JT - 1))
                        mm.then_inc(g_done, 1)
                    pe.wait_ge(g_ready, 2 * c + 2)
                    for s, (s0, w) in enumerate(SUB):
                        n = c * len(SUB) + s
                        if s >= 2:
                            pe.wait_ge(out_ready, 2 * n - 2)
                        nc.tensor.matmul(psG[n % 2][0][0:w], ones[:, 0:w], bias[:], start=True, stop=False, skip_group_check=True)
                        for t in range(2):
                            for h in range(GP):
                                mm = nc.tensor.matmul(psG[n % 2][t][0:w, h * P:(h + 1) * P], g[:, t, h, s0:s0 + w],
                                                      mix[:, t, h], start=(t == 1 and h == 0), stop=(h == GP - 1),
                                                      skip_group_check=True)
                        mm.then_inc(s_done, 1)


def stage_max(nc, d, name, src, heads, kv_of, width, keys, causal, out):
    with ExitStack() as stack:
        st = Stage(nc, name, stack)
        qf = st.sb("qf", [width, 2, S])
        kf = st.sb("kf", [width, 2, keys])
        qb = st.sb("qb", [width, 2, S], BF16)
        kb = st.sb("kb", [width, 2, keys], BF16)
        mx = st.sb("mx", [P, heads * NT, 2])
        neg = st.sb("neg", [P, heads * NT])
        negT = st.sb("negT", [heads * NT, P])
        ident = st.sb("ident", [P, P])
        half = keys // 2
        ps = [st.ps(f"ps{u}", [P, 1536]) for u in range(2)]
        psN = st.ps("psN", [P, P])
        loaded = [st.sem(f"loaded{k}") for k in range(2)]
        c_loaded = st.sem("c_loaded")
        cast = st.sem("cast")
        b_free = st.sem("b_free")
        s_done = st.sem("s_done")
        m_done = st.sem("m_done")
        n_step = st.sem("n_step")
        n_done = st.sem("n_done")
        n_ready = st.sem("n_ready")
        stored = st.sem("stored")
        filled = st.sem("filled")

        def units(t):
            if not causal:
                return [(0, half), (half, half)]
            end = (t + 1) * P
            return [(0, end)] if end <= 1024 else [(0, 1024), (1024, end - 1024)]

        total = sum(len(units(t)) for t in range(NT))

        with nc.Block() as block:

            @block.sync
            def _(sp):
                sp.dma_start(ident[:], d["ident"]).then_inc(c_loaded, 16)
                def load(h, k):
                    count, at_q, at_k = ahead(sp, h + 1, h * width, kv_of(h))
                    sp.wait_ge(cast, count)
                    sp.dma_start(qf[:, k], d[src[0]][bass.ds(at_q, width), 0:S]).then_inc(loaded[k], 16)
                    sp.dma_start(kf[:, k], d[src[1]][bass.ds(at_k, width), 0:keys]).then_inc(loaded[k], 16)
                with sp.Fori(0, heads // 2) as i:
                    for k in range(2):
                        load(2 * i + k, k)
                sp.wait_ge(n_ready, 1)
                sp.dma_start(d[out].rearrange("h (t p) -> (h t) p", p=P), negT[:]).then_inc(stored, 16)
                sp.wait_ge(stored, 16)

            @block.scalar
            def _(act):
                act.sem_inc(cast, 2)
                with act.Fori(0, heads // 2) as i:
                    for k in range(2):
                        act.wait_ge(loaded[k], 32 * i + 32)
                        act.wait_ge(b_free, 2 * i + k + 1)
                        nc.scalar.copy(qb[:, k], qf[:, k])
                        nc.scalar.copy(kb[:, k], kf[:, k]).then_inc(cast, 1)

            @block.tensor
            def _(pe):
                pe.sem_inc(b_free, 2)
                with pe.Fori(0, heads // 2) as i:
                    for k in range(2):
                        pe.wait_ge(cast, 2 * i + k + 3)
                        u = 0
                        for t in range(NT):
                            for k0, kw in units(t):
                                slot = (k * total + u) % 2
                                pe.wait_ge(m_done, (2 * i + k) * total + u + 1)
                                for c in range(0, kw, 512):
                                    w = min(512, kw - c)
                                    mm = nc.tensor.matmul(ps[slot][:, c:c + w], qb[:, k, t * P:(t + 1) * P],
                                                          kb[:, k, k0 + c:k0 + c + w], start=True, stop=True)
                                mm.then_inc(s_done, 1)
                                u += 1
                        pe.wait_ge(s_done, (2 * i + k) * total + total)
                        pe.sem_inc(b_free, 1)
                pe.wait_ge(c_loaded, 16)
                pe.wait_ge(n_step, 2)
                nc.tensor.transpose(psN[0:heads * NT, :], neg[:], ident[:]).then_inc(n_done, 1)

            @block.vector
            def _(dve):
                dve.sem_inc(m_done, 2)
                nc.vector.memset(mx[:], -1e30).then_inc(filled, 1)
                dve.wait_ge(filled, 1)
                with dve.Fori(0, heads // 2) as i:
                    for k in range(2):
                        u = 0
                        for t in range(NT):
                            for piece, (k0, kw) in enumerate(units(t)):
                                slot = (k * total + u) % 2
                                dve.wait_ge(s_done, (2 * i + k) * total + u + 1)
                                at = bass.ds((2 * i + k) * NT + t, 1)
                                if causal and k0 + kw == (t + 1) * P:
                                    nc.vector.reduce_max(mx[0:64, at, piece], ps[slot][0:64, 0:kw - 64], AX_X)
                                    nc.vector.reduce_max(mx[64:P, at, piece], ps[slot][64:P, 0:kw], AX_X).then_inc(m_done, 1)
                                else:
                                    nc.vector.reduce_max(mx[:, at, piece], ps[slot][:, 0:kw], AX_X).then_inc(m_done, 1)
                                u += 1
                dve.wait_ge(m_done, heads * total + 2)
                nc.vector.reduce_max(neg[:], mx[:], AX_X).then_inc(n_step, 1)
                dve.wait_ge(n_step, 1)
                nc.vector.tensor_scalar(neg[:], neg[:], -1.0, None, ALU.mult).then_inc(n_step, 1)
                dve.wait_ge(n_done, 1)
                nc.vector.tensor_copy(negT[:], psN[0:heads * NT, :]).then_inc(n_ready, 1)


def stage_attention1(nc, d):
    KT = NT + 1
    GQ = NQ // NKV
    J = NKV * KT
    LAG = 3
    with ExitStack() as stack:
        st = Stage(nc, "C", stack)
        ident = st.sb("ident", [P, P])
        kT = st.sb("kT", [HD + 1, NKV, L])
        v1 = st.sb("v1", [P, KT, NKV, HD + 1])
        qa = st.sb("qa", [HD + 1, 2, NQ, P])
        e = st.sb("e", [P, 4, 512])
        oT = st.sb("oT", [HD + 1, NKV, 512])
        rs = st.sb("rs", [P, GQ])
        ao = st.sb("ao", [P, 2, FW])
        psS = [st.ps(f"psS{s}", [P, 512]) for s in range(4)]
        psO = [st.ps(f"psO{g}", [P, 512]) for g in range(NKV)]
        psR = st.ps("psR", [P, GQ, HD + 1])
        set_done = st.sem("set_done")
        kv_loaded = st.sem("kv_loaded")
        q_loaded = [st.sem(f"q_loaded{k}") for k in range(2)]
        q_free = st.sem("q_free")
        s_done = st.sem("s_done")
        e_done = st.sem("e_done")
        pv_done = st.sem("pv_done")
        oT_ready = st.sem("oT_ready")
        t_done = st.sem("t_done")
        ao_ready = st.sem("ao_ready")
        ao_credit = st.sem("ao_credit")
        r_ready = st.sem("r_ready")
        stored = [st.sem(f"stored{k}") for k in range(2)]

        with nc.Block() as block:

            @block.sync
            def _(sp):
                sp.dma_start(ident[:], d["ident"]).then_inc(kv_loaded, 16)
                for g in range(NKV):
                    sp.dma_start(kT[0:HD, g], d["hT"][(NQ + g) * HD:(NQ + g + 1) * HD]).then_inc(kv_loaded, 16)
                sp.wait_ge(set_done, 1)
                for g in range(NKV):
                    sp.dma_start(v1[:, 0:NT, g, 0:HD], d["v"][0:S, g * HD:(g + 1) * HD].rearrange("(t p) c -> p t c", p=P)).then_inc(kv_loaded, 16)
                    sp.dma_start(v1[0:META, NT, g, 0:HD], d["v"][S:L, g * HD:(g + 1) * HD]).then_inc(kv_loaded, 16)

                def store(n, k):
                    count, at = ahead(sp, 2 * n + 2, n * P)
                    sp.wait_ge(ao_ready, count)
                    sp.wait_ge(set_done, 1)
                    sp.dma_start(d["attn"][bass.ds(at, P)], ao[:, k]).then_inc(stored[k], 16)

                with sp.Fori(0, NT // 2) as i:
                    for k in range(2):
                        store(2 * i + k, k)
                for k in range(2):
                    sp.wait_ge(stored[k], 16 * (NT // 2 + 1))

            @block.gpsimd
            def _(pool):
                with pool.Fori(0, NT // 2) as i:
                    for k in range(2):
                        at = (2 * i + k) * P
                        pool.wait_ge(q_free, 2 * i + k + 1)
                        pool.dma_start(qa[0:HD, k], d["hT"][0:NQ * HD, bass.ds(at, P)].rearrange("(h c) s -> c h s", c=HD)).then_inc(q_loaded[k], 16)
                        pool.dma_start(qa[HD:HD + 1, k], d["negm1"][:, bass.ds(at, P)].unsqueeze(0)).then_inc(q_loaded[k], 16)

            @block.vector
            def _(dve):
                nc.vector.memset(v1[:], 1.0)
                nc.vector.memset(kT[HD:HD + 1], 1.0).then_inc(set_done, 1)
                for k in range(2):
                    dve.sem_inc(stored[k], 16)
                with dve.Fori(0, NT // 2) as i:
                    for k in range(2):
                        n = 2 * i + k
                        for g in range(NKV):
                            dve.wait_ge(pv_done, n * J + (g + 1) * KT + 4)
                            nc.vector.tensor_copy(oT[:, g], psO[g][0:HD + 1]).then_inc(oT_ready, 1)
                            dve.wait_ge(t_done, 2 * n + g + 1)
                            nc.vector.reciprocal(rs[:], psR[:, :, HD]).then_inc(r_ready, 1)
                            dve.wait_ge(r_ready, 2 * n + g + 1)
                            if g == 0:
                                dve.wait_ge(stored[k], 16 * i + 16)
                            nc.vector.tensor_tensor(
                                ao[:, k, g * GQ * HD:(g + 1) * GQ * HD].rearrange("p (h c) -> p h c", c=HD), psR[:, :, 0:HD],
                                rs[:].unsqueeze(2).to_broadcast([P, GQ, HD]), ALU.mult).then_inc(ao_ready, 1)

            @block.scalar
            def _(act):
                nc.scalar.preload_act_table_set("natural_log_exp_and_others")
                with act.Fori(0, NT // 2) as i:
                    for k in range(2):
                        for j in range(J):
                            rows = P if j % KT < NT else META
                            slot = (k * J + j) % 4
                            act.wait_ge(s_done, (2 * i + k) * J + j + 1)
                            act.wait_ge(pv_done, (2 * i + k) * J + j + 1)
                            nc.scalar.activation(e[0:rows, slot], psS[slot][0:rows], ACT.Exp).then_inc(e_done, 1)

            @block.tensor
            def _(pe):
                pe.sem_inc(pv_done, 4)
                pe.sem_inc(q_free, 2)
                pe.wait_ge(set_done, 1)
                pe.wait_ge(kv_loaded, 112)
                with pe.Fori(0, NT // 2) as i:
                    for k in range(2):
                        n = 2 * i + k

                        def scores(j):
                            g, kt = j // KT, j % KT
                            rows = P if kt < NT else META
                            slot = (k * J + j) % 4
                            nc.tensor.matmul(psS[slot][0:rows], kT[:, g, kt * P:kt * P + rows],
                                             qa[:, k, g * GQ:(g + 1) * GQ].rearrange("c h s -> c (h s)"),
                                             start=True, stop=True).then_inc(s_done, 1)

                        def turn(g):
                            pe.wait_ge(oT_ready, 2 * n + g + 1)
                            for h in range(GQ):
                                t = nc.tensor.transpose(psR[:, h], oT[:, g, h * P:(h + 1) * P], ident[0:HD + 1, 0:HD + 1])
                            t.then_inc(t_done, 1)

                        pe.wait_ge(q_loaded[k], 32 * i + 32)
                        scores(0)
                        scores(1)
                        for j in range(J):
                            g, kt = j // KT, j % KT
                            rows = P if kt < NT else META
                            slot = (k * J + j) % 4
                            if j + 2 < J:
                                scores(j + 2)
                            if j == KT + LAG:
                                turn(0)
                            pe.wait_ge(e_done, n * J + j + 1)
                            nc.tensor.matmul(psO[g][0:HD + 1], v1[0:rows, kt, g], e[0:rows, slot],
                                             start=(kt == 0), stop=(kt == KT - 1)).then_inc(pv_done, 1)
                        turn(1)
                        pe.sem_inc(q_free, 1)


def stage_output(nc, d, name, left, right, gates, w, resid, gain, total, normed):
    with ExitStack() as stack:
        st = Stage(nc, name, stack)
        wt = st.sb("w", [P, KD, D])
        ident = st.sb("ident", [P, P])
        eps = st.sb("eps", [P, 1])
        gn = st.sb("gn", [P, D])
        mixed = st.sb("mixed", [P, 2, D])
        gt = st.sb("gt", [P, 2, D])
        rs = st.sb("rs", [P, 2, D])
        gm = st.sb("gm", [P, 2, D])
        mT = st.sb("mT", [P, 2, KD, P])
        h = st.sb("h", [P, 2, D])
        sq = st.sb("sq", [P, D])
        stat = st.sb("stat", [P, 2, 4])
        o = st.sb("o", [P, 2, D])
        psT = st.ps("psT", [P, KD, P])
        psH = [st.ps(f"psH{k}", [P, D]) for k in range(2)]
        w_loaded = st.sem("w_loaded")
        c_loaded = st.sem("c_loaded")
        loaded = [st.sem(f"loaded{k}") for k in range(2)]
        in_free = st.sem("in_free")
        eps_set = st.sem("eps_set")
        gated = st.sem("gated")
        t_done = st.sem("t_done")
        mT_a = st.sem("mT_a")
        mT_v = st.sem("mT_v")
        p_done = st.sem("p_done")
        h_ready = st.sem("h_ready")
        act_step = st.sem("act_step")
        r_ready = st.sem("r_ready")
        o_ready = st.sem("o_ready")
        stored = [st.sem(f"stored{k}") for k in range(2)]
        LOADS = 4 if gates else 3
        STORES = 2 if total else 1

        with nc.Block() as block:

            @block.sync
            def _(sp):
                sp.dma_start(ident[:], d["ident"]).then_inc(c_loaded, 16)
                sp.dma_start(gn[:], to_all(d[gain])).then_inc(c_loaded, 16)

                def load(n, k):
                    count, = ahead(sp, n + 1)
                    sp.wait_ge(in_free, count)
                    sp.dma_start(mixed[:, k, 0:FW], d[left][rows_of(n)]).then_inc(loaded[k], 16)
                    sp.dma_start(mixed[:, k, FW:D], d[right][rows_of(n)]).then_inc(loaded[k], 16)
                    if gates:
                        sp.dma_start(gt[:, k], d[gates][rows_of(n)]).then_inc(loaded[k], 16)
                    sp.dma_start(rs[:, k], d[resid][rows_of(n)]).then_inc(loaded[k], 16)

                def store(n, k):
                    count, = ahead(sp, n + 1)
                    sp.wait_ge(o_ready, count)
                    sp.dma_start(d[normed][rows_of(n)], o[:, k]).then_inc(stored[k], 16)
                    if total:
                        sp.dma_start(d[total][rows_of(n)], h[:, k]).then_inc(stored[k], 16)

                for k in range(2):
                    load(k, k)
                for kd in range(KD):
                    sp.dma_start(wt[:, kd], d[w][0, kd * P:(kd + 1) * P]).then_inc(w_loaded, 16)
                with sp.Fori(0, NT // 2 - 1) as i:
                    for k in range(2):
                        store(2 * i + k, k)
                        load(2 * i + k + 2, k)
                for k in range(2):
                    store(NT - 2 + k, k)
                for k in range(2):
                    sp.wait_ge(stored[k], 16 * STORES * (NT // 2 + 1))

            @block.gpsimd
            def _(pool):
                pool.wait_ge(eps_set, 1)
                if gates:
                    with pool.Fori(0, NT // 2) as i:
                        for k in range(2):
                            pool.wait_ge(loaded[k], 16 * LOADS * i + 16 * LOADS)
                            pool.wait_ge(t_done, 2 * i + k + 1)
                            nc.gpsimd.tensor_tensor(gm[:, k], mixed[:, k], gt[:, k], ALU.mult).then_inc(gated, 1)

            @block.scalar
            def _(act):
                nc.scalar.preload_act_table_set("natural_log_exp_and_others")
                chain = Chain(act, act_step)
                act.wait_ge(eps_set, 1)
                with act.Fori(0, NT // 2) as i:
                    for k in range(2):
                        n = 2 * i + k
                        if k == 0:
                            chain.at(4 * i)
                        act.wait_ge(t_done, n + 3)
                        act.wait_ge(p_done, n + 1)
                        nc.scalar.copy(mT[:, k, KD // 2:KD], psT[:, KD // 2:KD]).then_inc(mT_a, 1)
                        act.wait_ge(h_ready, n + 1)
                        chain.link(nc.scalar.activation(sq[:], h[:, k], ACT.Square, accum_out=stat[:, k, 0:1]))
                        chain.link(nc.scalar.activation(stat[:, k, 1:2], stat[:, k, 0:1], ACT.Ln, scale=1.0 / D, bias=eps[:, 0:1]))
                        nc.scalar.activation(stat[:, k, 2:3], stat[:, k, 1:2], ACT.Exp, scale=-0.5).then_inc(r_ready, 1)

            @block.tensor
            def _(pe):
                pe.sem_inc(t_done, 2)
                pe.sem_inc(p_done, 2)
                pe.wait_ge(c_loaded, 32)
                pe.wait_ge(w_loaded, 16 * KD)
                src = gm if gates else mixed
                with pe.Fori(0, NT // 2) as i:
                    for k in range(2):
                        n = 2 * i + k
                        if gates:
                            pe.wait_ge(gated, n + 1)
                        else:
                            pe.wait_ge(loaded[k], 16 * LOADS * i + 16 * LOADS)
                        for kd in range(KD):
                            t = nc.tensor.transpose(psT[:, kd], src[:, k, kd * P:(kd + 1) * P], ident[:])
                        t.then_inc(t_done, 1)
                        pe.wait_ge(mT_a, n + 1)
                        pe.wait_ge(mT_v, n + 1)
                        for half in range(2):
                            for kd in range(KD):
                                mm = nc.tensor.matmul(psH[k][:, half * 512:(half + 1) * 512], mT[:, k, kd],
                                                      wt[:, kd, half * 512:(half + 1) * 512], start=(kd == 0), stop=(kd == KD - 1))
                        mm.then_inc(p_done, 1)

            @block.vector
            def _(dve):
                nc.vector.memset(eps[:], EPS).then_inc(eps_set, 1)
                dve.sem_inc(in_free, 2)
                for k in range(2):
                    dve.sem_inc(stored[k], 16 * STORES)
                dve.wait_ge(c_loaded, 32)
                with dve.Fori(0, NT // 2) as i:
                    for k in range(2):
                        n = 2 * i + k
                        dve.wait_ge(t_done, n + 3)
                        dve.wait_ge(p_done, n + 1)
                        nc.vector.tensor_copy(mT[:, k, 0:KD // 2], psT[:, 0:KD // 2]).then_inc(mT_v, 1)
                        dve.wait_ge(p_done, n + 3)
                        dve.wait_ge(stored[k], 16 * STORES * i + 16 * STORES)
                        nc.vector.tensor_tensor(h[:, k], psH[k][:], rs[:, k], ALU.add).then_inc(h_ready, 1)
                        dve.wait_ge(h_ready, n + 1)
                        dve.sem_inc(in_free, 1)
                        dve.wait_ge(r_ready, n + 1)
                        nc.vector.scalar_tensor_tensor(o[:, k], h[:, k], stat[:, k, 2:3], gn[:], ALU.mult, ALU.mult).then_inc(o_ready, 1)


def stage_rope2(nc, d):
    NF = 16
    TP = S // P
    C1 = 6.28125
    C2 = 2 * np.pi - C1
    ROUND = 1.5 * 2 ** 23
    LIM = 3.1415925
    with ExitStack() as stack:
        st = Stage(nc, "R", stack)
        pi = st.sb("pi", [P, TP], I32)
        pf = st.sb("pf", [P, TP])
        inv = st.sb("inv", [P, NF])
        ang = st.sb("ang", [P, TP, NF])
        turns = st.sb("turns", [P, TP, NF])
        r = st.sb("r", [P, TP, 2, NF])
        cs = st.sb("cs", [P, TP, 2, NF])
        loaded = st.sem("loaded")
        step = st.sem("step")
        r_ready = st.sem("r_ready")
        done = st.sem("done")
        stored = st.sem("stored")
        with nc.Block() as block:

            @block.sync
            def _(sp):
                sp.dma_start(pi[:], d["positions_2"].rearrange("a (p t) -> p (a t)", p=P)).then_inc(loaded, 16)
                sp.dma_start(inv[:], to_all(d["rope2_inv"])).then_inc(loaded, 16)
                sp.wait_ge(done, 2)
                sp.dma_start(d["cs2"].rearrange("(p t) c -> p (t c)", p=P), cs[:].rearrange("p t a c -> p (t a c)")).then_inc(stored, 16)
                sp.wait_ge(stored, 16)

            @block.vector
            def _(dve):
                chain = Chain(dve, step)
                dve.wait_ge(loaded, 32)
                chain.link(nc.vector.tensor_copy(pf[:], pi[:]))
                chain.link(nc.vector.tensor_tensor(ang[:], pf[:].unsqueeze(2).to_broadcast([P, TP, NF]),
                                                   inv[:].unsqueeze(1).to_broadcast([P, TP, NF]), ALU.mult))
                for a, (shift, quarter) in enumerate(((0.25, np.pi / 2), (0.0, 0.0))):
                    chain.link(nc.vector.tensor_scalar(turns[:], ang[:], 1.0 / (2 * np.pi), shift, ALU.mult, ALU.add))
                    chain.link(nc.vector.tensor_scalar(turns[:], turns[:], ROUND, -ROUND, ALU.add, ALU.add))
                    chain.link(nc.vector.scalar_tensor_tensor(r[:, :, a], turns[:], -C1, ang[:], ALU.mult, ALU.add))
                    chain.link(nc.vector.scalar_tensor_tensor(r[:, :, a], turns[:], -C2, r[:, :, a], ALU.mult, ALU.add))
                    chain.link(nc.vector.tensor_scalar(r[:, :, a], r[:, :, a], quarter, LIM, ALU.add, ALU.min))
                    nc.vector.tensor_scalar(r[:, :, a], r[:, :, a], -LIM, None, ALU.max).then_inc(r_ready, 1)

            @block.scalar
            def _(act):
                for a in range(2):
                    act.wait_ge(r_ready, a + 1)
                    nc.scalar.activation(cs[:, :, a], r[:, :, a], ACT.Sin).then_inc(done, 1)


LAT = QL + KVL + RD
def stage_project2(nc, d):
    with ExitStack() as stack:
        st = Stage(nc, "D", stack)
        w = st.sb("w", [P, KD, W2])
        gain = st.sb("gain", [P, KD])
        ident = st.sb("ident", [P, P])
        eps = st.sb("eps", [P, 1])
        bias = st.sb("bias", [P, 2, MLH])
        zero = st.sb("zero", [CONV - 1, ML])
        x = st.sb("x", [P, 2, D])
        sq = st.sb("sq", [P, D])
        stat = st.sb("stat", [P, 2, 4])
        u = st.sb("u", [P, 2, D])
        uT = st.sb("uT", [P, 2, KD, P])
        lat = st.sb("lat", [P, 2, LAT])
        xm = st.sb("xm", [P, 2, ML])
        ze = st.sb("ze", [P, ML])
        zs = st.sb("zs", [P, 2, ML])
        gi = st.sb("gi", [P, 2, 2 * MLH])
        psT = st.ps("psT", [P, KD, P])
        psG = [st.ps(f"psG{g}", [P, 512]) for g in range(4)]
        groups = [(QL + KVL + RD, ML), (QL + KVL + RD + ML, ML), (0, LAT), (LAT + 2 * ML, 2 * MLH)]
        XM, Z, LT, GI = range(4)
        w_loaded = st.sem("w_loaded")
        c_loaded = st.sem("c_loaded")
        w_scaled = st.sem("w_scaled")
        eps_set = st.sem("eps_set")
        loaded = [st.sem(f"loaded{k}") for k in range(2)]
        act_step = st.sem("act_step")
        r_ready = st.sem("r_ready")
        u_ready = st.sem("u_ready")
        x_free = st.sem("x_free")
        t_done = st.sem("t_done")
        uT_a = st.sem("uT_a")
        uT_v = st.sem("uT_v")
        g_done = [st.sem(f"g_done{g}") for g in range(4)]
        g_free = [st.sem(f"g_free{g}") for g in range(4)]
        zx = st.sem("zx")
        dve_step = st.sem("dve_step")
        a_ready = st.sem("a_ready")
        v_ready = st.sem("v_ready")
        stored = [st.sem(f"stored{k}") for k in range(2)]
        zero_stored = st.sem("zero_stored")

        with nc.Block() as block:

            @block.sync
            def _(sp):
                sp.dma_start(ident[:], d["ident"]).then_inc(c_loaded, 16)
                sp.dma_start(gain[:], d["norm_mix_g_2"].rearrange("a (k p) -> p (a k)", p=P), allow_slow_non_contiguous=True).then_inc(c_loaded, 16)
                sp.dma_start(bias[:, 0], to_all(d["b_igate_2"])).then_inc(c_loaded, 16)
                sp.dma_start(bias[:, 1], to_all(d["b_fgate_2"])).then_inc(c_loaded, 16)
                sp.wait_ge(eps_set, 1)
                sp.dma_start(d["xm"][0:CONV - 1], zero[:]).then_inc(zero_stored, 16)

                def load(n, k):
                    count, = ahead(sp, n + 1)
                    sp.wait_ge(x_free, count)
                    sp.wait_ge(eps_set, 1)
                    sp.dma_start(x[:, k], d["x1"][rows_of(n)]).then_inc(loaded[k], 16)

                def store(n, k):
                    count, = ahead(sp, n + 1)
                    sp.wait_ge(v_ready, count)
                    sp.wait_ge(a_ready, count)
                    sp.dma_start(d["xm"][bass.ds(n * P + CONV - 1, P)], xm[:, k]).then_inc(stored[k], 16)
                    sp.dma_start(d["lat"][rows_of(n)], lat[:, k]).then_inc(stored[k], 16)
                    sp.dma_start(d["z"][rows_of(n)], zs[:, k]).then_inc(stored[k], 16)
                    sp.dma_start(d["gi"][rows_of(n)], gi[:, k]).then_inc(stored[k], 16)

                for k in range(2):
                    load(k, k)
                for kd in range(KD):
                    sp.dma_start(w[:, kd], d["w_in_2"][0, kd * P:(kd + 1) * P]).then_inc(w_loaded, 16)
                with sp.Fori(0, NT // 2 - 1) as i:
                    for k in range(2):
                        store(2 * i + k, k)
                        load(2 * i + k + 2, k)
                for k in range(2):
                    store(NT - 2 + k, k)
                for k in range(2):
                    sp.wait_ge(stored[k], 64 * (NT // 2 + 1))
                sp.wait_ge(zero_stored, 16)

            @block.gpsimd
            def _(pool):
                pool.sem_inc(x_free, 2)
                with pool.Fori(0, NT // 2) as i:
                    for k in range(2):
                        n = 2 * i + k
                        pool.wait_ge(r_ready, n + 1)
                        pool.wait_ge(t_done, n + 1)
                        nc.gpsimd.tensor_tensor(u[:, k], x[:, k], stat[:, k, 2:3].to_broadcast([P, D]), ALU.mult).then_inc(u_ready, 1)
                        pool.wait_ge(u_ready, n + 1)
                        pool.sem_inc(x_free, 1)

            @block.scalar
            def _(act):
                nc.scalar.preload_act_table_set("natural_log_exp_and_others")
                chain = Chain(act, act_step)
                for k in range(2):
                    act.sem_inc(stored[k], 64)
                act.wait_ge(eps_set, 1)

                def stats(k, m):
                    act.wait_ge(loaded[k], 16 * m)
                    chain.link(nc.scalar.activation(sq[:], x[:, k], ACT.Square, accum_out=stat[:, k, 0:1]))
                    chain.link(nc.scalar.activation(stat[:, k, 1:2], stat[:, k, 0:1], ACT.Ln, scale=1.0 / D, bias=eps[:, 0:1]))
                    nc.scalar.activation(stat[:, k, 2:3], stat[:, k, 1:2], ACT.Exp, scale=-0.5).then_inc(r_ready, 1)

                def rest(n, k, m):
                    act.wait_ge(t_done, n + 3)
                    act.wait_ge(g_done[GI], n + 1)
                    nc.scalar.copy(uT[:, k, KD // 2:KD], psT[:, KD // 2:KD]).then_inc(uT_a, 1)
                    act.wait_ge(g_done[XM], n + 1)
                    act.wait_ge(stored[k], 64 * m)
                    nc.scalar.copy(xm[:, k], psG[XM][:]).then_inc(g_free[XM], 1)
                    act.wait_ge(g_done[Z], n + 1)
                    chain.link(nc.scalar.activation(ze[:], psG[Z][:], ACT.Exp, scale=-1.0))
                    chain.link(nc.scalar.activation(ze[:], ze[:], ACT.Ln, bias=1.0))
                    chain.link(nc.scalar.activation(ze[:], ze[:], ACT.Exp, scale=-1.0))
                    act.sem_inc(zx, 1)
                    act.wait_ge(g_done[LT], n + 1)
                    nc.scalar.copy(lat[:, k], psG[LT][:, 0:LAT]).then_inc(a_ready, 1)
                    act.wait_ge(a_ready, n + 1)
                    act.sem_inc(g_free[LT], 1)
                    act.wait_ge(v_ready, n + 1)

                stats(0, 1)
                with act.Fori(0, NT // 2 - 1) as i:
                    chain.at(10 * i + 2)
                    stats(1, i + 1)
                    rest(2 * i, 0, i + 1)
                    stats(0, i + 2)
                    rest(2 * i + 1, 1, i + 1)
                chain.at(10 * (NT // 2 - 1) + 2)
                stats(1, NT // 2)
                rest(NT - 2, 0, NT // 2)
                rest(NT - 1, 1, NT // 2)

            @block.tensor
            def _(pe):
                pe.sem_inc(t_done, 2)
                pe.sem_inc(g_done[GI], 2)
                pe.wait_ge(c_loaded, 64)
                pe.wait_ge(w_scaled, KD)
                with pe.Fori(0, NT // 2) as i:
                    for k in range(2):
                        n = 2 * i + k
                        pe.wait_ge(u_ready, n + 1)
                        for kd in range(KD):
                            t = nc.tensor.transpose(psT[:, kd], u[:, k, kd * P:(kd + 1) * P], ident[:])
                        t.then_inc(t_done, 1)
                        pe.wait_ge(uT_a, n + 1)
                        pe.wait_ge(uT_v, n + 1)
                        for g, (c0, width) in enumerate(groups):
                            pe.wait_ge(g_free[g], n + 1)
                            for kd in range(KD):
                                mm = nc.tensor.matmul(psG[g][:, 0:width], uT[:, k, kd], w[:, kd, c0:c0 + width],
                                                      start=(kd == 0), stop=(kd == KD - 1))
                            mm.then_inc(g_done[g], 1)

            @block.vector
            def _(dve):
                nc.vector.memset(zero[:], 0.0)
                nc.vector.memset(eps[:], EPS).then_inc(eps_set, 1)
                for g in range(4):
                    dve.sem_inc(g_free[g], 1)
                dve.wait_ge(c_loaded, 64)
                dve.wait_ge(w_loaded, 16 * KD)
                for kd in range(KD):
                    nc.vector.tensor_scalar(w[:, kd], w[:, kd], gain[:, kd:kd + 1], None, ALU.mult).then_inc(w_scaled, 1)
                with dve.Fori(0, NT // 2) as i:
                    for k in range(2):
                        n = 2 * i + k
                        dve.wait_ge(t_done, n + 3)
                        dve.wait_ge(g_done[GI], n + 1)
                        nc.vector.tensor_copy(uT[:, k, 0:KD // 2], psT[:, 0:KD // 2]).then_inc(uT_v, 1)
                        dve.wait_ge(zx, n + 1)
                        dve.wait_ge(stored[k], 64 * i + 64)
                        nc.vector.tensor_tensor(zs[:, k], psG[Z][:], ze[:], ALU.mult).then_inc(g_free[Z], 1)
                        dve.wait_ge(g_done[GI], n + 3)
                        nc.vector.tensor_tensor(gi[:, k], psG[GI][:, 0:2 * MLH], bias[:].rearrange("p a h -> p (a h)"), ALU.add).then_inc(v_ready, 1)
                        dve.wait_ge(v_ready, n + 1)
                        dve.sem_inc(g_free[GI], 1)


def stage_mla_heads(nc, d):
    HQ = MH // 2
    with ExitStack() as stack:
        st = Stage(nc, "E", stack)
        ident = st.sb("ident", [P, P])
        eps = st.sb("eps", [P, 1])
        wq = st.sb("wq", [P, QL // P, MH * QD])
        wkv = st.sb("wkv", [P, MH * (ND + VD)])
        qg = st.sb("qg", [P, QL // P])
        kg = st.sb("kg", [P, 1])
        lat = st.sb("lat", [P, 2, LAT])
        cs = st.sb("cs", [P, 2, 2, RD // 2])
        sq = st.sb("sq", [P, QL])
        stat = st.sb("stat", [P, 2, 6])
        cn = st.sb("cn", [P, 2, QL + KVL])
        cT = st.sb("cT", [P, 2, 3, P])
        hq = st.sb("hq", [P, MH, QD])
        hk = st.sb("hk", [P, MH, QD])
        kr = st.sb("kr", [P, RD])
        rq = st.sb("rq", [P, 4, MH, RD // 2])
        rk = st.sb("rk", [P, 4, RD // 2])
        v = st.sb("v", [P, 2, MH, VD])
        qT = st.sb("qT", [QD, 2, MH, P])
        kT = st.sb("kT", [QD, 2, MH, P])
        psT = st.ps("psT", [P, 512])
        psQ = st.ps("psQ", [P, 2, 512])
        psK = st.ps("psK", [P, 2, 512])
        psX = st.ps("psX", [P, MH, P])
        loaded = [st.sem(f"loaded{k}") for k in range(2)]
        c_loaded = st.sem("c_loaded")
        w_loaded = st.sem("w_loaded")
        w_ready = st.sem("w_ready")
        eps_set = st.sem("eps_set")
        in_free = st.sem("in_free")
        act_step = st.sem("act_step")
        r_ready = st.sem("r_ready")
        cn_ready = st.sem("cn_ready")
        t_done = st.sem("t_done")
        cT_ready = st.sem("cT_ready")
        p_done = st.sem("p_done")
        hq_ready = st.sem("hq_ready")
        hk_ready = st.sem("hk_ready")
        dve_step = st.sem("dve_step")
        rot_q = st.sem("rot_q")
        rot_k = st.sem("rot_k")
        x_done = st.sem("x_done")
        qT_ready = st.sem("qT_ready")
        kT_ready = st.sem("kT_ready")
        stored = [st.sem(f"stored{k}") for k in range(2)]
        with nc.Block() as block:

            @block.sync
            def _(sp):
                def load(n, k):
                    count, = ahead(sp, n + 1)
                    sp.wait_ge(in_free, count)
                    sp.dma_start(lat[:, k], d["lat"][rows_of(n)]).then_inc(loaded[k], 16)
                    sp.dma_start(cs[:, k].rearrange("p a c -> p (a c)"), d["cs2"][rows_of(n)]).then_inc(loaded[k], 16)

                def store(n, k):
                    count, = ahead(sp, n + 1)
                    sp.wait_ge(qT_ready, count)
                    sp.wait_ge(kT_ready, count)
                    sp.dma_start(d["v2"][rows_of(n)], v[:, k].rearrange("p h c -> p (h c)")).then_inc(stored[k], 16)
                    sp.dma_start(d["qT2"][:, bass.ds(n * P, P)].rearrange("(h c) s -> c h s", c=QD), qT[:, k]).then_inc(stored[k], 16)
                    sp.dma_start(d["kT2"][:, bass.ds(n * P, P)].rearrange("(h c) s -> c h s", c=QD), kT[:, k]).then_inc(stored[k], 16)

                sp.dma_start(ident[:], d["ident"]).then_inc(c_loaded, 16)
                sp.dma_start(qg[:], d["q_norm_g_2"].rearrange("a (k p) -> p (a k)", p=P), allow_slow_non_contiguous=True).then_inc(c_loaded, 16)
                sp.dma_start(kg[:], d["kv_norm_g_2"].rearrange("a p -> p a"), allow_slow_non_contiguous=True).then_inc(c_loaded, 16)
                for k in range(2):
                    load(k, k)
                sp.dma_start(wq[:], d["w_uq_2"].rearrange("a (k p) n -> p (a k) n", p=P)).then_inc(w_loaded, 16)
                sp.dma_start(wkv[:], d["w_ukv_2"][0]).then_inc(w_loaded, 16)
                with sp.Fori(0, NT // 2 - 1) as i:
                    for k in range(2):
                        store(2 * i + k, k)
                        load(2 * i + k + 2, k)
                for k in range(2):
                    store(NT - 2 + k, k)
                for k in range(2):
                    sp.wait_ge(stored[k], 48 * (NT // 2 + 1))

            @block.scalar
            def _(act):
                nc.scalar.preload_act_table_set("natural_log_exp_and_others")
                chain = Chain(act, act_step)
                for k in range(2):
                    act.sem_inc(stored[k], 48)
                act.wait_ge(eps_set, 1)
                with act.Fori(0, NT // 2) as i:
                    for k in range(2):
                        n = 2 * i + k
                        if k == 0:
                            chain.at(8 * i)
                        act.wait_ge(loaded[k], 32 * i + 32)
                        chain.link(nc.scalar.activation(sq[:], lat[:, k, 0:QL], ACT.Square, accum_out=stat[:, k, 0:1]))
                        chain.link(nc.scalar.activation(sq[:, 0:KVL], lat[:, k, QL:QL + KVL], ACT.Square, accum_out=stat[:, k, 1:2]))
                        nc.scalar.activation(stat[:, k, 2:3], stat[:, k, 0:1], ACT.Ln, scale=1.0 / QL, bias=eps[:, 0:1])
                        chain.link(nc.scalar.activation(stat[:, k, 3:4], stat[:, k, 1:2], ACT.Ln, scale=1.0 / KVL, bias=eps[:, 0:1]))
                        nc.scalar.activation(stat[:, k, 4:6], stat[:, k, 2:4], ACT.Exp, scale=-0.5).then_inc(r_ready, 1)
                        act.wait_ge(p_done, n + 1)
                        act.wait_ge(x_done, 2 * n + 1)
                        for b in range(2):
                            copy = nc.scalar.copy(hq[:, b * HQ:(b + 1) * HQ].rearrange("p h c -> p (h c)"), psQ[:, b, 0:HQ * QD])
                        copy.then_inc(hq_ready, 1)
                        act.wait_ge(stored[k], 48 * i + 48)
                        for b in range(2):
                            kv = psK[:, b].rearrange("p (h c) -> p h c", c=ND + VD)
                            nc.scalar.copy(hk[:, b * HQ:(b + 1) * HQ, 0:ND], kv[:, :, 0:ND])
                            copy = nc.scalar.copy(v[:, k, b * HQ:(b + 1) * HQ], kv[:, :, ND:ND + VD])
                        copy.then_inc(hk_ready, 1)
                        act.wait_ge(x_done, 2 * n + 2)
                        chain.link(nc.scalar.copy(qT[:, k], psX[0:QD]))
                        act.sem_inc(qT_ready, 1)

            @block.vector
            def _(dve):
                chain = Chain(dve, dve_step)
                nc.vector.memset(eps[:], EPS).then_inc(eps_set, 1)
                dve.sem_inc(in_free, 2)
                dve.wait_ge(c_loaded, 48)
                dve.wait_ge(w_loaded, 32)
                for j in range(QL // P):
                    nc.vector.tensor_scalar(wq[:, j], wq[:, j], qg[:, j:j + 1], QD ** -0.5, ALU.mult, ALU.mult)
                nc.vector.tensor_scalar(wkv[:], wkv[:], kg[:, 0:1], None, ALU.mult).then_inc(w_ready, 1)
                with dve.Fori(0, NT // 2) as i:
                    for k in range(2):
                        n = 2 * i + k
                        if k == 0:
                            chain.at(6 * i)
                        dve.wait_ge(r_ready, n + 1)
                        dve.wait_ge(t_done, n + 1)
                        nc.vector.tensor_scalar(cn[:, k, 0:QL], lat[:, k, 0:QL], stat[:, k, 4:5], None, ALU.mult)
                        nc.vector.tensor_scalar(cn[:, k, QL:QL + KVL], lat[:, k, QL:QL + KVL], stat[:, k, 5:6], None,
                                                ALU.mult).then_inc(cn_ready, 1)
                        cos, sin = cs[:, k, 0], cs[:, k, 1]
                        half = RD // 2
                        x1, x2 = lat[:, k, QL + KVL:QL + KVL + half], lat[:, k, QL + KVL + half:LAT]
                        nc.vector.tensor_tensor(rk[:, 0], x1, cos, ALU.mult)
                        nc.vector.tensor_tensor(rk[:, 1], x2, sin, ALU.mult)
                        nc.vector.tensor_tensor(rk[:, 2], x1, sin, ALU.mult)
                        chain.link(nc.vector.tensor_tensor(rk[:, 3], x2, cos, ALU.mult))
                        nc.vector.tensor_tensor(kr[:, 0:half], rk[:, 0], rk[:, 1], ALU.subtract)
                        chain.link(nc.vector.tensor_tensor(kr[:, half:RD], rk[:, 2], rk[:, 3], ALU.add))
                        dve.wait_ge(t_done, n + 3)
                        nc.vector.tensor_copy(cT[:, k].rearrange("p a c -> p (a c)"), psT[:, 0:3 * P]).then_inc(cT_ready, 1)
                        dve.wait_ge(hq_ready, n + 1)
                        cosb, sinb = (a.unsqueeze(1).to_broadcast([P, MH, half]) for a in (cos, sin))
                        x1, x2 = hq[:, :, ND:ND + half], hq[:, :, ND + half:QD]
                        nc.vector.tensor_tensor(rq[:, 0], x1, cosb, ALU.mult)
                        nc.vector.tensor_tensor(rq[:, 1], x2, sinb, ALU.mult)
                        nc.vector.tensor_tensor(rq[:, 2], x1, sinb, ALU.mult)
                        chain.link(nc.vector.tensor_tensor(rq[:, 3], x2, cosb, ALU.mult))
                        dve.sem_inc(in_free, 1)
                        nc.vector.tensor_tensor(x1, rq[:, 0], rq[:, 1], ALU.subtract)
                        nc.vector.tensor_tensor(x2, rq[:, 2], rq[:, 3], ALU.add).then_inc(rot_q, 1)
                        dve.wait_ge(hk_ready, n + 1)
                        nc.vector.tensor_copy(hk[:, :, ND:QD], kr[:].unsqueeze(1).to_broadcast([P, MH, RD])).then_inc(rot_k, 1)
                        dve.wait_ge(x_done, 2 * n + 3)
                        dve.wait_ge(stored[k], 48 * i + 48)
                        nc.vector.tensor_copy(kT[:, k], psX[0:QD]).then_inc(kT_ready, 1)
                        if k == 1:
                            assert chain.n == 6
                            
            @block.tensor
            def _(pe):
                pe.sem_inc(t_done, 2)
                pe.sem_inc(x_done, 1)
                pe.wait_ge(c_loaded, 48)
                pe.wait_ge(w_ready, 1)
                with pe.Fori(0, NT // 2) as i:
                    for k in range(2):
                        n = 2 * i + k
                        pe.wait_ge(cn_ready, n + 1)
                        for j in range(3):
                            t = nc.tensor.transpose(psT[:, j * P:(j + 1) * P], cn[:, k, j * P:(j + 1) * P], ident[:])
                        t.then_inc(t_done, 1)
                        pe.wait_ge(cT_ready, n + 1)
                        for b in range(2):
                            for j in range(QL // P):
                                nc.tensor.matmul(psQ[:, b, 0:HQ * QD], cT[:, k, j], wq[:, j, b * HQ * QD:(b + 1) * HQ * QD],
                                                 start=(j == 0), stop=(j == QL // P - 1))
                        for b in range(2):
                            mm = nc.tensor.matmul(psK[:, b], cT[:, k, 2], wkv[:, b * 512:(b + 1) * 512], start=True, stop=True)
                        mm.then_inc(p_done, 1)
                        pe.wait_ge(rot_q, n + 1)
                        pe.wait_ge(hk_ready, n + 1)
                        for h in range(MH):
                            t = nc.tensor.transpose(psX[0:QD, h], hq[:, h], ident[:])
                        t.then_inc(x_done, 1)
                        pe.wait_ge(rot_k, n + 1)
                        pe.wait_ge(qT_ready, n + 1)
                        for h in range(MH):
                            t = nc.tensor.transpose(psX[0:QD, h], hk[:, h], ident[:])
                        t.then_inc(x_done, 1)


def stage_attention2(nc, d):
    QC = 512
    CH = S // QC
    PAIRS = [(c, kt) for c in range(CH) for kt in range((c + 1) * QC // P)]
    J = len(PAIRS)
    with ExitStack() as stack:
        st = Stage(nc, "F", stack)
        ident = st.sb("ident", [P, P])
        kT = st.sb("kT", [QD + 1, 2, S])
        qa = st.sb("qa", [QD + 1, 2, S])
        v1 = st.sb("v1", [P, 2, NT, VD + 1])
        e = st.sb("e", [P, 4, QC])
        oT = st.sb("oT", [VD + 1, 2, QC])
        rs = st.sb("rs", [P, QC // P])
        ao = st.sb("ao", [P, 2, QC // P, VD])
        psS = [st.ps(f"psS{s}", [P, QC]) for s in range(4)]
        psO = [st.ps(f"psO{g}", [P, QC]) for g in range(2)]
        psR = st.ps("psR", [P, QC // P, VD + 1])
        set_done = st.sem("set_done")
        c_loaded = st.sem("c_loaded")
        loaded = [st.sem(f"loaded{k}") for k in range(2)]
        h_free = st.sem("h_free")
        s_done = st.sem("s_done")
        e_done = st.sem("e_done")
        pv_done = st.sem("pv_done")
        oT_ready = st.sem("oT_ready")
        t_done = st.sem("t_done")
        r_ready = st.sem("r_ready")
        ao_ready = st.sem("ao_ready")
        stored = [st.sem(f"stored{k}") for k in range(2)]

        def shape(j):
            c, kt = PAIRS[j]
            first = max(0, kt * P - c * QC)
            return c, kt, first, QC - first, kt * P >= c * QC

        with nc.Block() as block:

            @block.sync
            def _(sp):
                sp.dma_start(ident[:], d["ident"]).then_inc(c_loaded, 16)
                sp.wait_ge(set_done, 1)
                with sp.Fori(0, MH // 2) as i:
                    for k in range(2):
                        h = 2 * i + k
                        count, row, col = ahead(sp, h + 1, h * QD, h * VD)
                        sp.wait_ge(h_free, count)
                        sp.dma_start(kT[0:QD, k], d["kT2"][bass.ds(row, QD)]).then_inc(loaded[k], 16)
                        sp.dma_start(qa[0:QD, k], d["qT2"][bass.ds(row, QD)]).then_inc(loaded[k], 16)
                        sp.dma_start(qa[QD:QD + 1, k], d["negm2"][bass.ds(h, 1)]).then_inc(loaded[k], 16)
                        sp.dma_start(v1[:, k, :, 0:VD], d["v2"][:, bass.ds(col, VD)].rearrange("(t p) c -> p t c", p=P)).then_inc(loaded[k], 16)

            @block.gpsimd
            def _(pool):
                with pool.Fori(0, MH // 2) as i:
                    for k in range(2):
                        for c in range(CH):
                            m = (2 * i + k) * CH + c
                            pool.wait_ge(ao_ready, m + 1)
                            at = d["attn2"][c * QC:(c + 1) * QC, bass.ds((2 * i + k) * VD, VD)].rearrange("(t p) v -> p t v", p=P)
                            pool.dma_start(at, ao[:, c % 2]).then_inc(stored[c % 2], 16)
                for k in range(2):
                    pool.wait_ge(stored[k], 16 * MH * CH // 2)

            @block.vector
            def _(dve):
                nc.vector.memset(v1[:], 1.0)
                nc.vector.memset(kT[QD:QD + 1], 1.0).then_inc(set_done, 1)

                def chunk(m, c, base, stores):
                    j = max(j for j in range(J) if PAIRS[j][0] == c)
                    dve.wait_ge(pv_done, base + j + 5)
                    nc.vector.tensor_copy(oT[:, c % 2], psO[c % 2][0:VD + 1]).then_inc(oT_ready, 1)
                    dve.wait_ge(t_done, m + 1)
                    nc.vector.reciprocal(rs[:], psR[:, :, VD]).then_inc(r_ready, 1)
                    dve.wait_ge(r_ready, m + 1)
                    if stores is not None:
                        dve.wait_ge(stored[c % 2], stores)
                    nc.vector.tensor_tensor(ao[:, c % 2], psR[:, :, 0:VD], rs[:].unsqueeze(2).to_broadcast([P, QC // P, VD]),
                                            ALU.mult).then_inc(ao_ready, 1)

                for c in range(CH):
                    chunk(c, c, 0, 16 if c >= 2 else None)
                for c in range(CH):
                    chunk(CH + c, c, J, 32 + 16 * (c // 2))
                with dve.Fori(1, MH // 2) as i:
                    for k in range(2):
                        h = 2 * i + k
                        for c in range(CH):
                            chunk(h * CH + c, c, h * J, h * 32 + 16 * (c // 2))

            @block.scalar
            def _(act):
                nc.scalar.preload_act_table_set("natural_log_exp_and_others")
                with act.Fori(0, MH // 2) as i:
                    for k in range(2):
                        for j in range(J):
                            c, kt, first, w, diagonal = shape(j)
                            slot = j % 4
                            act.wait_ge(s_done, (2 * i + k) * J + j + 1)
                            act.wait_ge(pv_done, (2 * i + k) * J + j + 1)
                            if diagonal:
                                nc.scalar.activation(e[0:64, slot, 0:64], psS[slot][0:64, 0:64], ACT.Exp)
                                nc.scalar.activation(e[:, slot, 64:w], psS[slot][:, 64:w], ACT.Exp).then_inc(e_done, 1)
                            else:
                                nc.scalar.activation(e[:, slot], psS[slot][:], ACT.Exp).then_inc(e_done, 1)

            @block.tensor
            def _(pe):
                pe.sem_inc(pv_done, 4)
                pe.sem_inc(h_free, 2)
                pe.wait_ge(set_done, 1)
                pe.wait_ge(c_loaded, 16)
                with pe.Fori(0, MH // 2) as i:
                    for k in range(2):
                        h = 2 * i + k

                        def scores(j):
                            c, kt, first, w, diagonal = shape(j)
                            nc.tensor.matmul(psS[j % 4][:, 0:w], kT[:, k, kt * P:(kt + 1) * P],
                                             qa[:, k, c * QC + first:(c + 1) * QC], start=True, stop=True).then_inc(s_done, 1)

                        def turn(c):
                            pe.wait_ge(oT_ready, h * CH + c + 1)
                            for t in range(QC // P):
                                mm = nc.tensor.transpose(psR[:, t], oT[:, c % 2, t * P:(t + 1) * P], ident[0:VD + 1, 0:VD + 1])
                            mm.then_inc(t_done, 1)

                        pe.wait_ge(loaded[k], 64 * i + 64)
                        scores(0)
                        scores(1)
                        for j in range(J):
                            c, kt, first, w, diagonal = shape(j)
                            if j + 2 < J:
                                scores(j + 2)
                            if c and kt == 3:
                                turn(c - 1)
                            pe.wait_ge(e_done, h * J + j + 1)
                            o = psO[c % 2][0:VD + 1]
                            last = kt == (c + 1) * QC // P - 1
                            if diagonal:
                                nc.tensor.matmul(o[:, first:first + 64], v1[0:64, k, kt], e[0:64, j % 4, 0:64],
                                                 start=(kt == 0), stop=last, skip_group_check=True)
                                mm = nc.tensor.matmul(o[:, first + 64:QC], v1[:, k, kt], e[:, j % 4, 64:w], start=False,
                                                      stop=last, skip_group_check=True)
                            else:
                                mm = nc.tensor.matmul(o[:], v1[:, k, kt], e[:, j % 4], start=(kt == 0), stop=last,
                                                      skip_group_check=True)
                            mm.then_inc(pv_done, 1)
                        turn(CH - 1)
                        pe.sem_inc(h_free, 1)


NG = 5
def stage_gates(nc, d):
    with ExitStack() as stack:
        st = Stage(nc, "G", stack)
        ident = st.sb("ident", [P, P])
        gi = st.sb("gi", [P, NT, 2 * MLH])
        ir = st.sb("ir", [MLH, S])
        fr = st.sb("fr", [MLH, S])
        t0 = st.sb("t0", [MLH, S])
        one = st.sb("one", [MLH, S])
        b = st.sb("b", [MLH, S])
        g = st.sb("g", [MLH, S])
        ends = st.sb("ends", [MLH, NT + 1, P])
        col = st.sb("col", [P, 3, NT, MLH])
        ge = st.sb("ge", [P, NT + 1, MLH])
        out = st.sb("out", [P, NT, NG, MLH])
        ps = st.ps("ps", [P, 2, 2048])
        loaded = st.sem("loaded")
        t_done = st.sem("t_done")
        step = st.sem("step")
        act_step = st.sem("act_step")
        rows_ready = st.sem("rows_ready")
        c_done = st.sem("c_done")
        args_ready = st.sem("args_ready")
        done = st.sem("done")
        stored = st.sem("stored")
        with nc.Block() as block:

            @block.sync
            def _(sp):
                sp.dma_start(ident[:], d["ident"]).then_inc(loaded, 16)
                sp.dma_start(gi[:], d["gi"].rearrange("(t p) c -> p t c", p=P)).then_inc(loaded, 16)
                sp.wait_ge(rows_ready, 1)
                sp.dma_start(d["G"], g[:]).then_inc(stored, 16)
                sp.wait_ge(done, 1)
                sp.dma_start(d["gcols"].rearrange("(t p) c -> p t c", p=P), out[:].rearrange("p t a h -> p t (a h)")).then_inc(stored, 16)
                sp.wait_ge(stored, 32)

            @block.tensor
            def _(pe):
                pe.wait_ge(loaded, 32)
                for a in range(2):
                    for t in range(NT):
                        mm = nc.tensor.transpose(ps[0:MLH, a, t * P:(t + 1) * P], gi[:, t, a * MLH:(a + 1) * MLH], ident[:])
                mm.then_inc(t_done, 1)
                pe.wait_ge(rows_ready, 1)
                for a, src in enumerate((ir, b, g)):
                    for t in range(NT):
                        nc.tensor.transpose(ps[:, 0, (a * NT + t) * MLH:(a * NT + t + 1) * MLH], src[:, t * P:(t + 1) * P],
                                            ident[0:MLH, 0:MLH])
                for t in range(NT + 1):
                    mm = nc.tensor.matmul(ps[:, 1, t * MLH:(t + 1) * MLH], ends[:, t], ident[0:MLH, 0:MLH], start=True, stop=True)
                mm.then_inc(c_done, 1)

            @block.scalar
            def _(act):
                nc.scalar.preload_act_table_set("natural_log_exp_and_others")
                chain = Chain(act, act_step)
                act.wait_ge(step, 4)
                chain.link(nc.scalar.activation(t0[:], t0[:], ACT.Exp, scale=-1.0))
                chain.link(nc.scalar.activation(t0[:], t0[:], ACT.Ln, bias=1.0))
                act.wait_ge(args_ready, 1)
                nc.scalar.activation(out[:, :, 1:NG].rearrange("p t a h -> p t (a h)"),
                                     out[:, :, 1:NG].rearrange("p t a h -> p t (a h)"), ACT.Exp).then_inc(done, 1)

            @block.vector
            def _(dve):
                chain = Chain(dve, step)
                nc.vector.memset(one[:], 1.0)
                chain.link(nc.vector.memset(ends[:], 0.0))
                dve.wait_ge(t_done, 1)
                chain.link(nc.vector.tensor_copy(ir[:], ps[0:MLH, 0]))
                chain.link(nc.vector.tensor_copy(fr[:], ps[0:MLH, 1]))
                chain.link(nc.vector.scalar_tensor_tensor(t0[:], fr[:], -1.0, fr[:], ALU.mult, ALU.max))
                chain.link(nc.vector.tensor_scalar(fr[:], fr[:], 0.0, None, ALU.min))
                dve.wait_ge(act_step, 2)
                chain.link(nc.vector.tensor_tensor(fr[:], fr[:], t0[:], ALU.subtract))
                chain.link(nc.vector.tensor_tensor_scan(b[:], one[:], fr[:], 0.0, ALU.mult, ALU.add))
                chain.link(nc.vector.tensor_tensor(ir[:], ir[:], b[:], ALU.subtract))
                chain.link(nc.vector.tensor_tensor_scan(g[:], ir[:], ir[:], 0.0, ALU.max, ALU.max))
                nc.vector.tensor_copy(ends[:, 1:NT + 1], g[:].rearrange("h (t p) -> h t p", p=P)[:, :, P - 1:P].to_broadcast([MLH, NT, P])).then_inc(rows_ready, 1)
                dve.wait_ge(c_done, 1)
                nc.vector.tensor_copy(col[:].rearrange("p a t h -> p (a t h)"), ps[:, 0, 0:3 * NT * MLH])
                chain.link(nc.vector.tensor_copy(ge[:].rearrange("p t h -> p (t h)"), ps[:, 1, 0:(NT + 1) * MLH]))
                a_, b_, g_ = (col[:, q] for q in range(3))
                nc.vector.tensor_copy(out[:, :, 0], a_)
                nc.vector.tensor_tensor(out[:, :, 1], ge[:, 0:NT], g_, ALU.subtract)
                nc.vector.tensor_tensor(out[:, :, 2], a_, ge[:, 1:NT + 1], ALU.subtract)
                nc.vector.tensor_tensor(out[:, :, 3], ge[:, 0:NT], ge[:, 1:NT + 1], ALU.subtract)
                chain.link(nc.vector.scalar_tensor_tensor(out[:, :, 4], b_, -1.0, g_, ALU.mult, ALU.subtract))
                nc.vector.tensor_scalar(out[:, :, 4], out[:, :, 4], 88.0, None, ALU.min).then_inc(args_ready, 1)


def stage_mlstm(nc, d):
    V1 = MLD + 1
    with ExitStack() as stack:
        st = Stage(nc, "L", stack)
        ident = st.sb("ident", [P, P])
        mask = st.sb("mask", [P, P])
        eps = st.sb("eps", [P, 1])
        wts = st.sb("wts", [P, 3, MLH, MLD])
        cw = st.sb("cw", [P, CONV, ML])
        cb = st.sb("cb", [P, ML])
        hg = st.sb("hg", [P, ML])
        sk = st.sb("sk", [P, ML])
        xs = st.sb("xs", [P, 2, CONV, ML])
        gb = st.sb("gb", [P, 2, MLH, P])
        z = st.sb("z", [P, 2, ML])
        gc = st.sb("gc", [P, 2, NG, MLH])
        ct = st.sb("ct", [P, CONV, ML])
        cx = st.sb("cx", [P, ML])
        xe = st.sb("xe", [P, ML])
        xc = st.sb("xc", [P, 2, ML])
        xcT = st.sb("xcT", [P, MLH, P])
        xmT = st.sb("xmT", [P, MLH, P])
        mq = st.sb("mq", [P, MLH, P])
        mk = st.sb("mk", [P, MLH, P])
        kw = st.sb("kw", [P, MLH, MLD])
        v1 = st.sb("v1", [P, MLH, V1])
        w = st.sb("w", [P, 2, MLH, P])
        pr = st.sb("pr", [P, MLH, P])
        cst = st.sb("cst", [P, MLH, V1])
        ni = st.sb("ni", [P, MLH, V1])
        den = st.sb("den", [P, MLH])
        hh = st.sb("hh", [P, 2, MLH, MLD])
        hs = st.sb("hs", [P, MLH, MLD])
        hst = st.sb("hst", [P, 4, MLH])
        xk = st.sb("xk", [P, ML])
        o = st.sb("o", [P, 2, ML])
        psA, psB, psC, psD = (st.ps(f"ps{q}", [P, MLH, P]) for q in "ABCD")
        psI = st.ps("psI", [P, 2, 512])
        psU = st.ps("psU", [P, 2, 512])
        psN = [psC, psD]

        def pair(ps, b):
            return ps[:, b, 0:2 * V1].rearrange("p (h c) -> p h c", c=V1)

        def pair_n(b):
            return psN[b][:].rearrange("p h c -> p (h c)")[:, 0:2 * V1].rearrange("p (h c) -> p h c", c=V1)

        c_loaded = st.sem("c_loaded")
        set_done = st.sem("set_done")
        w_ready = st.sem("w_ready")
        loaded = [st.sem(f"loaded{k}") for k in range(2)]
        in_free = st.sem("in_free")
        cx_ready = st.sem("cx_ready")
        pool_step = st.sem("pool_step")
        act_step = st.sem("act_step")
        xe_ready = st.sem("xe_ready")
        xc_ready = st.sem("xc_ready")
        dm_ready = st.sem("dm_ready")
        w_exp = st.sem("w_exp")
        w_masked = st.sem("w_masked")
        t_done = st.sem("t_done")
        xT_a = st.sem("xT_a")
        xT_v = st.sem("xT_v")
        qkv_done = st.sem("qkv_done")
        mq_ready = st.sem("mq_ready")
        mk_ready = st.sem("mk_ready")
        kw_ready = st.sem("kw_ready")
        v_ready = st.sem("v_ready")
        qk_done = st.sem("qk_done")
        pr_ready = st.sem("pr_ready")
        n_done = st.sem("n_done")
        u_done = st.sem("u_done")
        c_ready = st.sem("c_ready")
        dve_step = st.sem("dve_step")
        hc_ready = st.sem("hc_ready")
        hv_ready = st.sem("hv_ready")
        hr_ready = st.sem("hr_ready")
        hn_ready = st.sem("hn_ready")
        xk_ready = st.sem("xk_ready")
        o_ready = st.sem("o_ready")
        stored = [st.sem(f"stored{k}") for k in range(2)]

        with nc.Block() as block:

            @block.sync
            def _(sp):
                sp.dma_start(ident[:], d["ident"]).then_inc(c_loaded, 16)
                sp.dma_start(mask[:], d["mask_st"]).then_inc(c_loaded, 16)
                for j, name in enumerate(("w_mq_2", "w_mk_2", "w_mv_2")):
                    sp.dma_start(wts[:, j], d[name].rearrange("a h d e -> d (a h) e")).then_inc(c_loaded, 16)
                for j in range(CONV):
                    sp.dma_start(cw[:, j], to_all(d["conv_w_2"][0, j:j + 1])).then_inc(c_loaded, 16)
                sp.dma_start(cb[:], to_all(d["conv_b_2"])).then_inc(c_loaded, 16)
                sp.dma_start(hg[:], to_all(d["mh_norm_g_2"])).then_inc(c_loaded, 16)
                sp.dma_start(sk[:], to_all(d["ml_skip_2"])).then_inc(c_loaded, 16)

                def load(n, k):
                    count, at = ahead(sp, n + 1, n * P)
                    sp.wait_ge(in_free, count)
                    for j in range(CONV):
                        sp.dma_start(xs[:, k, j], d["xm"][bass.ds(n * P + j, P)]).then_inc(loaded[k], 16)
                    g = bass.AP(tensor=d["G"].tensor, offset=0, ap=[[0, P], [S, MLH], [1, S]])[:, :, bass.ds(at, P)]
                    sp.dma_start(gb[:, k], g).then_inc(loaded[k], 16)
                    sp.dma_start(z[:, k], d["z"][rows_of(n)]).then_inc(loaded[k], 16)
                    sp.dma_start(gc[:, k].rearrange("p a h -> p (a h)"), d["gcols"][rows_of(n)]).then_inc(loaded[k], 16)

                def store(n, k):
                    count, = ahead(sp, n + 1)
                    sp.wait_ge(o_ready, count)
                    sp.dma_start(d["mlo"][rows_of(n)], o[:, k]).then_inc(stored[k], 16)

                for k in range(2):
                    load(k, k)
                with sp.Fori(0, NT // 2 - 1) as i:
                    for k in range(2):
                        store(2 * i + k, k)
                        load(2 * i + k + 2, k)
                for k in range(2):
                    store(NT - 2 + k, k)
                for k in range(2):
                    sp.wait_ge(stored[k], 16 * (NT // 2 + 1))

            @block.gpsimd
            def _(pool):
                chain = Chain(pool, pool_step)
                for k in range(2):
                    pool.sem_inc(stored[k], 16)
                pool.wait_ge(c_loaded, 192)

                def front(n, k, m, first=False):
                    if not first:
                        pool.wait_ge(cx_ready, n)
                    pool.wait_ge(loaded[k], 112 * m)
                    for j in range(CONV):
                        step = nc.gpsimd.tensor_tensor(ct[:, j], xs[:, k, j], cw[:, j], ALU.mult)
                    chain.link(step)
                    nc.gpsimd.tensor_tensor(ct[:, 0], ct[:, 0], ct[:, 1], ALU.add)
                    chain.link(nc.gpsimd.tensor_tensor(ct[:, 2], ct[:, 2], ct[:, 3], ALU.add))
                    chain.link(nc.gpsimd.tensor_tensor(ct[:, 0], ct[:, 0], ct[:, 2], ALU.add))
                    pool.wait_ge(xc_ready, n + 1)
                    nc.gpsimd.tensor_tensor(cx[:], ct[:, 0], cb[:], ALU.add).then_inc(cx_ready, 1)
                    pool.wait_ge(w_exp, n + 1)
                    nc.gpsimd.tensor_tensor(w[:, k], w[:, k], mask[:].unsqueeze(1).to_broadcast([P, MLH, P]),
                                            ALU.mult).then_inc(w_masked, 1)

                def tail(n, k, m):
                    pool.wait_ge(xc_ready, n + 2)
                    chain.link(nc.gpsimd.tensor_tensor(xk[:], xc[:, k], sk[:], ALU.mult))
                    pool.wait_ge(hn_ready, n + 1)
                    pool.wait_ge(stored[k], 16 * m)
                    flat = hh[:, k].rearrange("p h c -> p (h c)")
                    chain.link(nc.gpsimd.tensor_tensor(o[:, k], flat, hg[:], ALU.mult))
                    chain.link(nc.gpsimd.tensor_tensor(o[:, k], o[:, k], xk[:], ALU.add))
                    nc.gpsimd.tensor_tensor(o[:, k], o[:, k], z[:, k], ALU.mult).then_inc(o_ready, 1)
                    pool.wait_ge(o_ready, n + 1)
                    pool.sem_inc(in_free, 1)

                front(0, 0, 1, first=True)
                with pool.Fori(0, NT // 2 - 1) as i:
                    chain.at(12 * i + 3)
                    front(2 * i + 1, 1, i + 1)
                    tail(2 * i, 0, i + 1)
                    front(2 * i + 2, 0, i + 2)
                    tail(2 * i + 1, 1, i + 1)
                    assert chain.n == 12
                chain.at(6 * NT - 12 + 3)
                front(NT - 1, 1, NT // 2)
                tail(NT - 2, 0, NT // 2)
                tail(NT - 1, 1, NT // 2)

            @block.scalar
            def _(act):
                nc.scalar.preload_act_table_set("natural_log_exp_and_others")
                chain = Chain(act, act_step)
                act.wait_ge(set_done, 1)

                def front(n, k):
                    act.wait_ge(dm_ready, n + 1)
                    nc.scalar.activation(w[:, k], w[:, k], ACT.Exp).then_inc(w_exp, 1)
                    act.wait_ge(cx_ready, n + 1)
                    chain.link(nc.scalar.activation(xe[:], cx[:], ACT.Exp, scale=-1.0))
                    chain.link(nc.scalar.activation(xe[:], xe[:], ACT.Ln, bias=1.0))
                    nc.scalar.activation(xe[:], xe[:], ACT.Exp, scale=-1.0).then_inc(xe_ready, 1)

                def copies(n, k):
                    act.wait_ge(t_done, n + 1)
                    nc.scalar.copy(xcT[:], psA[:]).then_inc(xT_a, 1)
                    act.wait_ge(qkv_done, n + 1)
                    nc.scalar.copy(mq[:], psC[:]).then_inc(mq_ready, 1)
                    nc.scalar.copy(v1[:, :, 0:MLD], psI[:, 1].rearrange("p (h c) -> p h c", c=MLD)).then_inc(v_ready, 1)

                def norm(n, k):
                    act.wait_ge(hc_ready, n + 1)
                    nc.scalar.activation(hs[:], hh[:, k], ACT.Square).then_inc(hv_ready, 1)
                    act.wait_ge(hv_ready, 2 * n + 2)
                    chain.link(nc.scalar.activation(hst[:, 2], hst[:, 1], ACT.Ln, scale=1.0 / MLD, bias=eps[:, 0:1]))
                    nc.scalar.activation(hst[:, 3], hst[:, 2], ACT.Exp, scale=-0.5).then_inc(hr_ready, 1)

                def step(n, k):
                    copies(n, k)
                    front(n + 1, 1 - k)
                    norm(n, k)

                front(0, 0)
                with act.Fori(0, NT // 2 - 1) as i:
                    chain.at(6 * i + 2)
                    for k in range(2):
                        step(2 * i + k, k)
                    assert chain.n == 6
                chain.at(3 * NT - 6 + 2)
                step(NT - 2, 0)
                copies(NT - 1, 1)
                norm(NT - 1, 1)

            @block.vector
            def _(dve):
                chain = Chain(dve, dve_step)
                nc.vector.memset(v1[:], 1.0)
                nc.vector.memset(cst[:], 0.0)
                nc.vector.memset(eps[:], EPS).then_inc(set_done, 1)
                dve.sem_inc(in_free, 2)
                dve.sem_inc(xc_ready, 1)
                dve.sem_inc(c_ready, 1)
                dve.wait_ge(c_loaded, 192)
                nc.vector.tensor_scalar(wts[:, 1], wts[:, 1], MLD ** -0.5, None, ALU.mult).then_inc(w_ready, 1)

                def head(k, q):
                    return gc[:, k, q].unsqueeze(2)

                def exponents(n, k, m):
                    dve.wait_ge(loaded[k], 112 * m)
                    chain.link(nc.vector.tensor_tensor(w[:, k], head(k, 0).to_broadcast([P, MLH, P]), gb[:, k], ALU.subtract))
                    nc.vector.tensor_scalar(w[:, k], w[:, k], 0.0, None, ALU.min).then_inc(dm_ready, 1)

                def convolved(n, k):
                    dve.wait_ge(xe_ready, n + 1)
                    nc.vector.tensor_tensor(xc[:, k], cx[:], xe[:], ALU.mult).then_inc(xc_ready, 1)

                def copies(n, k):
                    dve.wait_ge(t_done, n + 1)
                    nc.vector.tensor_copy(xmT[:], psB[:]).then_inc(xT_v, 1)
                    dve.wait_ge(qkv_done, n + 1)
                    nc.vector.tensor_copy(mk[:], psD[:]).then_inc(mk_ready, 1)
                    nc.vector.tensor_tensor(kw[:], psI[:, 0].rearrange("p (h c) -> p h c", c=MLD),
                                            head(k, 2).to_broadcast([P, MLH, MLD]), ALU.mult).then_inc(kw_ready, 1)

                def within(n, k):
                    dve.wait_ge(qk_done, n + 1)
                    dve.wait_ge(w_masked, n + 1)
                    nc.vector.tensor_tensor(pr[:], psA[:], w[:, k], ALU.mult).then_inc(pr_ready, 1)

                def state(n, k):
                    dve.wait_ge(n_done, n + 1)
                    for b in range(2):
                        step = nc.vector.tensor_tensor(ni[:, 2 * b:2 * b + 2], pair(psI, b),
                                                       head(k, 1)[:, 2 * b:2 * b + 2].to_broadcast([P, 2, V1]), ALU.mult)
                    chain.link(step)
                    for b in range(2):
                        step = nc.vector.tensor_tensor(ni[:, 2 * b:2 * b + 2], pair_n(b), ni[:, 2 * b:2 * b + 2], ALU.add)
                    chain.link(step)
                    dve.wait_ge(u_done, n + 1)
                    chain.link(nc.vector.tensor_tensor(cst[:], cst[:], head(k, 3).to_broadcast([P, MLH, V1]), ALU.mult))
                    for b in range(2):
                        step = nc.vector.tensor_tensor(cst[:, 2 * b:2 * b + 2], pair(psU, b), cst[:, 2 * b:2 * b + 2], ALU.add)
                    step.then_inc(c_ready, 1)

                def norm(n, k):
                    chain.link(nc.vector.scalar_tensor_tensor(den[:], ni[:, :, MLD], -1.0, ni[:, :, MLD], ALU.mult, ALU.max))
                    chain.link(nc.vector.tensor_tensor(den[:], den[:], gc[:, k, 4], ALU.max))
                    chain.link(nc.vector.reciprocal(den[:], den[:]))
                    dve.wait_ge(in_free, n + 1)
                    chain.link(nc.vector.tensor_tensor(hh[:, k], ni[:, :, 0:MLD], den[:].unsqueeze(2).to_broadcast([P, MLH, MLD]), ALU.mult))
                    chain.link(nc.vector.reduce_sum(hst[:, 0], hh[:, k], AX_X))
                    chain.link(nc.vector.tensor_scalar(hst[:, 0], hst[:, 0], 1.0 / MLD, None, ALU.mult))
                    chain.link(nc.vector.tensor_tensor(hh[:, k], hh[:, k], hst[:, 0].unsqueeze(2).to_broadcast([P, MLH, MLD]), ALU.subtract))
                    dve.sem_inc(hc_ready, 1)

                def normed(n, k):
                    dve.wait_ge(hv_ready, 2 * n + 1)
                    nc.vector.reduce_sum(hst[:, 1], hs[:], AX_X).then_inc(hv_ready, 1)
                    dve.wait_ge(hr_ready, n + 1)
                    nc.vector.tensor_tensor(hh[:, k], hh[:, k], hst[:, 3].unsqueeze(2).to_broadcast([P, MLH, MLD]), ALU.mult).then_inc(hn_ready, 1)

                def step_of(n, k, m_next):
                    copies(n, k)
                    exponents(n + 1, 1 - k, m_next)
                    within(n, k)
                    state(n, k)
                    convolved(n + 1, 1 - k)
                    norm(n, k)
                    normed(n, k)

                exponents(0, 0, 1)
                convolved(0, 0)
                with dve.Fori(0, NT // 2 - 1) as i:
                    chain.at(22 * i + 1)
                    step_of(2 * i, 0, i + 1)
                    step_of(2 * i + 1, 1, i + 2)
                    assert chain.n == 22, chain.n
                chain.at(11 * NT - 22 + 1)
                step_of(NT - 2, 0, NT // 2)
                copies(NT - 1, 1)
                within(NT - 1, 1)
                state(NT - 1, 1)
                norm(NT - 1, 1)
                normed(NT - 1, 1)

            @block.tensor
            def _(pe):
                pe.wait_ge(c_loaded, 192)
                pe.wait_ge(w_ready, 1)
                with pe.Fori(0, NT // 2) as i:
                    for k in range(2):
                        n = 2 * i + k
                        pe.wait_ge(xc_ready, n + 2)
                        for h in range(MLH):
                            nc.tensor.transpose(psB[:, h], xs[:, k, CONV - 1, h * P:(h + 1) * P], ident[:])
                        for h in range(MLH):
                            t = nc.tensor.transpose(psA[:, h], xc[:, k, h * P:(h + 1) * P], ident[:])
                        t.then_inc(t_done, 1)
                        pe.wait_ge(xT_a, n + 1)
                        pe.wait_ge(xT_v, n + 1)
                        pe.wait_ge(c_ready, n + 1)
                        for h in range(MLH):
                            nc.tensor.matmul(psC[:, h], wts[:, 0, h], xcT[:, h], start=True, stop=True)
                            nc.tensor.matmul(psD[:, h], wts[:, 1, h], xcT[:, h], start=True, stop=True)
                            nc.tensor.matmul(psI[:, 0, h * P:(h + 1) * P], xcT[:, h], wts[:, 1, h], start=True, stop=True)
                            mm = nc.tensor.matmul(psI[:, 1, h * P:(h + 1) * P], xmT[:, h], wts[:, 2, h], start=True, stop=True)
                        mm.then_inc(qkv_done, 1)
                        pe.wait_ge(mq_ready, n + 1)
                        pe.wait_ge(mk_ready, n + 1)
                        for h in range(MLH):
                            mm = nc.tensor.matmul(psA[:, h], mk[:, h], mq[:, h], start=True, stop=True)
                        mm.then_inc(qk_done, 1)
                        pe.wait_ge(kw_ready, n + 1)
                        pe.wait_ge(v_ready, n + 1)
                        for h in range(MLH):
                            nc.tensor.matmul(pair(psI, h // 2)[:, h % 2], mq[:, h], cst[:, h], start=True, stop=True)
                        for h in range(MLH):
                            mm = nc.tensor.matmul(pair(psU, h // 2)[:, h % 2], kw[:, h], v1[:, h], start=True, stop=True)
                        mm.then_inc(u_done, 1)
                        pe.wait_ge(pr_ready, n + 1)
                        for h in range(MLH):
                            mm = nc.tensor.matmul(pair_n(h // 2)[:, h % 2], pr[:, h], v1[:, h], start=True, stop=True)
                        mm.then_inc(n_done, 1)


def stage_route(nc, d):
    NL = GRP + NE
    BIG = 1e30
    ROUND = 1.5 * 2 ** 23
    with ExitStack() as stack:
        st = Stage(nc, "T", stack)
        ident = st.sb("ident", [P, P])
        tri = st.sb("tri", [P, P])
        ones = st.sb("ones", [P, P])
        wr = st.sb("wr", [P, KD, NL])
        br = st.sb("br", [P, NL])
        io = st.sb("io", [P, 2, NE])
        iob = st.sb("iob", [P, NBLK])
        pcol = st.sb("pcol", [P, 1])
        tok = st.sb("tok", [P, NT], I32)
        x = st.sb("x", [P, 2, D])
        xT = st.sb("xT", [P, 2, KD, P])
        lg = st.sb("lg", [P, NE])
        g8 = st.sb("g8", [P, 8])
        gm = st.sb("gm", [P, 8])
        gidx = st.sb("gidx", [P, 8], U32)
        gf = st.sb("gf", [P, 8])
        gneg = st.sb("gneg", [P, 1])
        ge = st.sb("ge", [P, GRP])
        gs = st.sb("gs", [P, 4])
        sel = st.sb("sel", [P, NE])
        pen = st.sb("pen", [P, NE])
        em = st.sb("em", [P, NE])
        spare = st.sb("spare", [P, 1])
        e8 = st.sb("e8", [P, 8])
        eidx = st.sb("eidx", [P, 8], U32)
        ef = st.sb("ef", [P, 8])
        tw = st.sb("tw", [P, 4])
        oh = st.sb("oh", [P, NT, 2, NE])
        both = st.sb("both", [P, NE])
        acc = st.sb("acc", [P, NE])
        prod = st.sb("prod", [P, 2, NE])
        rank = st.sb("rank", [P, NT, 2])
        wts = st.sb("wts", [P, NT, 2])
        nb = st.sb("nb", [P, NE])
        one = st.sb("one", [P, NE])
        ends = st.sb("ends", [P, NE])
        cmp = st.sb("cmp", [P, NBLK, NE])
        be = st.sb("be", [P, NBLK])
        wi = st.sb("wi", [P, NBLK], I32)
        big = st.sb("big", [P, NT, 2, NE])
        dest = st.sb("dest", [P, NT, 2])
        desti = st.sb("desti", [P, NT, 2], I32)
        db = st.sb("db", [P, NT, 2])
        addr = st.sb("addr", [P, NT, 2], I32)
        zero = st.sb("zero", [P, NBLK], I32)
        psT = st.ps("psT", [P, KD, P])
        psL = st.ps("psL", [P, 512])
        psR = st.ps("psR", [P, 512])
        c_loaded = st.sem("c_loaded")
        loaded = [st.sem(f"loaded{k}") for k in range(2)]
        in_free = st.sem("in_free")
        t_done = st.sem("t_done")
        xT_a = st.sem("xT_a")
        xT_v = st.sem("xT_v")
        l_done = st.sem("l_done")
        set_done = st.sem("set_done")
        step = st.sem("step")
        act_in = st.sem("act_in")
        act_out = st.sem("act_out")
        both_ready = st.sem("both_ready")
        r_done = st.sem("r_done")
        acc_ready = st.sem("acc_ready")
        addr_ready = st.sem("addr_ready")
        zero_stored = st.sem("zero_stored")
        scattered = st.sem("scattered")
        stored = st.sem("stored")
        with nc.Block() as block:

            @block.sync
            def _(sp):
                for name, t in (("ident", ident), ("tri", tri), ("ones", ones), ("iota_e", io), ("iota_b", iob), ("iota_p", pcol), ("tokens", tok)):
                    sp.dma_start(t[:], d[name]).then_inc(c_loaded, 16)
                sp.dma_start(wr[:, :, 0:GRP], d["w_router_group_2"].rearrange("a (k p) n -> p (a k) n", p=P)).then_inc(c_loaded, 16)
                sp.dma_start(wr[:, :, GRP:NL], d["w_router_expert_2"].rearrange("a (k p) n -> p (a k) n", p=P)).then_inc(c_loaded, 16)
                sp.dma_start(br[:, 0:GRP], to_all(d["b_router_group_2"])).then_inc(c_loaded, 16)
                sp.dma_start(br[:, GRP:NL], to_all(d["b_router_expert_2"])).then_inc(c_loaded, 16)
                sp.wait_ge(set_done, 1)
                sp.dma_start(d["rowtok"], zero[:]).then_inc(zero_stored, 16)
                with sp.Fori(0, NT // 2) as i:
                    for k in range(2):
                        count, at = ahead(sp, 2 * i + k + 1, (2 * i + k) * P)
                        sp.wait_ge(in_free, count)
                        sp.dma_start(x[:, k], d["hf"][bass.ds(at, P)]).then_inc(loaded[k], 16)
                sp.wait_ge(addr_ready, 1)
                sp.dma_start(d["widx"], wi[:]).then_inc(stored, 16)
                sp.dma_start(d["dest"], desti[:].rearrange("p t k -> p (t k)")).then_inc(stored, 16)
                sp.dma_start(d["wts"], wts[:].rearrange("p t k -> p (t k)")).then_inc(stored, 16)
                sp.wait_ge(stored, 48)

            @block.gpsimd
            def _(pool):
                pool.wait_ge(zero_stored, 16)
                pool.wait_ge(addr_ready, 1)
                table = d["rowtok"].rearrange("p (b a) -> (p b) a", a=1)
                for t in range(NT):
                    for k in range(2):
                        pool.indirect_dma_start(table, bass.IndirectOffsetOnAxis(addr[:, t, k:k + 1], 0), tok[:, t:t + 1], None).then_inc(scattered, 16)
                pool.wait_ge(scattered, 16 * 2 * NT)

            @block.tensor
            def _(pe):
                pe.sem_inc(in_free, 2)
                pe.wait_ge(c_loaded, 176)
                pe.wait_ge(set_done, 1)
                with pe.Fori(0, NT // 2) as i:
                    for k in range(2):
                        n = 2 * i + k
                        pe.wait_ge(loaded[k], 16 * i + 16)
                        for kd in range(KD):
                            t = nc.tensor.transpose(psT[:, kd], x[:, k, kd * P:(kd + 1) * P], ident[:])
                        t.then_inc(t_done, 1)
                        pe.wait_ge(t_done, n + 1)
                        pe.sem_inc(in_free, 1)
                        pe.wait_ge(xT_a, n + 1)
                        pe.wait_ge(xT_v, n + 1)
                        for kd in range(KD):
                            mm = nc.tensor.matmul(psL[:, 0:NL], xT[:, k, kd], wr[:, kd], start=(kd == 0), stop=(kd == KD - 1))
                        mm.then_inc(l_done, 1)
                        pe.wait_ge(both_ready, n + 1)
                        nc.tensor.matmul(psR[:, 0:NE], tri[:], both[:], start=True, stop=False)
                        nc.tensor.matmul(psR[:, 0:NE], ones[:], acc[:], start=False, stop=True).then_inc(r_done, 1)
                pe.wait_ge(acc_ready, NT)
                nc.tensor.matmul(psR[:, 0:NE], ones[:], acc[:], start=True, stop=True).then_inc(r_done, 1)

            @block.scalar
            def _(act):
                nc.scalar.preload_act_table_set("natural_log_exp_and_others")
                with act.Fori(0, NT // 2) as i:
                    for k in range(2):
                        n = 2 * i + k
                        act.wait_ge(t_done, n + 1)
                        nc.scalar.copy(xT[:, k, KD // 2:KD], psT[:, KD // 2:KD]).then_inc(xT_a, 1)
                        act.wait_ge(act_in, n + 1)
                        nc.scalar.activation(ge[:], g8[:, 0:GRP], ACT.Exp, bias=gneg[:, 0:1], accum_out=gs[:, 0:1])
                        nc.scalar.activation(tw[:, 1:2], tw[:, 0:1], ACT.Exp).then_inc(act_out, 1)

            @block.vector
            def _(dve):
                chain = Chain(dve, step)
                nc.vector.memset(zero[:], 0)
                nc.vector.memset(one[:], 1.0)
                nc.vector.memset(acc[:], 0.0)
                nc.vector.memset(g8[:], -BIG).then_inc(set_done, 1)
                dve.wait_ge(c_loaded, 176)
                LINKS = 19
                with dve.Fori(0, NT // 2) as i:
                    for k in range(2):
                        n = 2 * i + k
                        if k == 0:
                            chain.at(2 * LINKS * i)
                        dve.wait_ge(t_done, n + 1)
                        nc.vector.tensor_copy(xT[:, k, 0:KD // 2], psT[:, 0:KD // 2]).then_inc(xT_v, 1)
                        dve.wait_ge(l_done, n + 1)
                        chain.link(nc.vector.tensor_tensor(g8[:, 0:GRP], psL[:, 0:GRP], br[:, 0:GRP], ALU.add))
                        nc.vector.tensor_tensor(lg[:], psL[:, GRP:NL], br[:, GRP:NL], ALU.add)
                        chain.link(nc.vector.max(gm[:], g8[:]))
                        nc.vector.tensor_scalar(gneg[:], gm[:, 0:1], -1.0, None, ALU.mult)
                        chain.link(nc.vector.max_index(gidx[:], gm[:], g8[:]))
                        chain.link(nc.vector.tensor_copy(gf[:], gidx[:]))
                        chain.link(nc.vector.tensor_scalar(sel[:], io[:, 1], gf[:, 0:1], None, ALU.is_equal))
                        chain.link(nc.vector.tensor_scalar(pen[:], sel[:], BIG, -BIG, ALU.mult, ALU.add))
                        chain.link(nc.vector.tensor_tensor(em[:], lg[:], sel[:], ALU.mult))
                        chain.link(nc.vector.tensor_tensor(em[:], em[:], pen[:], ALU.add))
                        nc.vector.tensor_copy(spare[:], one[:, 0:1])
                        chain.link(nc.vector.max(e8[:], em[:]))
                        nc.vector.tensor_tensor(tw[:, 0:1], e8[:, 1:2], e8[:, 0:1], ALU.subtract).then_inc(act_in, 1)
                        chain.link(nc.vector.max_index(eidx[:], e8[:], em[:]))
                        chain.link(nc.vector.tensor_copy(ef[:], eidx[:]))
                        for q in range(2):
                            step_ = nc.vector.tensor_scalar(oh[:, bass.ds(n, 1), q], io[:, 0:1], ef[:, q:q + 1], None, ALU.is_equal)
                        chain.link(step_)
                        nc.vector.tensor_tensor(both[:].unsqueeze(1), oh[:, bass.ds(n, 1), 0], oh[:, bass.ds(n, 1), 1], ALU.add).then_inc(both_ready, 1)
                        dve.wait_ge(act_out, n + 1)
                        chain.link(nc.vector.tensor_scalar(tw[:, 2:3], tw[:, 1:2], 1.0, None, ALU.add))
                        chain.link(nc.vector.tensor_tensor(tw[:, 2:3], tw[:, 2:3], gs[:, 0:1], ALU.mult))
                        chain.link(nc.vector.reciprocal(tw[:, 2:3], tw[:, 2:3]))
                        chain.link(nc.vector.tensor_tensor(tw[:, 3:4], tw[:, 2:3], tw[:, 1:2], ALU.mult))
                        nc.vector.tensor_copy(wts[:, bass.ds(n, 1)], tw[:, 2:4].unsqueeze(1))
                        dve.wait_ge(r_done, n + 1)
                        chain.link(nc.vector.tensor_tensor(prod[:].unsqueeze(1), oh[:, bass.ds(n, 1)],
                                                           psR[:, 0:NE].unsqueeze(1).unsqueeze(1).to_broadcast([P, 1, 2, NE]), ALU.mult))
                        chain.link(nc.vector.reduce_sum(rank[:, bass.ds(n, 1)], prod[:].unsqueeze(1), AX_X))
                        chain.link(nc.vector.tensor_tensor(acc[:], acc[:], both[:], ALU.add))
                        dve.sem_inc(acc_ready, 1)
                    assert chain.n == 2 * LINKS, chain.n
                chain.at(LINKS * NT)
                dve.wait_ge(r_done, NT + 1)
                chain.link(nc.vector.tensor_scalar(nb[:], psR[:, 0:NE], 63.5, 1.0 / P, ALU.add, ALU.mult))
                chain.link(nc.vector.tensor_scalar(nb[:], nb[:], ROUND, -ROUND, ALU.add, ALU.add))
                chain.link(nc.vector.tensor_tensor_scan(ends[:], one[:], nb[:], 0.0, ALU.mult, ALU.add))
                chain.link(nc.vector.tensor_tensor(cmp[:], ends[:].unsqueeze(1).to_broadcast([P, NBLK, NE]),
                                                   iob[:].unsqueeze(2).to_broadcast([P, NBLK, NE]), ALU.is_le))
                chain.link(nc.vector.reduce_sum(be[:], cmp[:], AX_X))
                chain.link(nc.vector.tensor_scalar(be[:], be[:], float(NE - 1), float(P), ALU.min, ALU.mult))
                chain.link(nc.vector.tensor_scalar(be[:], be[:], pcol[:, 0:1], None, ALU.add))
                chain.link(nc.vector.tensor_copy(wi[:], be[:]))
                chain.link(nc.vector.tensor_tensor(nb[:], ends[:], nb[:], ALU.subtract))
                chain.link(nc.vector.tensor_scalar(nb[:], nb[:], float(P), None, ALU.mult))
                for q in range(2):
                    step_ = nc.vector.tensor_tensor(big[:, :, q], oh[:, :, q], nb[:].unsqueeze(1).to_broadcast([P, NT, NE]), ALU.mult)
                chain.link(step_)
                chain.link(nc.vector.reduce_sum(dest[:], big[:], AX_X))
                chain.link(nc.vector.tensor_tensor(dest[:], dest[:], rank[:], ALU.add))
                chain.link(nc.vector.tensor_copy(desti[:], dest[:]))
                chain.link(nc.vector.tensor_scalar(db[:], dest[:], -63.5, 1.0 / P, ALU.add, ALU.mult))
                chain.link(nc.vector.tensor_scalar(db[:], db[:], ROUND, -ROUND, ALU.add, ALU.add))
                chain.link(nc.vector.tensor_scalar(dest[:], dest[:], float(NBLK), None, ALU.mult))
                chain.link(nc.vector.scalar_tensor_tensor(dest[:], db[:], -float(P * NBLK - 1), dest[:], ALU.mult, ALU.add))
                nc.vector.tensor_copy(addr[:], dest[:]).then_inc(addr_ready, 1)


def stage_experts(nc, d):
    KE = DE // P
    NB = 4
    with ExitStack() as stack:
        st = Stage(nc, "X", stack)
        ident = st.sb("ident", [P, P])
        rt = st.sb("rt", [P, NBLK], I32)
        none = st.sb("none", [P, 2], I32)
        wi = st.sb("wi", [P, NBLK], I32)
        ix = st.sb("ix", [P, NB, 2], I32)
        x = st.sb("x", [P, NB, D])
        wg = st.sb("wg", [P, NB, KD * DE])
        wu = st.sb("wu", [P, NB, KD * DE])
        wd = st.sb("wd", [P, NB, KE * D])
        xT = st.sb("xT", [P, 2, KD, P])
        se = st.sb("se", [P, DE])
        sg = st.sb("sg", [P, DE])
        a = st.sb("a", [P, DE])
        aT = st.sb("aT", [P, KE, P])
        y = st.sb("y", [P, 2, D])
        psT = st.ps("psT", [P, KD, P])
        psG = [st.ps(f"psG{k}", [P, 2, DE]) for k in range(2)]
        psA = st.ps("psA", [P, KE, P])
        psY = st.ps("psY", [P, D])
        c_loaded = st.sem("c_loaded")
        ix_ready = st.sem("ix_ready")
        none_set = st.sem("none_set")
        x_loaded = [st.sem(f"x_loaded{k}") for k in range(NB)]
        gu_loaded = [st.sem(f"gu_loaded{k}") for k in range(NB)]
        wd_loaded = [st.sem(f"wd_loaded{k}") for k in range(NB)]
        t_done = st.sem("t_done")
        xT_a = st.sem("xT_a")
        xT_v = st.sem("xT_v")
        g_done = st.sem("g_done")
        act_step = st.sem("act_step")
        se_ready = st.sem("se_ready")
        dve_step = st.sem("dve_step")
        a_ready = st.sem("a_ready")
        at_done = st.sem("at_done")
        aT_ready = st.sem("aT_ready")
        y_done = st.sem("y_done")
        y_a = st.sem("y_a")
        y_v = st.sem("y_v")
        stored = [st.sem(f"stored{k}") for k in range(2)]
        views = {
            "wg": d["w_gate_e_2"].rearrange("a e (p k) f -> (a e p) (k f)", p=P),
            "wu": d["w_up_e_2"].rearrange("a e (p k) f -> (a e p) (k f)", p=P),
            "wd": d["w_down_e_2"].rearrange("a e (p k) f -> (a e p) (k f)", p=P),
        }
        with nc.Block() as block:

            @block.gpsimd
            def _(pool):
                nc.gpsimd.memset(none[:], 0).then_inc(none_set, 1)
                pool.wait_ge(none_set, 1)
                pool.wait_ge(c_loaded, 48)

                def load(n, k, free):
                    if free:
                        pool.wait_ge(y_done, n - (NB - 1))
                    nc.gpsimd.tensor_tensor(ix[:, k, 0:1], rt[:, bass.ds(n, 1)], none[:, 0:1], ALU.add)
                    nc.gpsimd.tensor_tensor(ix[:, k, 1:2], wi[:, bass.ds(n, 1)], none[:, 0:1], ALU.add).then_inc(ix_ready, 1)
                    pool.wait_ge(ix_ready, n + 1)
                    nc.gpsimd.tensor_tensor(none[:, 1:2], none[:, 0:1], none[:, 0:1], ALU.add)
                    rows = bass.IndirectOffsetOnAxis(ix[:, k, 0:1], 0)
                    weights = bass.IndirectOffsetOnAxis(ix[:, k, 1:2], 0)
                    pool.indirect_dma_start(x[:, k], None, d["hf"], rows).then_inc(x_loaded[k], 16)
                    pool.indirect_dma_start(wg[:, k], None, views["wg"], weights).then_inc(gu_loaded[k], 16)
                    pool.indirect_dma_start(wu[:, k], None, views["wu"], weights).then_inc(gu_loaded[k], 16)
                    pool.indirect_dma_start(wd[:, k], None, views["wd"], weights).then_inc(wd_loaded[k], 16)

                for k in range(NB):
                    load(k, k, False)
                with pool.Fori(1, NBLK // NB) as i:
                    for k in range(NB):
                        load(NB * i + k, k, True)

            @block.sync
            def _(sp):
                sp.dma_start(ident[:], d["ident"]).then_inc(c_loaded, 16)
                sp.dma_start(rt[:], d["rowtok"]).then_inc(c_loaded, 16)
                sp.dma_start(wi[:], d["widx"]).then_inc(c_loaded, 16)
                with sp.Fori(0, NBLK // 2) as i:
                    for k in range(2):
                        n = 2 * i + k
                        count, at = ahead(sp, n + 2, n * P)
                        sp.wait_ge(y_a, count)
                        sp.wait_ge(y_v, count)
                        sp.dma_start(d["y"][bass.ds(at, P)], y[:, k]).then_inc(stored[k], 16)
                for k in range(2):
                    sp.wait_ge(stored[k], 16 * (NBLK // 2 + 1))

            @block.tensor
            def _(pe):
                pe.wait_ge(c_loaded, 48)

                def front(n, b, m):
                    k = b % 2
                    pe.wait_ge(x_loaded[b], 16 * m)
                    cols = x[:, b].rearrange("p (c k) -> p k c", k=KD)
                    for kd in range(KD):
                        t = nc.tensor.transpose(psT[:, kd], cols[:, kd], ident[:])
                    t.then_inc(t_done, 1)
                    pe.wait_ge(gu_loaded[b], 32 * m)
                    pe.wait_ge(xT_a, n + 1)
                    pe.wait_ge(xT_v, n + 1)
                    for q, w in enumerate((wg, wu)):
                        for kd in range(KD):
                            mm = nc.tensor.matmul(psG[k][:, q], xT[:, k, kd], w[:, b, kd * DE:(kd + 1) * DE],
                                                  start=(kd == 0), stop=(kd == KD - 1))
                    mm.then_inc(g_done, 1)

                def back(n, b, m):
                    pe.wait_ge(a_ready, n + 2)
                    cols = a[:].rearrange("p (c j) -> p j c", j=KE)
                    for j in range(KE):
                        t = nc.tensor.transpose(psA[:, j], cols[:, j], ident[:])
                    t.then_inc(at_done, 1)
                    pe.wait_ge(wd_loaded[b], 16 * m)
                    pe.wait_ge(y_a, n + 1)
                    pe.wait_ge(y_v, n + 1)
                    pe.wait_ge(aT_ready, n + 1)
                    for half in range(2):
                        for j in range(KE):
                            mm = nc.tensor.matmul(psY[:, half * 512:(half + 1) * 512], aT[:, j],
                                                  wd[:, b, j * D + half * 512:j * D + (half + 1) * 512],
                                                  start=(j == 0), stop=(j == KE - 1))
                    mm.then_inc(y_done, 1)

                front(0, 0, 1)
                with pe.Fori(0, NBLK // NB - 1) as i:
                    for k in range(NB):
                        front(NB * i + k + 1, (k + 1) % NB, i + 1 + (k + 1) // NB)
                        back(NB * i + k, k, i + 1)
                for k in range(NB):
                    if k + 1 < NB:
                        front(NBLK - NB + k + 1, k + 1, NBLK // NB)
                    back(NBLK - NB + k, k, NBLK // NB)

            @block.scalar
            def _(act):
                nc.scalar.preload_act_table_set("natural_log_exp_and_others")
                chain = Chain(act, act_step)
                for k in range(2):
                    act.sem_inc(stored[k], 16)
                act.sem_inc(y_a, 1)

                def front(n, k):
                    act.wait_ge(t_done, n + 1)
                    nc.scalar.copy(xT[:, k, KD // 2:KD], psT[:, KD // 2:KD]).then_inc(xT_a, 1)
                    act.wait_ge(g_done, n + 1)
                    act.wait_ge(a_ready, n + 1)
                    chain.link(nc.scalar.activation(se[:], psG[k][:, 0], ACT.Exp, scale=-1.0))
                    chain.link(nc.scalar.activation(se[:], se[:], ACT.Ln, bias=1.0))
                    nc.scalar.activation(se[:], se[:], ACT.Exp, scale=-1.0).then_inc(se_ready, 1)

                def back(n, k, m):
                    act.wait_ge(y_done, n + 1)
                    act.wait_ge(stored[k], 16 * m)
                    nc.scalar.copy(y[:, k, 0:512], psY[:, 0:512]).then_inc(y_a, 1)

                front(0, 0)
                with act.Fori(0, NBLK // 2 - 1) as i:
                    chain.at(4 * i + 2)
                    front(2 * i + 1, 1)
                    back(2 * i, 0, i + 1)
                    front(2 * i + 2, 0)
                    back(2 * i + 1, 1, i + 1)
                chain.at(4 * (NBLK // 2 - 1) + 2)
                front(NBLK - 1, 1)
                back(NBLK - 2, 0, NBLK // 2)
                back(NBLK - 1, 1, NBLK // 2)

            @block.vector
            def _(dve):
                chain = Chain(dve, dve_step)
                dve.sem_inc(y_v, 1)
                dve.sem_inc(a_ready, 1)

                def turned(n, k):
                    dve.wait_ge(t_done, n + 1)
                    nc.vector.tensor_copy(xT[:, k, 0:KD // 2], psT[:, 0:KD // 2]).then_inc(xT_v, 1)

                def gated(n, k):
                    dve.wait_ge(se_ready, n + 1)
                    chain.link(nc.vector.tensor_tensor(sg[:], psG[k][:, 0], se[:], ALU.mult))
                    nc.vector.tensor_tensor(a[:], psG[k][:, 1], sg[:], ALU.mult).then_inc(a_ready, 1)

                def a_turned(n):
                    dve.wait_ge(at_done, n + 1)
                    nc.vector.tensor_copy(aT[:], psA[:]).then_inc(aT_ready, 1)

                def evacuate(n, k, m):
                    dve.wait_ge(y_done, n + 1)
                    dve.wait_ge(stored[k], 16 * m)
                    nc.vector.tensor_copy(y[:, k, 512:D], psY[:, 512:D]).then_inc(y_v, 1)

                def step(n, k, m):
                    turned(n + 1, 1 - k)
                    a_turned(n)
                    gated(n + 1, 1 - k)
                    evacuate(n, k, m)

                turned(0, 0)
                gated(0, 0)
                with dve.Fori(0, NBLK // 2 - 1) as i:
                    chain.at(2 * i + 1)
                    step(2 * i, 0, i + 1)
                    step(2 * i + 1, 1, i + 1)
                chain.at(2 * (NBLK // 2 - 1) + 1)
                step(NBLK - 2, 0, NBLK // 2)
                a_turned(NBLK - 1)
                evacuate(NBLK - 1, 1, NBLK // 2)


def stage_final(nc, d, out):
    KP = PD // P
    with ExitStack() as stack:
        st = Stage(nc, "Z", stack)
        ident = st.sb("ident", [P, P])
        eps = st.sb("eps", [P, 1])
        gain = st.sb("gain", [P, KD])
        fg = st.sb("fg", [P, D])
        wg = st.sb("wg", [P, KD, D])
        wp = st.sb("wp", [P, KP, D])
        dest = st.sb("dest", [P, 2 * NT], I32)
        none = st.sb("none", [P, 2], I32)
        wts = st.sb("wts", [P, 2 * NT])
        ix = st.sb("ix", [P, 2, 2], I32)
        wc = st.sb("wc", [P, 2, 2])
        x = st.sb("x", [P, 2, D])
        pt = st.sb("pt", [P, 2, PD])
        y = st.sb("y", [P, 2, 2, D])
        x3 = st.sb("x3", [P, 2, D])
        sq = st.sb("sq", [P, D])
        stat = st.sb("stat", [P, 2, 8])
        u = st.sb("u", [P, D])
        uT = st.sb("uT", [P, KD, P])
        pT = st.sb("pT", [P, KP, P])
        sg = st.sb("sg", [P, D])
        x4 = st.sb("x4", [P, D])
        o = st.sb("o", [P, 2, D])
        psT = st.ps("psT", [P, KD, P])
        psP = st.ps("psP", [P, KP, P])
        psG = st.ps("psG", [P, D])
        psE = st.ps("psE", [P, D])
        c_loaded = st.sem("c_loaded")
        w_loaded = st.sem("w_loaded")
        w_scaled = st.sem("w_scaled")
        eps_set = st.sem("eps_set")
        loaded = [st.sem(f"loaded{k}") for k in range(2)]
        ix_ready = st.sem("ix_ready")
        none_set = st.sem("none_set")
        y_loaded = [st.sem(f"y_loaded{k}") for k in range(2)]
        in_free = st.sem("in_free")
        dve_step = st.sem("dve_step")
        act_step = st.sem("act_step")
        x3_ready = st.sem("x3_ready")
        r_ready = st.sem("r_ready")
        u_ready = st.sem("u_ready")
        t_done = st.sem("t_done")
        uT_a = st.sem("uT_a")
        uT_v = st.sem("uT_v")
        g_done = st.sem("g_done")
        e_done = st.sem("e_done")
        l_ready = st.sem("l_ready")
        m_ready = st.sem("m_ready")
        s_ready = st.sem("s_ready")
        x4_ready = st.sem("x4_ready")
        r4_ready = st.sem("r4_ready")
        o_ready = st.sem("o_ready")
        stored = [st.sem(f"stored{k}") for k in range(2)]
        out_rows = out.rearrange("a s m -> (a s) m")
        with nc.Block() as block:

            @block.sync
            def _(sp):
                sp.dma_start(ident[:], d["ident"]).then_inc(c_loaded, 16)
                sp.dma_start(dest[:], d["dest"]).then_inc(c_loaded, 16)
                sp.dma_start(wts[:], d["wts"]).then_inc(c_loaded, 16)
                sp.dma_start(gain[:], d["norm_ple_g_2"].rearrange("a (k p) -> p (a k)", p=P), allow_slow_non_contiguous=True).then_inc(c_loaded, 16)
                sp.dma_start(fg[:], to_all(d["final_g2_row"])).then_inc(c_loaded, 16)

                def load(n, k):
                    count, = ahead(sp, n + 1)
                    sp.wait_ge(in_free, count)
                    sp.dma_start(x[:, k], d["x2"][rows_of(n)]).then_inc(loaded[k], 16)
                    sp.dma_start(pt[:, k], d["p_rows"][rows_of(n)]).then_inc(loaded[k], 16)

                def store(n, k):
                    count, at = ahead(sp, n + 1, n * P)
                    sp.wait_ge(o_ready, count)
                    sp.dma_start(out_rows[bass.ds(at, P)], o[:, k]).then_inc(stored[k], 16)

                for k in range(2):
                    load(k, k)
                for kd in range(KD):
                    sp.dma_start(wg[:, kd], d["w_ple_gate_2"][0, kd * P:(kd + 1) * P]).then_inc(w_loaded, 16)
                for kd in range(KP):
                    sp.dma_start(wp[:, kd], d["w_ple_2"][0, kd * P:(kd + 1) * P]).then_inc(w_loaded, 16)
                with sp.Fori(0, NT // 2 - 1) as i:
                    for k in range(2):
                        store(2 * i + k, k)
                        load(2 * i + k + 2, k)
                for k in range(2):
                    store(NT - 2 + k, k)
                for k in range(2):
                    sp.wait_ge(stored[k], 16 * (NT // 2 + 1))

            @block.gpsimd
            def _(pool):
                nc.gpsimd.memset(none[:], 0).then_inc(none_set, 1)
                pool.wait_ge(none_set, 1)
                pool.wait_ge(c_loaded, 80)

                def gather(n, k, free):
                    if free:
                        pool.wait_ge(x3_ready, n - 1)
                    nc.gpsimd.tensor_tensor(ix[:, k], dest[:, bass.ds(n * 2, 2)], none[:, 0:1].to_broadcast([P, 2]), ALU.add)
                    nc.gpsimd.tensor_copy(wc[:, k], wts[:, bass.ds(n * 2, 2)]).then_inc(ix_ready, 1)
                    pool.wait_ge(ix_ready, n + 1)
                    nc.gpsimd.tensor_tensor(none[:, 1:2], none[:, 0:1], none[:, 0:1], ALU.add)
                    for q in range(2):
                        pool.indirect_dma_start(y[:, k, q], None, d["y"], bass.IndirectOffsetOnAxis(ix[:, k, q:q + 1], 0)).then_inc(y_loaded[k], 16)

                for k in range(2):
                    gather(k, k, False)
                with pool.Fori(1, NT // 2) as i:
                    for k in range(2):
                        gather(2 * i + k, k, True)

            @block.scalar
            def _(act):
                nc.scalar.preload_act_table_set("natural_log_exp_and_others")
                chain = Chain(act, act_step)
                act.wait_ge(eps_set, 1)
                with act.Fori(0, NT // 2) as i:
                    for k in range(2):
                        n = 2 * i + k
                        if k == 0:
                            chain.at(14 * i)
                        act.wait_ge(x3_ready, n + 1)
                        chain.link(nc.scalar.activation(sq[:], x3[:, k], ACT.Square, accum_out=stat[:, k, 0:1]))
                        chain.link(nc.scalar.activation(stat[:, k, 1:2], stat[:, k, 0:1], ACT.Ln, scale=1.0 / D, bias=eps[:, 0:1]))
                        chain.link(nc.scalar.activation(stat[:, k, 2:3], stat[:, k, 1:2], ACT.Exp, scale=-0.5))
                        act.wait_ge(t_done, n + 1)
                        nc.scalar.mul(u[:], x3[:, k], stat[:, k, 2:3]).then_inc(u_ready, 1)
                        act.wait_ge(t_done, n + 2)
                        nc.scalar.copy(uT[:, KD // 2:KD], psT[:, KD // 2:KD]).then_inc(uT_a, 1)
                        act.wait_ge(g_done, n + 1)
                        act.wait_ge(x4_ready, n + 1)
                        chain.link(nc.scalar.activation(sg[:], psG[:], ACT.Abs))
                        chain.link(nc.scalar.activation(sg[:], sg[:], ACT.Exp, scale=-1.0))
                        nc.scalar.activation(sg[:], sg[:], ACT.Ln, bias=1.0).then_inc(l_ready, 1)
                        act.wait_ge(m_ready, n + 1)
                        nc.scalar.activation(sg[:], sg[:], ACT.Exp).then_inc(s_ready, 1)
                        act.wait_ge(x4_ready, n + 2)
                        chain.link(nc.scalar.activation(sq[:], x4[:], ACT.Square, accum_out=stat[:, k, 4:5]))
                        chain.link(nc.scalar.activation(stat[:, k, 5:6], stat[:, k, 4:5], ACT.Ln, scale=1.0 / D, bias=eps[:, 0:1]))
                        nc.scalar.activation(stat[:, k, 6:7], stat[:, k, 5:6], ACT.Exp, scale=-0.5).then_inc(r4_ready, 1)
                    assert chain.n == 14, chain.n

            @block.tensor
            def _(pe):
                pe.sem_inc(t_done, 1)
                pe.wait_ge(c_loaded, 80)
                pe.wait_ge(w_loaded, 16 * (KD + KP))
                pe.wait_ge(w_scaled, KD)
                with pe.Fori(0, NT // 2) as i:
                    for k in range(2):
                        n = 2 * i + k
                        pe.wait_ge(u_ready, n + 1)
                        pe.wait_ge(loaded[k], 32 * i + 32)
                        for kd in range(KP):
                            nc.tensor.transpose(psP[:, kd], pt[:, k, kd * P:(kd + 1) * P], ident[:])
                        for kd in range(KD):
                            t = nc.tensor.transpose(psT[:, kd], u[:, kd * P:(kd + 1) * P], ident[:])
                        t.then_inc(t_done, 1)
                        pe.wait_ge(uT_a, n + 1)
                        pe.wait_ge(uT_v, n + 1)
                        pe.wait_ge(x4_ready, n + 1)
                        for half in range(2):
                            for kd in range(KD):
                                mm = nc.tensor.matmul(psG[:, half * 512:(half + 1) * 512], uT[:, kd], wg[:, kd, half * 512:(half + 1) * 512],
                                                      start=(kd == 0), stop=(kd == KD - 1))
                        mm.then_inc(g_done, 1)
                        for half in range(2):
                            for kd in range(KP):
                                mm = nc.tensor.matmul(psE[:, half * 512:(half + 1) * 512], pT[:, kd], wp[:, kd, half * 512:(half + 1) * 512],
                                                      start=(kd == 0), stop=(kd == KP - 1))
                        mm.then_inc(e_done, 1)

            @block.vector
            def _(dve):
                chain = Chain(dve, dve_step)
                nc.vector.memset(eps[:], EPS).then_inc(eps_set, 1)
                dve.sem_inc(in_free, 2)
                dve.sem_inc(x4_ready, 1)
                for k in range(2):
                    dve.sem_inc(stored[k], 16)
                dve.wait_ge(c_loaded, 80)
                dve.wait_ge(w_loaded, 16 * (KD + KP))
                for kd in range(KD):
                    nc.vector.tensor_scalar(wg[:, kd], wg[:, kd], gain[:, kd:kd + 1], None, ALU.mult).then_inc(w_scaled, 1)

                def experts(k, m):
                    dve.wait_ge(loaded[k], 32 * m)
                    dve.wait_ge(y_loaded[k], 32 * m)
                    chain.link(nc.vector.scalar_tensor_tensor(x3[:, k], y[:, k, 0], wc[:, k, 0:1], x[:, k], ALU.mult, ALU.add))
                    nc.vector.scalar_tensor_tensor(x3[:, k], y[:, k, 1], wc[:, k, 1:2], x3[:, k], ALU.mult, ALU.add).then_inc(x3_ready, 1)

                def rest(n, k, m):
                    dve.wait_ge(t_done, n + 2)
                    nc.vector.tensor_copy(pT[:], psP[:])
                    nc.vector.tensor_copy(uT[:, 0:KD // 2], psT[:, 0:KD // 2]).then_inc(uT_v, 1)
                    dve.sem_inc(in_free, 1)
                    dve.wait_ge(l_ready, n + 1)
                    nc.vector.scalar_tensor_tensor(sg[:], psG[:], 0.0, sg[:], ALU.min, ALU.subtract).then_inc(m_ready, 1)
                    dve.wait_ge(e_done, n + 1)
                    dve.wait_ge(s_ready, n + 1)
                    chain.link(nc.vector.tensor_tensor(x4[:], psE[:], sg[:], ALU.mult))
                    nc.vector.tensor_tensor(x4[:], x4[:], x3[:, k], ALU.add).then_inc(x4_ready, 1)
                    dve.wait_ge(r4_ready, n + 1)
                    dve.wait_ge(stored[k], 16 * m)
                    nc.vector.scalar_tensor_tensor(o[:, k], x4[:], stat[:, k, 6:7], fg[:], ALU.mult, ALU.mult).then_inc(o_ready, 1)

                experts(0, 1)
                with dve.Fori(0, NT // 2 - 1) as i:
                    chain.at(4 * i + 1)
                    experts(1, i + 1)
                    rest(2 * i, 0, i + 1)
                    experts(0, i + 2)
                    rest(2 * i + 1, 1, i + 1)
                chain.at(4 * (NT // 2 - 1) + 1)
                experts(1, NT // 2)
                rest(NT - 2, 0, NT // 2)
                rest(NT - 1, 1, NT // 2)


def constants():
    c = {"ident": np.eye(P, dtype=np.float32)}
    rows = S // 64
    j = np.arange(S)
    freqs = (1.0 / (np.float32(10000.0) ** (np.arange(16, dtype=np.float32) * 2.0 / 32))).astype(np.float32)
    ang = np.concatenate([(j // 64 - rows // 2).astype(np.float32)[:, None] * freqs,
                          (j % 64 - 32).astype(np.float32)[:, None] * freqs], axis=-1)
    c["rope"] = np.stack([np.cos(ang), np.sin(ang)], axis=1).astype(np.float32)
    c["rope_meta"] = np.stack([np.ones((META, 32)), np.zeros((META, 32))], axis=1).astype(np.float32)
    l, k = np.arange(LF + 1)[:, None], np.arange(1, LF + 1)[None, :]
    turn = 2 * np.pi * ((l * k) % L) / L
    weight = np.where(l == LF, 0.5, 1.0) / np.sqrt(L * HD)
    c["dft_cos"] = (np.cos(turn) * weight).astype(np.float32)
    c["dft_sin"] = (np.sin(turn) * weight).astype(np.float32)
    turn = 2 * np.pi * np.outer(np.arange(HD), np.arange(HD)) / HD
    c["cdsd"] = np.stack([np.kron(np.eye(2), np.cos(turn)), np.kron(np.eye(2), np.sin(turn))], axis=1).astype(np.float32)
    p = np.arange(P)[:, None]
    c["fourier_back_in"] = np.minimum(L - 1, np.maximum(0, L - (P * np.arange(LF // P + 1)[None, :] + p))).astype(np.int32)
    c["fourier_back_out"] = np.maximum(0, L - META - (1 + p + np.array([[q * KC + s * P for q in range(NC) for s in range(3)]]))).astype(np.int32)
    c["mask_st"] = (np.arange(P)[:, None] <= np.arange(P)[None, :]).astype(np.float32)
    c["tri"] = (np.arange(P)[:, None] < np.arange(P)[None, :]).astype(np.float32)
    c["ones"] = np.ones((P, P), np.float32)
    e = np.arange(NE)
    c["iota_e"] = np.broadcast_to(np.stack([e, e // (NE // GRP)]).astype(np.float32), (P, 2, NE))
    c["iota_b"] = np.broadcast_to(np.arange(NBLK, dtype=np.float32), (P, NBLK))
    c["iota_p"] = np.arange(P, dtype=np.float32)[:, None]
    c["tokens"] = (P * np.arange(NT)[None, :] + np.arange(P)[:, None]).astype(np.int32)
    c["rope2_inv"] = (1.0 / (np.float32(10000.0) ** (np.arange(0, RD, 2, dtype=np.float32) / np.float32(RD)))).astype(np.float32)[None]
    return c


def scratch(nc, d):
    for name, shape in (("fin", (L, FW)), ("four", (S, FW)), ("negm1", (NQ, S)), ("attn", (S, FW)), ("x1", (S, D)), ("cs2", (S, 32)), ("xm", (S + CONV - 1, ML)), ("lat", (S, QL + KVL + RD)),
                        ("qT2", (MH * QD, S)), ("kT2", (MH * QD, S)), ("v2", (S, MH * VD)), ("negm2", (MH, S)), ("attn2", (S, MH * VD)),
                        ("G", (MLH, S)), ("gcols", (S, NG * MLH)), ("mlo", (S, ML)), ("x2", (S, D)), ("hf", (S, D)),
                        ("y", (NBLK * P, D)), ("wts", (P, 2 * NT)),
                        ("z", (S, ML)), ("gi", (S, 2 * MLH)), ("v", (L, NKV * HD)), ("hT", (NH * HD, L)), ("gates", (S, 2 * FW))):
        d[name] = nc.dram_tensor(name, shape, F32, kind="Internal").ap()
    for name, shape in (("rowtok", (P, NBLK)), ("widx", (P, NBLK)), ("dest", (P, 2 * NT))):
        d[name] = nc.dram_tensor(name, shape, I32, kind="Internal").ap()


def build(nc, d, out):
    scratch(nc, d)
    d["final_g_row"] = d["final_g"].rearrange("(a n) -> a n", a=1)
    stage_project1(nc, d)
    stage_fourier(nc, d)
    stage_max(nc, d, "M1", ("hT", "hT"), NQ, lambda h: NQ * HD + (h // (NQ // NKV)) * HD, HD, L, False, "negm1")
    stage_attention1(nc, d)
    d["x_rows"] = d["x"].rearrange("a s m -> (a s) m")
    stage_output(nc, d, "O1", "four", "attn", "gates", "w_out", "x_rows", "final_g_row", None, "x1")
    stage_rope2(nc, d)
    stage_project2(nc, d)
    stage_mla_heads(nc, d)
    stage_max(nc, d, "M2", ("qT2", "kT2"), MH, lambda h: h * QD, QD, S, True, "negm2")
    stage_attention2(nc, d)
    stage_gates(nc, d)
    stage_mlstm(nc, d)
    stage_output(nc, d, "O2", "attn2", "mlo", None, "w_o_2", "x1", "norm_ffn_g_2", "x2", "hf")
    stage_route(nc, d)
    stage_experts(nc, d)
    d["final_g2_row"] = d["final_norm_g_2"].rearrange("(a n) -> a n", a=1)
    d["p_rows"] = d["p_2"].rearrange("a b s n -> (a b s) n")
    stage_final(nc, d, out)


def kernel(**inputs):
    import numpy as _np
    import concourse.bacc as _bacc
    from concourse import mybir as _mybir
    from concourse.bass_utils import run_bass_kernel_spmd as _run

    nc = _bacc.Bacc("TRN2", target_bir_lowering=False, num_devices=1)
    arrays, d = {}, {}
    for name, a in list(inputs.items()) + list(constants().items()):
        a = _np.ascontiguousarray(a)
        arrays[f"in_{name}"] = a
        d[name] = nc.dram_tensor(f"in_{name}", a.shape, _mybir.dt.from_np(a.dtype), kind="ExternalInput").ap()
    out = nc.dram_tensor("out_0", (1, S, D), F32, kind="ExternalOutput").ap()
    build(nc, d, out)
    return _run(nc, [arrays], core_ids=[0]).results[0]["out_0"]
```

```python
from contextlib import ExitStack

import numpy as np

import concourse.bass as bass
from concourse import mybir

F32 = mybir.dt.float32
BF16 = mybir.dt.bfloat16
F32R = mybir.dt.float32r
I32 = mybir.dt.int32
U32 = mybir.dt.uint32
ALU = mybir.AluOpType
ACT = mybir.ActivationFunctionType
AX_X = mybir.AxisListType.X

P = 128
D = 1024
KD = D // P
S = 2048
NT = S // P
META = 16
L = S + META
EPS = 1e-6
HD = 64
NQ, NKV = 8, 2
NH = NQ + NKV
FW = 512
W1 = 2 * FW + NQ * HD + 2 * NKV * HD + NQ * HD
LF = L // 2
KC = 344
NC = LF // KC

QL, KVL, RD, ND, VD = 256, 128, 32, 64, 64
MH = 8
QD = ND + RD
MLH, MLD = 4, 128
ML = MLH * MLD
CONV = 4
GRP, NE, DE = 4, 32, 256
NBLK = 2 * S // P + NE
PD = 256
W2 = QL + KVL + RD + 2 * ML + 2 * MLH


class Chain:

    def __init__(self, eng, sem, base=0):
        self.eng, self.sem, self.base, self.n = eng, sem, base, 0

    def link(self, ins):
        self.n += 1
        ins.then_inc(self.sem, 1)
        self.eng.wait_ge(self.sem, self.base + self.n)

    def at(self, base):
        self.base, self.n = base, 0


class Stage:

    def __init__(self, nc, name, stack):
        self.nc, self.name, self.stack, self.sems = nc, name, stack, []
        stack.callback(self.give_back)

    def give_back(self):
        self.nc.clear_and_free_semaphores(self.sems)
        self.nc.all_engine_barrier()

    def sb(self, name, shape, dt=F32):
        return self.stack.enter_context(self.nc.sbuf_tensor(f"{self.name}_{name}", shape, dt))

    def ps(self, name, shape, dt=F32):
        return self.stack.enter_context(self.nc.psum_tensor(f"{self.name}_{name}", shape, dt))

    def sem(self, name):
        self.sems.append(self.nc.alloc_semaphore(f"{self.name}_{name}"))
        return self.sems[-1]


def rows_of(n):
    return bass.ds(n * P, P)


def ahead(eng, *values):
    return [v if isinstance(v, int) else eng.snap(eng.to_reg(v)) for v in values]


def to_all(row, *repeats):
    width = row.shape[-1]
    return bass.AP(tensor=row.tensor, offset=row.offset, ap=[[0, P], *[[0, r] for r in repeats], [1, width]])


def stage_project1(nc, d):
    with ExitStack() as stack:
        st = Stage(nc, "A", stack)
        w = st.sb("w", [P, KD, W1])
        gain = st.sb("gain", [P, KD])
        ident = st.sb("ident", [P, P])
        eps = st.sb("eps", [P, 1])
        hgain = st.sb("hgain", [P, NH, HD])
        cs = st.sb("cs", [P, 2, 2, HD // 2])
        x = st.sb("x", [P, 2, D])
        sq = st.sb("sq", [P, D])
        stat = st.sb("stat", [P, 2, 4])
        u = st.sb("u", [P, 2, D])
        uT = st.sb("uT", [P, 2, KD, P])
        hsq = st.sb("hsq", [P, NH, HD])
        hstat = st.sb("hstat", [P, 3, NH])
        hn = st.sb("hn", [P, NH, HD])
        rt = st.sb("rt", [P, 4, NH, HD // 2])
        hr = st.sb("hr", [P, NH, HD])
        hT = st.sb("hT", [P, 2, NH // 2, P])
        fin = st.sb("fin", [P, 2, FW])
        v = st.sb("v", [P, 2, NKV * HD])
        ge = st.sb("ge", [P, 2, FW])
        gs = st.sb("gs", [P, 2, 2 * FW])
        psT = st.ps("psT", [P, KD, P])
        psG = [st.ps(f"psG{g}", [P, 512]) for g in range(5)]
        psH = st.ps("psH", [P, 4, P])
        FIN, FG, Q, KV, AG = range(5)
        cols = {FIN: (0, FW), FG: (FW, FW), Q: (2 * FW, FW), KV: (3 * FW, 256), AG: (3 * FW + 256, FW)}
        order = (Q, KV, FIN, FG, AG)

        w_loaded = [st.sem(f"w_loaded{g}") for g in range(5)]
        c_loaded = st.sem("c_loaded")
        w_scaled = st.sem("w_scaled")
        eps_set = st.sem("eps_set")
        x_loaded = [st.sem(f"x_loaded{k}") for k in range(2)]
        cs_loaded = [st.sem(f"cs_loaded{k}") for k in range(2)]
        cs_free = st.sem("cs_free")
        x_free = st.sem("x_free")
        act_step = st.sem("act_step")
        r_ready = st.sem("r_ready")
        u_ready = st.sem("u_ready")
        t_done = st.sem("t_done")
        uT_a = st.sem("uT_a")
        uT_v = st.sem("uT_v")
        g_done = [st.sem(f"g_done{g}") for g in range(5)]
        g_free = [st.sem(f"g_free{g}") for g in range(5)]
        hsq_ready = st.sem("hsq_ready")
        hss_ready = st.sem("hss_ready")
        hr_stat = st.sem("hr_stat")
        ge_ready = st.sem("ge_ready")
        ge_used = st.sem("ge_used")
        rot_ready = st.sem("rot_ready")
        hT_done = st.sem("hT_done")
        hT_ready = st.sem("hT_ready")
        fv_ready = st.sem("fv_ready")
        gs_ready = st.sem("gs_ready")
        dve_step = st.sem("dve_step")
        f_stored = [st.sem(f"f_stored{k}") for k in range(2)]
        h_stored = [st.sem(f"h_stored{k}") for k in range(2)]
        u_free = st.sem("u_free")
        g_stored = [st.sem(f"g_stored{k}") for k in range(2)]

        w_dram = d["w_in"].rearrange("a (k p) n -> p (a k) n", p=P)
        x_dram = d["x"].rearrange("a s m -> (a s) m")

        with nc.Block() as block:

            @block.sync
            def _(sp):
                sp.dma_start(ident[:], d["ident"]).then_inc(c_loaded, 16)
                sp.dma_start(gain[:], d["norm_g"].rearrange("a (k p) -> p (a k)", p=P), allow_slow_non_contiguous=True).then_inc(c_loaded, 16)
                sp.dma_start(hgain[:, 0:NQ, :], to_all(d["q_norm_g"], NQ)).then_inc(c_loaded, 16)
                sp.dma_start(hgain[:, NQ:NH, :], to_all(d["k_norm_g"], NKV)).then_inc(c_loaded, 16)

                def load(n, k):
                    sp.wait_ge(x_free, n + 1)
                    if isinstance(n, int) and n == NT:
                        sp.dma_start(x[0:META, k], d["meta_tokens"]).then_inc(x_loaded[k], 16)
                    else:
                        sp.dma_start(x[:, k], x_dram[rows_of(n)]).then_inc(x_loaded[k], 16)
                    sp.wait_ge(cs_free, n + 1)
                    if isinstance(n, int) and n == NT:
                        sp.dma_start(cs[0:META, k], d["rope_meta"]).then_inc(cs_loaded[k], 16)
                    else:
                        sp.dma_start(cs[:, k], d["rope"][rows_of(n)]).then_inc(cs_loaded[k], 16)

                def store(n, k, meta=False):
                    rows = META if meta else P
                    hT_count, = ahead(sp, n + 2)
                    sp.wait_ge(fv_ready, n + 1)
                    at = slice(0, META) if meta else bass.ds(n * P + META, P)
                    sp.dma_start(d["fin"][at], fin[0:rows, k]).then_inc(f_stored[k], 16)
                    at = slice(S, L) if meta else rows_of(n)
                    sp.dma_start(d["v"][at], v[0:rows, k]).then_inc(f_stored[k], 16)
                    if not meta:
                        sp.wait_ge(gs_ready, 2 * n + 2)
                    sp.wait_ge(hT_ready, hT_count)
                    if not meta:
                        sp.dma_start(d["gates"][rows_of(n)], gs[:, k]).then_inc(g_stored[k], 16)
                    sp.dma_start(d["hT"][:, at].rearrange("(j p) s -> p j s", p=P),
                                 hT[:, k, :, 0:rows]).then_inc(h_stored[k], 16)

                for n in range(2):
                    load(n, n)
                for g in order:
                    c0, width = cols[g]
                    sp.dma_start(w[:, :, c0:c0 + width], w_dram[:, :, c0:c0 + width]).then_inc(w_loaded[g], 16)
                with sp.Fori(0, NT // 2 - 1) as i:
                    for k in range(2):
                        load(2 * i + k + 2, k)
                        store(2 * i + k, k)
                load(NT, 0)
                store(NT - 2, 0)
                store(NT - 1, 1)
                store(NT, 0, meta=True)
                for k in range(2):
                    sp.wait_ge(f_stored[k], 32 * (NT // 2 + 2 - k))
                    sp.wait_ge(h_stored[k], 16 * (NT // 2 + 2 - k))
                    sp.wait_ge(g_stored[k], 16 * (NT // 2 + 1))

            @block.scalar
            def _(act):
                nc.scalar.preload_act_table_set("natural_log_exp_and_others")
                chain = Chain(act, act_step)
                for k in range(2):
                    act.sem_inc(f_stored[k], 32)
                act.wait_ge(eps_set, 1)

                def stats(n, k, m):
                    act.wait_ge(x_loaded[k], 16 * m)
                    chain.link(nc.scalar.activation(sq[:], x[:, k], ACT.Square, accum_out=stat[:, k, 0:1]))
                    chain.link(nc.scalar.activation(stat[:, k, 1:2], stat[:, k, 0:1], ACT.Ln, scale=1.0 / D, bias=eps[:, 0:1]))
                    nc.scalar.activation(stat[:, k, 2:3], stat[:, k, 1:2], ACT.Exp, scale=-0.5).then_inc(r_ready, 1)

                def turned(n, k):
                    act.wait_ge(t_done, n + 1)
                    nc.scalar.copy(uT[:, k, KD // 2:KD], psT[:, KD // 2:KD]).then_inc(uT_a, 1)

                def tile(n, k, m, m_next, meta):
                    if not meta:
                        stats(n + 1, 1 - k, m_next)
                    act.wait_ge(g_done[KV], n + 1)
                    if not meta:
                        nc.scalar.activation(hsq[:, 0:NQ].rearrange("p h c -> p (h c)"), psG[Q][:, 0:NQ * HD], ACT.Square)
                    nc.scalar.activation(hsq[:, NQ:NH].rearrange("p h c -> p (h c)"), psG[KV][:, 0:NKV * HD],
                                         ACT.Square).then_inc(hsq_ready, 1)
                    act.wait_ge(f_stored[k], 32 * m)
                    nc.scalar.copy(v[:, k], psG[KV][:, NKV * HD:2 * NKV * HD])
                    act.wait_ge(hss_ready, n + 1)
                    chain.link(nc.scalar.activation(hstat[:, 1], hstat[:, 0], ACT.Ln, scale=1.0 / HD, bias=eps[:, 0:1]))
                    nc.scalar.activation(hstat[:, 2], hstat[:, 1], ACT.Exp, scale=-0.5).then_inc(hr_stat, 1)
                    act.wait_ge(g_done[FIN], n + 1)
                    nc.scalar.copy(fin[:, k], psG[FIN][:]).then_inc(fv_ready, 1)
                    if not meta:
                        turned(n + 1, 1 - k)
                        act.wait_ge(g_done[FG], n + 1)
                        act.wait_ge(ge_used, n + 1)
                        nc.scalar.activation(ge[:, 0], psG[FG][:], ACT.Exp, scale=-1.0).then_inc(ge_ready, 1)
                        act.wait_ge(g_done[AG], n + 1)
                        nc.scalar.activation(ge[:, 1], psG[AG][:], ACT.Exp, scale=-1.0).then_inc(ge_ready, 1)

                stats(0, 0, 1)
                turned(0, 0)
                with act.Fori(0, NT // 2) as i:
                    for k in range(2):
                        if k == 0:
                            chain.at(i * 6 + 2)
                        tile(2 * i + k, k, i + 1, i + 1 + k, False)
                chain.at(3 * NT + 2)
                tile(NT, 0, NT // 2 + 1, 0, True)

            @block.gpsimd
            def _(pool):
                pool.sem_inc(x_free, 2)

                def tile(n, k):
                    pool.wait_ge(r_ready, n + 1)
                    pool.wait_ge(u_free, n + 1)
                    nc.gpsimd.tensor_tensor(u[:, k], x[:, k], stat[:, k, 2:3].to_broadcast([P, D]), ALU.mult).then_inc(u_ready, 1)
                    pool.wait_ge(u_ready, n + 1)
                    pool.sem_inc(x_free, 1)

                with pool.Fori(0, NT // 2) as i:
                    for k in range(2):
                        tile(2 * i + k, k)
                tile(NT, 0)

            @block.tensor
            def _(pe):
                pe.wait_ge(c_loaded, 64)
                pe.sem_inc(u_free, 2)

                def turn(n, k):
                    pe.wait_ge(u_ready, n + 1)
                    for kd in range(KD):
                        t = nc.tensor.transpose(psT[:, kd], u[:, k, kd * P:(kd + 1) * P], ident[:])
                    t.then_inc(t_done, 1)
                    pe.wait_ge(t_done, n + 1)
                    pe.sem_inc(u_free, 1)

                def tile(n, k, meta=False, first=False):
                    pe.wait_ge(uT_a, n + 1)
                    pe.wait_ge(uT_v, n + 1)
                    for g in (KV, FIN) if meta else order:
                        c0, width = cols[g]
                        if first:
                            pe.wait_ge(w_scaled, KD * (order.index(g) + 1))
                        pe.wait_ge(g_free[g], n + 1)
                        for kd in range(KD):
                            m = nc.tensor.matmul(psG[g][:, 0:width], uT[:, k, kd], w[:, kd, c0:c0 + width],
                                                 start=(kd == 0), stop=(kd == KD - 1))
                        m.then_inc(g_done[g], 1)
                        if g == FIN and not meta:
                            turn(n + 1, 1 - k)
                    pe.wait_ge(hT_ready, n + 1)
                    pe.wait_ge(rot_ready, n + 1)
                    for j in range(NH // 2):
                        t = nc.tensor.transpose(psH[:, j] if j < 4 else psG[KV][:, 256:256 + P], hr[:, 2 * j:2 * j + 2].rearrange("p h c -> p (h c)"), ident[:])
                    t.then_inc(hT_done, 1)

                turn(0, 0)
                tile(0, 0, first=True)
                with pe.Fori(0, NT // 2 - 1) as i:
                    tile(2 * i + 1, 1)
                    tile(2 * i + 2, 0)
                tile(NT - 1, 1)
                tile(NT, 0, meta=True)

            @block.vector
            def _(dve):
                chain = Chain(dve, dve_step)
                for k in range(2):
                    dve.sem_inc(h_stored[k], 16)
                    dve.sem_inc(g_stored[k], 16)
                nc.vector.memset(eps[:], EPS).then_inc(eps_set, 1)
                nc.vector.memset(hsq[:], 0.0)
                dve.sem_inc(cs_free, 2)
                dve.sem_inc(hT_ready, 1)
                dve.sem_inc(ge_used, 1)
                for g in range(5):
                    dve.sem_inc(g_free[g], 1)
                dve.wait_ge(c_loaded, 64)
                nc.vector.tensor_scalar(hgain[:, 0:NQ], hgain[:, 0:NQ], HD ** -0.5, None, ALU.mult)
                def scale_weights(g):
                    c0, width = cols[g]
                    dve.wait_ge(w_loaded[g], 16)
                    for kd in range(KD):
                        nc.vector.tensor_scalar(w[:, kd, c0:c0 + width], w[:, kd, c0:c0 + width], gain[:, kd:kd + 1], None,
                                                ALU.mult).then_inc(w_scaled, 1)

                def turned(n, k):
                    dve.wait_ge(t_done, n + 1)
                    nc.vector.tensor_copy(uT[:, k, 0:KD // 2], psT[:, 0:KD // 2]).then_inc(uT_v, 1)

                def tile(n, k, m, meta):
                    dve.wait_ge(hsq_ready, n + 1)
                    nc.vector.reduce_sum(hstat[:, 0], hsq[:], AX_X).then_inc(hss_ready, 1)
                    dve.wait_ge(hr_stat, n + 1)
                    if not meta:
                        nc.vector.tensor_tensor(hn[:, 0:NQ], psG[Q][:].rearrange("p (h c) -> p h c", c=HD),
                                                hstat[:, 2, 0:NQ].unsqueeze(2).to_broadcast([P, NQ, HD]),
                                                ALU.mult).then_inc(g_free[Q], 1)
                    chain.link(nc.vector.tensor_tensor(hn[:, NQ:NH], psG[KV][:, 0:NKV * HD].rearrange("p (h c) -> p h c", c=HD),
                                                       hstat[:, 2, NQ:NH].unsqueeze(2).to_broadcast([P, NKV, HD]), ALU.mult))
                    chain.link(nc.vector.tensor_tensor(hn[:], hn[:], hgain[:], ALU.mult))
                    dve.wait_ge(fv_ready, n + 1)
                    dve.sem_inc(g_free[FIN], 1)
                    dve.wait_ge(cs_loaded[k], 16 * m)
                    pairs = hn[:].rearrange("p h (c two) -> p h c two", two=2)
                    outs = hr[:].rearrange("p h (c two) -> p h c two", two=2)
                    cos = cs[:, k, 0].unsqueeze(1).to_broadcast([P, NH, HD // 2])
                    sin = cs[:, k, 1].unsqueeze(1).to_broadcast([P, NH, HD // 2])
                    nc.vector.tensor_tensor(rt[:, 0], pairs[:, :, :, 0], cos, ALU.mult)
                    nc.vector.tensor_tensor(rt[:, 1], pairs[:, :, :, 1], sin, ALU.mult)
                    nc.vector.tensor_tensor(rt[:, 2], pairs[:, :, :, 0], sin, ALU.mult)
                    chain.link(nc.vector.tensor_tensor(rt[:, 3], pairs[:, :, :, 1], cos, ALU.mult))
                    dve.sem_inc(cs_free, 1)
                    if not (isinstance(n, int) and n == 0):
                        dve.wait_ge(hT_done, n)
                    nc.vector.tensor_tensor(outs[:, :, :, 0], rt[:, 0], rt[:, 1], ALU.subtract)
                    nc.vector.tensor_tensor(outs[:, :, :, 1], rt[:, 2], rt[:, 3], ALU.add).then_inc(rot_ready, 1)
                    if not meta:
                        turned(n + 1, 1 - k)
                        dve.wait_ge(g_stored[k], 16 * m)
                        for j, g in enumerate((FG, AG)):
                            dve.wait_ge(ge_ready, 2 * n + j + 1)
                            chain.link(nc.vector.tensor_scalar(ge[:, j], ge[:, j], 1.0, None, ALU.add))
                            chain.link(nc.vector.reciprocal(ge[:, j], ge[:, j]))
                            nc.vector.tensor_tensor(gs[:, k, j * FW:(j + 1) * FW], psG[g][:], ge[:, j],
                                                    ALU.mult).then_inc(gs_ready, 1)
                        dve.wait_ge(gs_ready, 2 * n + 2)
                        dve.sem_inc(ge_used, 1)
                        dve.sem_inc(g_free[FG], 1)
                        dve.sem_inc(g_free[AG], 1)
                    dve.wait_ge(hT_done, n + 1)
                    dve.wait_ge(h_stored[k], 16 * m)
                    nc.vector.tensor_copy(hT[:, k, 4], psG[KV][:, 256:256 + P]).then_inc(g_free[KV], 1)
                    nc.vector.tensor_copy(hT[:, k, 0:4], psH[:]).then_inc(hT_ready, 1)

                turned(0, 0)
                for g in order:
                    scale_weights(g)
                LINKS = 7
                with dve.Fori(0, NT // 2) as i:
                    for k in range(2):
                        if k == 0:
                            chain.at(i * (2 * LINKS))
                        tile(2 * i + k, k, i + 1, False)
                    assert chain.n == 2 * LINKS
                chain.at(LINKS * NT)
                tile(NT, 0, NT // 2 + 1, True)


def stage_fourier(nc, d):
    JT = LF // P + 1
    LAST = LF + 1 - (JT - 1) * P
    GP = FW // P
    SUB = [(0, P), (P, P), (2 * P, KC - 2 * P)]
    with ExitStack() as stack:
        st = Stage(nc, "B", stack)
        f = st.sb("f", [P, JT, FW])
        fr = st.sb("fr", [P, JT, FW])
        e = st.sb("e", [P, JT, FW])
        o = st.sb("o", [P, JT, FW])
        tab = st.sb("tab", [P, 2, JT, LF])
        back_in = st.sb("back_in", [P, JT], I32)
        back_out = st.sb("back_out", [P, NC * len(SUB)], I32)
        cdsd = st.sb("cdsd", [P, 2, P])
        wf = st.sb("wf", [P, GP, P])
        mix = st.sb("mix", [P, 2, GP, P])
        bias = st.sb("bias", [1, FW])
        ones = st.sb("ones", [1, P])
        g = st.sb("g", [P, 2, GP, KC])
        osb = st.sb("osb", [P, 2, FW])
        lo = st.sb("lo", [P, 2, FW])
        hi = st.sb("hi", [P, 2, FW])
        psG = [[st.ps(f"psG{t}{c}", [P, 512]) for c in range(GP)] for t in range(2)]

        set_done = st.sem("set_done")
        f_loaded = st.sem("f_loaded")
        r_loaded = st.sem("r_loaded")
        i_loaded = st.sem("i_loaded")
        scattered = [st.sem(f"scattered{k}") for k in range(2)]
        c_loaded = st.sem("c_loaded")
        t_loaded = [st.sem(f"t_loaded{t}") for t in range(2)]
        folded = st.sem("folded")
        mix_done = st.sem("mix_done")
        mix_ready = st.sem("mix_ready")
        g_done = st.sem("g_done")
        g_ready = st.sem("g_ready")
        s_done = st.sem("s_done")
        o_ready = st.sem("o_ready")
        out_ready = st.sem("out_ready")
        stored = [st.sem(f"stored{k}") for k in range(2)]

        with nc.Block() as block:

            @block.sync
            def _(sp):
                sp.wait_ge(set_done, 1)
                for j in range(JT):
                    n = P if j < JT - 1 else LAST
                    sp.dma_start(f[0:n, j], d["fin"][j * P:j * P + n]).then_inc(f_loaded, 16)
                sp.dma_start(cdsd[:], d["cdsd"]).then_inc(c_loaded, 16)
                for c in range(GP):
                    for h in range(2):
                        sp.dma_start(wf[h * HD:(h + 1) * HD, c, h * HD:(h + 1) * HD],
                                     d["w_fmix"][0, 2 * c + h]).then_inc(c_loaded, 16)
                sp.dma_start(bias[:], d["b_fmix"].rearrange("a g c -> a (g c)")).then_inc(c_loaded, 16)
                for n in range(NC * len(SUB)):
                    c, (s0, w) = n // len(SUB), SUB[n % len(SUB)]
                    k0 = 1 + c * KC + s0
                    sp.wait_ge(out_ready, 2 * n + 2)
                    skip = max(0, META - k0)
                    sp.dma_start(d["four"][k0 + skip - META:k0 + w - META], lo[skip:w, n % 2]).then_inc(stored[n % 2], 16)
                sp.wait_ge(stored[0], 16 * 5)
                sp.wait_ge(stored[1], 16 * 4)

            @block.gpsimd
            def _(pool):
                pool.dma_start(back_in[:], d["fourier_back_in"]).then_inc(i_loaded, 16)
                pool.dma_start(back_out[:], d["fourier_back_out"]).then_inc(i_loaded, 16)
                pool.wait_ge(i_loaded, 32)
                for j in range(JT):
                    n = P if j < JT - 1 else LAST
                    pool.indirect_dma_start(fr[0:n, j], None, d["fin"],
                                            bass.IndirectOffsetOnAxis(back_in[0:n, j:j + 1], 0)).then_inc(r_loaded, 16)
                for t, table in enumerate(("dft_cos", "dft_sin")):
                    for j in range(JT):
                        n = P if j < JT - 1 else LAST
                        pool.dma_start(tab[0:n, t, j], d[table][j * P:j * P + n]).then_inc(t_loaded[t], 16)
                for n in range(NC * len(SUB)):
                    c, (s0, w) = n // len(SUB), SUB[n % len(SUB)]
                    m = w - (c * KC + s0 + w == LF)
                    pool.wait_ge(out_ready, 2 * n + 2)
                    pool.indirect_dma_start(d["four"], bass.IndirectOffsetOnAxis(back_out[0:m, n:n + 1], 0),
                                            hi[0:m, n % 2], None).then_inc(scattered[n % 2], 16)
                pool.wait_ge(scattered[0], 16 * 5)
                pool.wait_ge(scattered[1], 16 * 4)

            @block.vector
            def _(dve):
                nc.vector.memset(wf[:], 0.0)
                nc.vector.memset(ones[:], 1.0).then_inc(set_done, 1)
                dve.wait_ge(f_loaded, 16 * JT)
                dve.wait_ge(r_loaded, 16 * JT)
                nc.vector.memset(fr[0:1, 0], 0.0).then_inc(set_done, 1)
                dve.wait_ge(set_done, 2)
                for j in range(JT):
                    n = P if j < JT - 1 else LAST
                    nc.vector.tensor_tensor(e[0:n, j], f[0:n, j], fr[0:n, j], ALU.add)
                    nc.vector.tensor_tensor(o[0:n, j], f[0:n, j], fr[0:n, j], ALU.subtract).then_inc(folded, 1)
                dve.wait_ge(mix_done, 2)
                for t in range(2):
                    nc.vector.tensor_copy(mix[:, t], psG[t][0][:].rearrange("p (c n) -> p c n", n=P)).then_inc(mix_ready, 1)
                for c in range(NC):
                    dve.wait_ge(g_done, 2 * c + 2)
                    for t in range(2):
                        for h in range(2):
                            copy = nc.vector.tensor_copy(g[:, t, h], psG[t][h][:, 0:KC])
                    copy.then_inc(g_ready, 1)
                    for s, (s0, w) in enumerate(SUB):
                        n = c * len(SUB) + s
                        dve.wait_ge(o_ready, n + 1)
                        if n >= 2:
                            dve.wait_ge(stored[n % 2], 16 * (n // 2))
                            dve.wait_ge(scattered[n % 2], 16 * (n // 2))
                        ps = psG[n % 2][0]
                        nc.vector.tensor_tensor(lo[0:w, n % 2], ps[0:w], osb[0:w, n % 2], ALU.subtract).then_inc(out_ready, 1)
                        nc.vector.tensor_tensor(hi[0:w, n % 2], ps[0:w], osb[0:w, n % 2], ALU.add).then_inc(out_ready, 1)

            @block.scalar
            def _(act):
                for c in range(NC):
                    act.wait_ge(g_done, 2 * c + 2)
                    for t in range(2):
                        for h in range(2, GP):
                            copy = nc.scalar.copy(g[:, t, h], psG[t][h][:, 0:KC])
                    copy.then_inc(g_ready, 1)
                    for s, (s0, w) in enumerate(SUB):
                        n = c * len(SUB) + s
                        act.wait_ge(s_done, n + 1)
                        if n >= 2:
                            act.wait_ge(out_ready, 2 * n - 2)
                        nc.scalar.copy(osb[0:w, n % 2], psG[n % 2][1][0:w]).then_inc(o_ready, 1)

            @block.tensor
            def _(pe):
                pe.wait_ge(set_done, 1)
                pe.wait_ge(c_loaded, 16 * (2 + 2 * GP))
                for t in range(2):
                    for c in range(GP):
                        mm = nc.tensor.matmul(psG[t][0][:, c * P:(c + 1) * P], cdsd[:, t], wf[:, c], start=(c == 0),
                                              stop=True, skip_group_check=True)
                    mm.then_inc(mix_done, 1)
                pe.wait_ge(mix_ready, 2)
                for c in range(NC):
                    if c:
                        pe.wait_ge(out_ready, 2 * len(SUB) * c)
                    for t, src in enumerate((e, o)):
                        if c == 0:
                            pe.wait_ge(t_loaded[t], 16 * JT)
                        for j in range(JT):
                            n = P if j < JT - 1 else LAST
                            if c == 0 and t == 0:
                                pe.wait_ge(folded, j + 1)
                            for h in range(GP):
                                mm = nc.tensor.matmul(psG[t][h][:, 0:KC], src[0:n, j, h * P:(h + 1) * P],
                                                      tab[0:n, t, j, c * KC:(c + 1) * KC], start=(j == 0), stop=(j == JT - 1))
                        mm.then_inc(g_done, 1)
                    pe.wait_ge(g_ready, 2 * c + 2)
                    for s, (s0, w) in enumerate(SUB):
                        n = c * len(SUB) + s
                        if s >= 2:
                            pe.wait_ge(out_ready, 2 * n - 2)
                        nc.tensor.matmul(psG[n % 2][0][0:w], ones[:, 0:w], bias[:], start=True, stop=False, skip_group_check=True)
                        for t in range(2):
                            for h in range(GP):
                                mm = nc.tensor.matmul(psG[n % 2][t][0:w, h * P:(h + 1) * P], g[:, t, h, s0:s0 + w],
                                                      mix[:, t, h], start=(t == 1 and h == 0), stop=(h == GP - 1),
                                                      skip_group_check=True)
                        mm.then_inc(s_done, 1)


def stage_max(nc, d, name, src, heads, kv_of, width, keys, causal, out):
    with ExitStack() as stack:
        st = Stage(nc, name, stack)
        qf = st.sb("qf", [width, 2, S])
        kf = st.sb("kf", [width, 2, keys])
        qb = st.sb("qb", [width, 2, S], BF16)
        kb = st.sb("kb", [width, 2, keys], BF16)
        mx = st.sb("mx", [P, heads * NT, 2])
        neg = st.sb("neg", [P, heads * NT])
        negT = st.sb("negT", [heads * NT, P])
        ident = st.sb("ident", [P, P])
        half = keys // 2
        ps = [st.ps(f"ps{u}", [P, 1536]) for u in range(2)]
        psN = st.ps("psN", [P, P])
        loaded = [st.sem(f"loaded{k}") for k in range(2)]
        c_loaded = st.sem("c_loaded")
        cast = st.sem("cast")
        b_free = st.sem("b_free")
        s_done = st.sem("s_done")
        m_done = st.sem("m_done")
        n_step = st.sem("n_step")
        n_done = st.sem("n_done")
        n_ready = st.sem("n_ready")
        stored = st.sem("stored")
        filled = st.sem("filled")

        def units(t):
            if not causal:
                return [(0, half), (half, half)]
            end = (t + 1) * P
            return [(0, end)] if end <= 1024 else [(0, 1024), (1024, end - 1024)]

        total = sum(len(units(t)) for t in range(NT))

        with nc.Block() as block:

            @block.sync
            def _(sp):
                sp.dma_start(ident[:], d["ident"]).then_inc(c_loaded, 16)
                def load(h, k):
                    count, at_q, at_k = ahead(sp, h + 1, h * width, kv_of(h))
                    sp.wait_ge(cast, count)
                    sp.dma_start(qf[:, k], d[src[0]][bass.ds(at_q, width), 0:S]).then_inc(loaded[k], 16)
                    sp.dma_start(kf[:, k], d[src[1]][bass.ds(at_k, width), 0:keys]).then_inc(loaded[k], 16)
                with sp.Fori(0, heads // 2) as i:
                    for k in range(2):
                        load(2 * i + k, k)
                sp.wait_ge(n_ready, 1)
                sp.dma_start(d[out].rearrange("h (t p) -> (h t) p", p=P), negT[:]).then_inc(stored, 16)
                sp.wait_ge(stored, 16)

            @block.scalar
            def _(act):
                act.sem_inc(cast, 2)
                with act.Fori(0, heads // 2) as i:
                    for k in range(2):
                        act.wait_ge(loaded[k], 32 * i + 32)
                        act.wait_ge(b_free, 2 * i + k + 1)
                        nc.scalar.copy(qb[:, k], qf[:, k])
                        nc.scalar.copy(kb[:, k], kf[:, k]).then_inc(cast, 1)

            @block.tensor
            def _(pe):
                pe.sem_inc(b_free, 2)
                with pe.Fori(0, heads // 2) as i:
                    for k in range(2):
                        pe.wait_ge(cast, 2 * i + k + 3)
                        u = 0
                        for t in range(NT):
                            for k0, kw in units(t):
                                slot = (k * total + u) % 2
                                pe.wait_ge(m_done, (2 * i + k) * total + u + 1)
                                for c in range(0, kw, 512):
                                    w = min(512, kw - c)
                                    mm = nc.tensor.matmul(ps[slot][:, c:c + w], qb[:, k, t * P:(t + 1) * P],
                                                          kb[:, k, k0 + c:k0 + c + w], start=True, stop=True)
                                mm.then_inc(s_done, 1)
                                u += 1
                        pe.wait_ge(s_done, (2 * i + k) * total + total)
                        pe.sem_inc(b_free, 1)
                pe.wait_ge(c_loaded, 16)
                pe.wait_ge(n_step, 2)
                nc.tensor.transpose(psN[0:heads * NT, :], neg[:], ident[:]).then_inc(n_done, 1)

            @block.vector
            def _(dve):
                dve.sem_inc(m_done, 2)
                nc.vector.memset(mx[:], -1e30).then_inc(filled, 1)
                dve.wait_ge(filled, 1)
                with dve.Fori(0, heads // 2) as i:
                    for k in range(2):
                        u = 0
                        for t in range(NT):
                            for piece, (k0, kw) in enumerate(units(t)):
                                slot = (k * total + u) % 2
                                dve.wait_ge(s_done, (2 * i + k) * total + u + 1)
                                at = bass.ds((2 * i + k) * NT + t, 1)
                                if causal and k0 + kw == (t + 1) * P:
                                    nc.vector.reduce_max(mx[0:64, at, piece], ps[slot][0:64, 0:kw - 64], AX_X)
                                    nc.vector.reduce_max(mx[64:P, at, piece], ps[slot][64:P, 0:kw], AX_X).then_inc(m_done, 1)
                                else:
                                    nc.vector.reduce_max(mx[:, at, piece], ps[slot][:, 0:kw], AX_X).then_inc(m_done, 1)
                                u += 1
                dve.wait_ge(m_done, heads * total + 2)
                nc.vector.reduce_max(neg[:], mx[:], AX_X).then_inc(n_step, 1)
                dve.wait_ge(n_step, 1)
                nc.vector.tensor_scalar(neg[:], neg[:], -1.0, None, ALU.mult).then_inc(n_step, 1)
                dve.wait_ge(n_done, 1)
                nc.vector.tensor_copy(negT[:], psN[0:heads * NT, :]).then_inc(n_ready, 1)


def stage_attention1(nc, d):
    KT = NT + 1
    GQ = NQ // NKV
    J = NKV * KT
    LAG = 3
    with ExitStack() as stack:
        st = Stage(nc, "C", stack)
        ident = st.sb("ident", [P, P])
        kT = st.sb("kT", [HD + 1, NKV, L])
        kh = st.sb("kh", [HD + 1, NKV, L], F32R)
        kl = st.sb("kl", [HD + 1, NKV, L], F32R)
        v1 = st.sb("v1", [P, KT, NKV, HD + 1])
        vh = st.sb("vh", [P, KT, NKV, HD + 1], F32R)
        vl = st.sb("vl", [P, KT, NKV, HD + 1], F32R)
        qa = st.sb("qa", [HD + 1, 2, NQ, P])
        qh = st.sb("qh", [HD + 1, 2, NQ, P], F32R)
        ql = st.sb("ql", [HD + 1, 2, NQ, P], F32R)
        e = st.sb("e", [P, 4, 512])
        eh = st.sb("eh", [P, 4, 512], F32R)
        el = st.sb("el", [P, 4, 512], F32R)
        oT = st.sb("oT", [HD + 1, NKV, 512])
        rs = st.sb("rs", [P, GQ])
        ao = st.sb("ao", [P, 2, FW])
        psS = [st.ps(f"psS{s}", [P, 512]) for s in range(4)]
        psO = [st.ps(f"psO{g}", [P, 512]) for g in range(NKV)]
        psR = st.ps("psR", [P, GQ, HD + 1])
        set_done = st.sem("set_done")
        kv_loaded = st.sem("kv_loaded")
        q_loaded = [st.sem(f"q_loaded{k}") for k in range(2)]
        q_free = st.sem("q_free")
        s_done = st.sem("s_done")
        e_done = st.sem("e_done")
        pv_done = st.sem("pv_done")
        oT_ready = st.sem("oT_ready")
        t_done = st.sem("t_done")
        ao_ready = st.sem("ao_ready")
        kv_split = st.sem("kv_split")
        qh_ready = st.sem("qh_ready")
        ql_ready = st.sem("ql_ready")
        el_done = st.sem("el_done")
        r_ready = st.sem("r_ready")
        stored = [st.sem(f"stored{k}") for k in range(2)]

        with nc.Block() as block:

            @block.sync
            def _(sp):
                sp.dma_start(ident[:], d["ident"]).then_inc(kv_loaded, 16)
                for g in range(NKV):
                    sp.dma_start(kT[0:HD, g], d["hT"][(NQ + g) * HD:(NQ + g + 1) * HD]).then_inc(kv_loaded, 16)
                sp.wait_ge(set_done, 1)
                for g in range(NKV):
                    sp.dma_start(v1[:, 0:NT, g, 0:HD], d["v"][0:S, g * HD:(g + 1) * HD].rearrange("(t p) c -> p t c", p=P)).then_inc(kv_loaded, 16)
                    sp.dma_start(v1[0:META, NT, g, 0:HD], d["v"][S:L, g * HD:(g + 1) * HD]).then_inc(kv_loaded, 16)

                def store(n, k):
                    count, at = ahead(sp, 2 * n + 2, n * P)
                    sp.wait_ge(ao_ready, count)
                    sp.wait_ge(set_done, 1)
                    sp.dma_start(d["attn"][bass.ds(at, P)], ao[:, k]).then_inc(stored[k], 16)

                with sp.Fori(0, NT // 2) as i:
                    for k in range(2):
                        store(2 * i + k, k)
                for k in range(2):
                    sp.wait_ge(stored[k], 16 * (NT // 2 + 1))

            @block.gpsimd
            def _(pool):
                with pool.Fori(0, NT // 2) as i:
                    for k in range(2):
                        at = (2 * i + k) * P
                        pool.wait_ge(q_free, 2 * i + k + 1)
                        pool.dma_start(qa[0:HD, k], d["hT"][0:NQ * HD, bass.ds(at, P)].rearrange("(h c) s -> c h s", c=HD)).then_inc(q_loaded[k], 16)
                        pool.dma_start(qa[HD:HD + 1, k], d["negm1"][:, bass.ds(at, P)].unsqueeze(0)).then_inc(q_loaded[k], 16)

            @block.vector
            def _(dve):
                nc.vector.memset(v1[:], 1.0)
                nc.vector.memset(kT[HD:HD + 1], 1.0).then_inc(set_done, 1)
                for k in range(2):
                    dve.sem_inc(stored[k], 16)
                dve.wait_ge(kv_loaded, 112)
                dve.wait_ge(set_done, 1)
                nc.vector.tensor_copy(kh[:], kT[:]).then_inc(kv_split, 1)
                nc.vector.tensor_copy(vh[:], v1[:]).then_inc(kv_split, 1)
                dve.wait_ge(kv_split, 2)
                nc.vector.tensor_tensor(kl[:], kT[:], kh[:], ALU.subtract).then_inc(kv_split, 1)
                nc.vector.tensor_tensor(vl[:], v1[:], vh[:], ALU.subtract).then_inc(kv_split, 1)

                def split_q(n, k, m):
                    dve.wait_ge(q_loaded[k], 32 * m)
                    nc.vector.tensor_copy(qh[:, k], qa[:, k]).then_inc(qh_ready, 1)
                    dve.wait_ge(qh_ready, n + 1)
                    nc.vector.tensor_tensor(ql[:, k], qa[:, k], qh[:, k], ALU.subtract).then_inc(ql_ready, 1)

                def take(n, g):
                    dve.wait_ge(pv_done, n * J + (g + 1) * KT + 4)
                    nc.vector.tensor_copy(oT[:, g], psO[g][0:HD + 1]).then_inc(oT_ready, 1)

                def divide(n, k, g, m):
                    dve.wait_ge(t_done, 2 * n + g + 1)
                    nc.vector.reciprocal(rs[:], psR[:, :, HD]).then_inc(r_ready, 1)
                    dve.wait_ge(r_ready, 2 * n + g + 1)
                    if g == 0:
                        dve.wait_ge(stored[k], 16 * m)
                    nc.vector.tensor_tensor(
                        ao[:, k, g * GQ * HD:(g + 1) * GQ * HD].rearrange("p (h c) -> p h c", c=HD), psR[:, :, 0:HD],
                        rs[:].unsqueeze(2).to_broadcast([P, GQ, HD]), ALU.mult).then_inc(ao_ready, 1)

                def tile(n, k, m, first=False, last=False):
                    for j in range(J):
                        rows = P if j % KT < NT else META
                        slot = (k * J + j) % 4
                        dve.wait_ge(e_done, n * J + j + 1)
                        nc.vector.tensor_tensor(el[0:rows, slot], e[0:rows, slot], eh[0:rows, slot], ALU.subtract).then_inc(el_done, 1)
                        if j == 1 and not first:
                            take(n - 1, 1)
                        if j == LAG + 2 and not first:
                            divide(n - 1, 1 - k, 1, 0)
                        if j == KT + 1:
                            take(n, 0)
                        if j == KT + LAG + 2:
                            divide(n, k, 0, m)
                        if j == KT + 8 and not last:
                            split_q(n + 1, 1 - k, m + k)

                split_q(0, 0, 1)
                tile(0, 0, 1, first=True)
                with dve.Fori(0, NT // 2 - 1) as i:
                    tile(2 * i + 1, 1, i + 1)
                    tile(2 * i + 2, 0, i + 2)
                tile(NT - 1, 1, NT // 2, last=True)
                take(NT - 1, 1)
                divide(NT - 1, 1, 1, 0)

            @block.scalar
            def _(act):
                nc.scalar.preload_act_table_set("natural_log_exp_and_others")
                with act.Fori(0, NT // 2) as i:
                    for k in range(2):
                        for j in range(J):
                            rows = P if j % KT < NT else META
                            slot = (k * J + j) % 4
                            act.wait_ge(s_done, (2 * i + k) * J + j + 1)
                            act.wait_ge(pv_done, (2 * i + k) * J + j + 1)
                            nc.scalar.activation(e[0:rows, slot], psS[slot][0:rows], ACT.Exp)
                            nc.scalar.activation(eh[0:rows, slot], psS[slot][0:rows], ACT.Exp).then_inc(e_done, 1)

            @block.tensor
            def _(pe):
                pe.sem_inc(pv_done, 4)
                pe.sem_inc(q_free, 2)
                pe.wait_ge(kv_loaded, 112)
                pe.wait_ge(kv_split, 4)

                def scores(n, k, j):
                    g, kt = j // KT, j % KT
                    rows = P if kt < NT else META
                    slot = (k * J + j) % 4
                    keys = slice(kt * P, kt * P + rows)
                    if j == 0:
                        pe.wait_ge(ql_ready, n + 1)
                    high = qh[:, k, g * GQ:(g + 1) * GQ].rearrange("c h s -> c (h s)")
                    low = ql[:, k, g * GQ:(g + 1) * GQ].rearrange("c h s -> c (h s)")
                    nc.tensor.matmul(psS[slot][0:rows], kh[:, g, keys], high, start=True, stop=False)
                    nc.tensor.matmul(psS[slot][0:rows], kh[:, g, keys], low, start=False, stop=False)
                    nc.tensor.matmul(psS[slot][0:rows], kl[:, g, keys], high, start=False, stop=True).then_inc(s_done, 1)

                def turn(n, g):
                    pe.wait_ge(oT_ready, 2 * n + g + 1)
                    for h in range(GQ):
                        t = nc.tensor.transpose(psR[:, h], oT[:, g, h * P:(h + 1) * P], ident[0:HD + 1, 0:HD + 1])
                    t.then_inc(t_done, 1)

                def tile(n, k, first=False):
                    scores(n, k, 0)
                    scores(n, k, 1)
                    for j in range(J):
                        g, kt = j // KT, j % KT
                        rows = P if kt < NT else META
                        slot = (k * J + j) % 4
                        if j + 2 < J:
                            scores(n, k, j + 2)
                        if j == LAG and not first:
                            turn(n - 1, 1)
                        if j == KT + LAG:
                            turn(n, 0)
                        pe.wait_ge(e_done, n * J + j + 1)
                        nc.tensor.matmul(psO[g][0:HD + 1], vh[0:rows, kt, g], eh[0:rows, slot], start=(kt == 0), stop=False)
                        nc.tensor.matmul(psO[g][0:HD + 1], vl[0:rows, kt, g], eh[0:rows, slot], start=False, stop=False)
                        pe.wait_ge(el_done, n * J + j + 1)
                        nc.tensor.matmul(psO[g][0:HD + 1], vh[0:rows, kt, g], el[0:rows, slot],
                                         start=False, stop=(kt == KT - 1)).then_inc(pv_done, 1)
                    pe.wait_ge(pv_done, n * J + J + 4)
                    pe.sem_inc(q_free, 1)

                tile(0, 0, first=True)
                with pe.Fori(0, NT // 2 - 1) as i:
                    tile(2 * i + 1, 1)
                    tile(2 * i + 2, 0)
                tile(NT - 1, 1)
                turn(NT - 1, 1)


def stage_output(nc, d, name, left, right, gates, w, resid, gain, total, normed):
    with ExitStack() as stack:
        st = Stage(nc, name, stack)
        wt = st.sb("w", [P, KD, D])
        wh = st.sb("wh", [P, KD, D], F32R)
        wl = st.sb("wl", [P, KD, D], F32R)
        ident = st.sb("ident", [P, P])
        eps = st.sb("eps", [P, 1])
        gn = st.sb("gn", [P, D])
        mixed = st.sb("mixed", [P, 2, D])
        gt = st.sb("gt", [P, 2, D])
        rs = st.sb("rs", [P, 2, D])
        gm = st.sb("gm", [P, 2, D])
        mh = st.sb("mh", [P, 2, KD, P], F32R)
        ml = st.sb("ml", [P, 2, KD, P], F32R)
        h = st.sb("h", [P, 2, D])
        sq = st.sb("sq", [P, D])
        stat = st.sb("stat", [P, 2, 4])
        o = st.sb("o", [P, 2, D])
        psT = st.ps("psT", [P, KD, P])
        psH = [st.ps(f"psH{k}", [P, D]) for k in range(2)]
        w_loaded = [st.sem(f"w_loaded{kd}") for kd in range(KD)]
        wh_ready = st.sem("wh_ready")
        wl_ready = st.sem("wl_ready")
        c_loaded = st.sem("c_loaded")
        loaded = [st.sem(f"loaded{k}") for k in range(2)]
        r_loaded = [st.sem(f"r_loaded{k}") for k in range(2)]
        in_free = st.sem("in_free")
        eps_set = st.sem("eps_set")
        gated = st.sem("gated")
        t_done = st.sem("t_done")
        mh_ready = st.sem("mh_ready")
        ml_ready = st.sem("ml_ready")
        p_done = st.sem("p_done")
        h_ready = st.sem("h_ready")
        act_step = st.sem("act_step")
        r_ready = st.sem("r_ready")
        o_ready = st.sem("o_ready")
        stored = [st.sem(f"stored{k}") for k in range(2)]
        LOADS = 3 if gates else 2
        STORES = 2 if total else 1

        with nc.Block() as block:

            @block.sync
            def _(sp):
                sp.dma_start(ident[:], d["ident"]).then_inc(c_loaded, 16)
                sp.dma_start(gn[:], to_all(d[gain])).then_inc(c_loaded, 16)

                def load(n, k):
                    count, = ahead(sp, n + 1)
                    sp.wait_ge(t_done, count)
                    sp.dma_start(mixed[:, k, 0:FW], d[left][rows_of(n)]).then_inc(loaded[k], 16)
                    sp.dma_start(mixed[:, k, FW:D], d[right][rows_of(n)]).then_inc(loaded[k], 16)
                    if gates:
                        sp.dma_start(gt[:, k], d[gates][rows_of(n)]).then_inc(loaded[k], 16)
                    sp.wait_ge(in_free, count)
                    sp.dma_start(rs[:, k], d[resid][rows_of(n)]).then_inc(r_loaded[k], 16)

                def store(n, k):
                    count, = ahead(sp, n + 1)
                    sp.wait_ge(o_ready, count)
                    sp.dma_start(d[normed][rows_of(n)], o[:, k]).then_inc(stored[k], 16)
                    if total:
                        sp.dma_start(d[total][rows_of(n)], h[:, k]).then_inc(stored[k], 16)

                for k in range(2):
                    load(k, k)
                for kd in range(KD):
                    sp.dma_start(wt[:, kd], d[w][0, kd * P:(kd + 1) * P]).then_inc(w_loaded[kd], 16)
                with sp.Fori(0, NT // 2 - 1) as i:
                    for k in range(2):
                        load(2 * i + k + 2, k)
                        store(2 * i + k, k)
                for k in range(2):
                    store(NT - 2 + k, k)
                for k in range(2):
                    sp.wait_ge(stored[k], 16 * STORES * (NT // 2 + 1))

            @block.gpsimd
            def _(pool):
                pool.wait_ge(eps_set, 1)
                if gates:
                    with pool.Fori(0, NT // 2) as i:
                        for k in range(2):
                            pool.wait_ge(loaded[k], 16 * LOADS * i + 16 * LOADS)
                            pool.wait_ge(t_done, 2 * i + k + 1)
                            nc.gpsimd.tensor_tensor(gm[:, k], mixed[:, k], gt[:, k], ALU.mult).then_inc(gated, 1)

            @block.scalar
            def _(act):
                nc.scalar.preload_act_table_set("natural_log_exp_and_others")
                chain = Chain(act, act_step)
                act.wait_ge(eps_set, 1)
                for kd in range(KD):
                    act.wait_ge(w_loaded[kd], 16)
                    nc.scalar.copy(wh[:, kd], wt[:, kd]).then_inc(wh_ready, 1)

                def turned(n, k):
                    act.wait_ge(t_done, n + 3)
                    act.wait_ge(p_done, n + 1)
                    nc.scalar.copy(mh[:, k], psT[:]).then_inc(mh_ready, 1)

                def stats(n, k):
                    act.wait_ge(h_ready, n + 1)
                    chain.link(nc.scalar.activation(sq[:], h[:, k], ACT.Square, accum_out=stat[:, k, 0:1]))
                    chain.link(nc.scalar.activation(stat[:, k, 1:2], stat[:, k, 0:1], ACT.Ln, scale=1.0 / D, bias=eps[:, 0:1]))
                    nc.scalar.activation(stat[:, k, 2:3], stat[:, k, 1:2], ACT.Exp, scale=-0.5).then_inc(r_ready, 1)

                turned(0, 0)
                with act.Fori(0, NT // 2 - 1) as i:
                    chain.at(4 * i)
                    for k in range(2):
                        turned(2 * i + k + 1, 1 - k)
                        stats(2 * i + k, k)
                chain.at(2 * NT - 4)
                turned(NT - 1, 1)
                stats(NT - 2, 0)
                stats(NT - 1, 1)

            @block.tensor
            def _(pe):
                pe.sem_inc(t_done, 2)
                pe.sem_inc(p_done, 2)
                pe.wait_ge(c_loaded, 32)
                src = gm if gates else mixed

                def turn(n, k, m):
                    if gates:
                        pe.wait_ge(gated, n + 1)
                    else:
                        pe.wait_ge(loaded[k], 16 * LOADS * m)
                    for kd in range(KD):
                        t = nc.tensor.transpose(psT[:, kd], src[:, k, kd * P:(kd + 1) * P], ident[:])
                    t.then_inc(t_done, 1)

                def products(n, k, half):
                    cols = slice(half * 512, (half + 1) * 512)
                    for kd in range(KD):
                        nc.tensor.matmul(psH[k][:, cols], mh[:, k, kd], wh[:, kd, cols], start=(kd == 0), stop=False)
                        nc.tensor.matmul(psH[k][:, cols], mh[:, k, kd], wl[:, kd, cols], start=False, stop=False)
                        mm = nc.tensor.matmul(psH[k][:, cols], ml[:, k, kd], wh[:, kd, cols], start=False, stop=(kd == KD - 1))
                    return mm

                def tile(n, k, m_next, last=False):
                    pe.wait_ge(mh_ready, n + 1)
                    pe.wait_ge(ml_ready, n + 1)
                    products(n, k, 0)
                    if not last:
                        turn(n + 1, 1 - k, m_next)
                    products(n, k, 1).then_inc(p_done, 1)

                turn(0, 0, 1)
                pe.wait_ge(wh_ready, KD)
                pe.wait_ge(wl_ready, KD)
                with pe.Fori(0, NT // 2 - 1) as i:
                    tile(2 * i, 0, i + 1)
                    tile(2 * i + 1, 1, i + 2)
                tile(NT - 2, 0, NT // 2)
                tile(NT - 1, 1, 0, last=True)

            @block.vector
            def _(dve):
                nc.vector.memset(eps[:], EPS).then_inc(eps_set, 1)
                dve.sem_inc(in_free, 2)
                for k in range(2):
                    dve.sem_inc(stored[k], 16 * STORES)
                for kd in range(KD):
                    dve.wait_ge(wh_ready, kd + 1)
                    nc.vector.tensor_tensor(wl[:, kd], wt[:, kd], wh[:, kd], ALU.subtract).then_inc(wl_ready, 1)
                dve.wait_ge(c_loaded, 32)

                def turned(n, k):
                    dve.wait_ge(mh_ready, n + 1)
                    nc.vector.tensor_tensor(ml[:, k], psT[:], mh[:, k], ALU.subtract).then_inc(ml_ready, 1)

                def total_and_norm(n, k, m):
                    dve.wait_ge(r_loaded[k], 16 * m)
                    dve.wait_ge(p_done, n + 3)
                    dve.wait_ge(stored[k], 16 * STORES * m)
                    nc.vector.tensor_tensor(h[:, k], psH[k][:], rs[:, k], ALU.add).then_inc(h_ready, 1)
                    dve.wait_ge(h_ready, n + 1)
                    dve.sem_inc(in_free, 1)
                    dve.wait_ge(r_ready, n + 1)
                    nc.vector.scalar_tensor_tensor(o[:, k], h[:, k], stat[:, k, 2:3], gn[:], ALU.mult, ALU.mult).then_inc(o_ready, 1)

                turned(0, 0)
                with dve.Fori(0, NT // 2 - 1) as i:
                    for k in range(2):
                        turned(2 * i + k + 1, 1 - k)
                        total_and_norm(2 * i + k, k, i + 1)
                turned(NT - 1, 1)
                for k in range(2):
                    total_and_norm(NT - 2 + k, k, NT // 2)


def stage_rope2(nc, d):
    NF = 16
    TP = S // P
    C1 = 6.28125
    C2 = 2 * np.pi - C1
    ROUND = 1.5 * 2 ** 23
    LIM = 3.1415925
    with ExitStack() as stack:
        st = Stage(nc, "R", stack)
        pi = st.sb("pi", [P, TP], I32)
        pf = st.sb("pf", [P, TP])
        inv = st.sb("inv", [P, NF])
        ang = st.sb("ang", [P, TP, NF])
        turns = st.sb("turns", [P, TP, NF])
        r = st.sb("r", [P, TP, 2, NF])
        cs = st.sb("cs", [P, TP, 2, NF])
        loaded = st.sem("loaded")
        step = st.sem("step")
        r_ready = st.sem("r_ready")
        done = st.sem("done")
        stored = st.sem("stored")
        with nc.Block() as block:

            @block.sync
            def _(sp):
                sp.dma_start(pi[:], d["positions_2"].rearrange("a (p t) -> p (a t)", p=P)).then_inc(loaded, 16)
                sp.dma_start(inv[:], to_all(d["rope2_inv"])).then_inc(loaded, 16)
                sp.wait_ge(done, 2)
                sp.dma_start(d["cs2"].rearrange("(p t) c -> p (t c)", p=P), cs[:].rearrange("p t a c -> p (t a c)")).then_inc(stored, 16)
                sp.wait_ge(stored, 16)

            @block.vector
            def _(dve):
                chain = Chain(dve, step)
                dve.wait_ge(loaded, 32)
                chain.link(nc.vector.tensor_copy(pf[:], pi[:]))
                chain.link(nc.vector.tensor_tensor(ang[:], pf[:].unsqueeze(2).to_broadcast([P, TP, NF]),
                                                   inv[:].unsqueeze(1).to_broadcast([P, TP, NF]), ALU.mult))
                for a, (shift, quarter) in enumerate(((0.25, np.pi / 2), (0.0, 0.0))):
                    chain.link(nc.vector.tensor_scalar(turns[:], ang[:], 1.0 / (2 * np.pi), shift, ALU.mult, ALU.add))
                    chain.link(nc.vector.tensor_scalar(turns[:], turns[:], ROUND, -ROUND, ALU.add, ALU.add))
                    chain.link(nc.vector.scalar_tensor_tensor(r[:, :, a], turns[:], -C1, ang[:], ALU.mult, ALU.add))
                    chain.link(nc.vector.scalar_tensor_tensor(r[:, :, a], turns[:], -C2, r[:, :, a], ALU.mult, ALU.add))
                    chain.link(nc.vector.tensor_scalar(r[:, :, a], r[:, :, a], quarter, LIM, ALU.add, ALU.min))
                    nc.vector.tensor_scalar(r[:, :, a], r[:, :, a], -LIM, None, ALU.max).then_inc(r_ready, 1)

            @block.scalar
            def _(act):
                for a in range(2):
                    act.wait_ge(r_ready, a + 1)
                    nc.scalar.activation(cs[:, :, a], r[:, :, a], ACT.Sin).then_inc(done, 1)


LAT = QL + KVL + RD
def stage_project2(nc, d):
    with ExitStack() as stack:
        st = Stage(nc, "D", stack)
        ws = st.sb("ws", [P, 2, W2])
        wh = st.sb("wh", [P, KD, W2], F32R)
        wl = st.sb("wl", [P, KD, W2], F32R)
        gain = st.sb("gain", [P, KD])
        ident = st.sb("ident", [P, P])
        eps = st.sb("eps", [P, 1])
        bias = st.sb("bias", [P, 2, MLH])
        zero = st.sb("zero", [CONV - 1, ML])
        x = st.sb("x", [P, 2, D])
        sq = st.sb("sq", [P, D])
        stat = st.sb("stat", [P, 2, 4])
        u = st.sb("u", [P, 2, D])
        uh = st.sb("uh", [P, 2, KD, P], F32R)
        ul = st.sb("ul", [P, 2, KD, P], F32R)
        lat = st.sb("lat", [P, 2, LAT])
        xm = st.sb("xm", [P, 2, ML])
        ze = st.sb("ze", [P, ML])
        zs = st.sb("zs", [P, 2, ML])
        gi = st.sb("gi", [P, 2, 2 * MLH])
        psT = st.ps("psT", [P, KD, P])
        psG = [st.ps(f"psG{g}", [P, 512]) for g in range(4)]
        groups = [(QL + KVL + RD, ML), (QL + KVL + RD + ML, ML), (0, LAT), (LAT + 2 * ML, 2 * MLH)]
        XM, Z, LT, GI = range(4)
        w_loaded = [st.sem(f"w_loaded{k}") for k in range(2)]
        c_loaded = st.sem("c_loaded")
        wh_ready = st.sem("wh_ready")
        wl_ready = st.sem("wl_ready")
        eps_set = st.sem("eps_set")
        loaded = [st.sem(f"loaded{k}") for k in range(2)]
        act_step = st.sem("act_step")
        r_ready = st.sem("r_ready")
        u_ready = st.sem("u_ready")
        x_free = st.sem("x_free")
        t_done = st.sem("t_done")
        uh_ready = st.sem("uh_ready")
        ul_ready = st.sem("ul_ready")
        g_done = [st.sem(f"g_done{g}") for g in range(4)]
        g_free = [st.sem(f"g_free{g}") for g in range(4)]
        zx = st.sem("zx")
        a_ready = st.sem("a_ready")
        v_ready = st.sem("v_ready")
        stored = [st.sem(f"stored{k}") for k in range(2)]
        zero_stored = st.sem("zero_stored")

        with nc.Block() as block:

            @block.sync
            def _(sp):
                sp.dma_start(ident[:], d["ident"]).then_inc(c_loaded, 16)
                sp.dma_start(gain[:], d["norm_mix_g_2"].rearrange("a (k p) -> p (a k)", p=P), allow_slow_non_contiguous=True).then_inc(c_loaded, 16)
                sp.dma_start(bias[:, 0], to_all(d["b_igate_2"])).then_inc(c_loaded, 16)
                sp.dma_start(bias[:, 1], to_all(d["b_fgate_2"])).then_inc(c_loaded, 16)
                sp.wait_ge(eps_set, 1)
                sp.dma_start(d["xm"][0:CONV - 1], zero[:]).then_inc(zero_stored, 16)

                def load(n, k):
                    count, = ahead(sp, n + 1)
                    sp.wait_ge(x_free, count)
                    sp.wait_ge(eps_set, 1)
                    sp.dma_start(x[:, k], d["x1"][rows_of(n)]).then_inc(loaded[k], 16)

                def store(n, k):
                    count, = ahead(sp, n + 1)
                    sp.wait_ge(v_ready, count)
                    sp.wait_ge(a_ready, count)
                    sp.dma_start(d["xm"][bass.ds(n * P + CONV - 1, P)], xm[:, k]).then_inc(stored[k], 16)
                    sp.dma_start(d["lat"][rows_of(n)], lat[:, k]).then_inc(stored[k], 16)
                    sp.dma_start(d["z"][rows_of(n)], zs[:, k]).then_inc(stored[k], 16)
                    sp.dma_start(d["gi"][rows_of(n)], gi[:, k]).then_inc(stored[k], 16)

                for k in range(2):
                    load(k, k)
                for kd in range(KD):
                    if kd >= 2:
                        sp.wait_ge(wl_ready, kd - 1)
                    sp.dma_start(ws[:, kd % 2], d["w_in_2"][0, kd * P:(kd + 1) * P]).then_inc(w_loaded[kd % 2], 16)
                with sp.Fori(0, NT // 2 - 1) as i:
                    for k in range(2):
                        load(2 * i + k + 2, k)
                        store(2 * i + k, k)
                for k in range(2):
                    store(NT - 2 + k, k)
                for k in range(2):
                    sp.wait_ge(stored[k], 64 * (NT // 2 + 1))
                sp.wait_ge(zero_stored, 16)

            @block.gpsimd
            def _(pool):
                pool.sem_inc(x_free, 2)
                with pool.Fori(0, NT // 2) as i:
                    for k in range(2):
                        n = 2 * i + k
                        pool.wait_ge(r_ready, n + 1)
                        pool.wait_ge(t_done, n + 1)
                        nc.gpsimd.tensor_tensor(u[:, k], x[:, k], stat[:, k, 2:3].to_broadcast([P, D]), ALU.mult).then_inc(u_ready, 1)
                        pool.wait_ge(u_ready, n + 1)
                        pool.sem_inc(x_free, 1)

            @block.scalar
            def _(act):
                nc.scalar.preload_act_table_set("natural_log_exp_and_others")
                chain = Chain(act, act_step)
                for k in range(2):
                    act.sem_inc(stored[k], 64)
                act.wait_ge(eps_set, 1)
                act.wait_ge(c_loaded, 64)

                def weights():
                    for kd in range(KD):
                        act.wait_ge(w_loaded[kd % 2], 16 * (kd // 2) + 16)
                        nc.scalar.mul(wh[:, kd], ws[:, kd % 2], gain[:, kd:kd + 1]).then_inc(wh_ready, 1)

                def stats(k, m):
                    act.wait_ge(loaded[k], 16 * m)
                    chain.link(nc.scalar.activation(sq[:], x[:, k], ACT.Square, accum_out=stat[:, k, 0:1]))
                    chain.link(nc.scalar.activation(stat[:, k, 1:2], stat[:, k, 0:1], ACT.Ln, scale=1.0 / D, bias=eps[:, 0:1]))
                    nc.scalar.activation(stat[:, k, 2:3], stat[:, k, 1:2], ACT.Exp, scale=-0.5).then_inc(r_ready, 1)

                def turned(n, k):
                    act.wait_ge(t_done, n + 3)
                    act.wait_ge(g_done[GI], n + 1)
                    nc.scalar.copy(uh[:, k], psT[:]).then_inc(uh_ready, 1)

                def rest(n, k, m, last=False):
                    act.wait_ge(g_done[XM], n + 1)
                    act.wait_ge(stored[k], 64 * m)
                    nc.scalar.copy(xm[:, k], psG[XM][:]).then_inc(g_free[XM], 1)
                    if not last:
                        turned(n + 1, 1 - k)
                    act.wait_ge(g_done[Z], n + 1)
                    chain.link(nc.scalar.activation(ze[:], psG[Z][:], ACT.Exp, scale=-1.0))
                    chain.link(nc.scalar.activation(ze[:], ze[:], ACT.Ln, bias=1.0))
                    chain.link(nc.scalar.activation(ze[:], ze[:], ACT.Exp, scale=-1.0))
                    act.sem_inc(zx, 1)
                    act.wait_ge(g_done[LT], n + 1)
                    nc.scalar.copy(lat[:, k], psG[LT][:, 0:LAT]).then_inc(a_ready, 1)
                    act.wait_ge(a_ready, n + 1)
                    act.sem_inc(g_free[LT], 1)
                    act.wait_ge(v_ready, n + 1)

                stats(0, 1)
                weights()
                turned(0, 0)
                with act.Fori(0, NT // 2 - 1) as i:
                    chain.at(10 * i + 2)
                    stats(1, i + 1)
                    rest(2 * i, 0, i + 1)
                    stats(0, i + 2)
                    rest(2 * i + 1, 1, i + 1)
                chain.at(10 * (NT // 2 - 1) + 2)
                stats(1, NT // 2)
                rest(NT - 2, 0, NT // 2)
                rest(NT - 1, 1, NT // 2, last=True)

            @block.tensor
            def _(pe):
                pe.sem_inc(t_done, 2)
                pe.sem_inc(g_done[GI], 2)
                pe.wait_ge(c_loaded, 64)

                def turn(n, k):
                    pe.wait_ge(u_ready, n + 1)
                    for kd in range(KD):
                        t = nc.tensor.transpose(psT[:, kd], u[:, k, kd * P:(kd + 1) * P], ident[:])
                    t.then_inc(t_done, 1)

                def tile(n, k, last=False):
                    pe.wait_ge(uh_ready, n + 1)
                    pe.wait_ge(ul_ready, n + 1)
                    for g, (c0, width) in enumerate(groups):
                        pe.wait_ge(g_free[g], n + 1)
                        for kd in range(KD):
                            out, cols = psG[g][:, 0:width], slice(c0, c0 + width)
                            nc.tensor.matmul(out, uh[:, k, kd], wh[:, kd, cols], start=(kd == 0), stop=False)
                            nc.tensor.matmul(out, uh[:, k, kd], wl[:, kd, cols], start=False, stop=False)
                            mm = nc.tensor.matmul(out, ul[:, k, kd], wh[:, kd, cols], start=False, stop=(kd == KD - 1))
                        mm.then_inc(g_done[g], 1)
                        if g == XM and not last:
                            turn(n + 1, 1 - k)

                turn(0, 0)
                pe.wait_ge(wh_ready, KD)
                pe.wait_ge(wl_ready, KD)
                with pe.Fori(0, NT // 2 - 1) as i:
                    for k in range(2):
                        tile(2 * i + k, k)
                tile(NT - 2, 0)
                tile(NT - 1, 1, last=True)

            @block.vector
            def _(dve):
                nc.vector.memset(zero[:], 0.0)
                nc.vector.memset(eps[:], EPS).then_inc(eps_set, 1)
                for g in range(4):
                    dve.sem_inc(g_free[g], 1)
                dve.wait_ge(c_loaded, 64)
                for kd in range(KD):
                    dve.wait_ge(wh_ready, kd + 1)
                    nc.vector.scalar_tensor_tensor(wl[:, kd], ws[:, kd % 2], gain[:, kd:kd + 1], wh[:, kd],
                                                   ALU.mult, ALU.subtract).then_inc(wl_ready, 1)

                def turned(n, k):
                    dve.wait_ge(uh_ready, n + 1)
                    nc.vector.tensor_tensor(ul[:, k], psT[:], uh[:, k], ALU.subtract).then_inc(ul_ready, 1)

                def tile(n, k, m, last=False):
                    if not last:
                        turned(n + 1, 1 - k)
                    dve.wait_ge(zx, n + 1)
                    dve.wait_ge(stored[k], 64 * m)
                    nc.vector.tensor_tensor(zs[:, k], psG[Z][:], ze[:], ALU.mult).then_inc(g_free[Z], 1)
                    dve.wait_ge(g_done[GI], n + 3)
                    nc.vector.tensor_tensor(gi[:, k], psG[GI][:, 0:2 * MLH], bias[:].rearrange("p a h -> p (a h)"), ALU.add).then_inc(v_ready, 1)
                    dve.wait_ge(v_ready, n + 1)
                    dve.sem_inc(g_free[GI], 1)

                turned(0, 0)
                with dve.Fori(0, NT // 2 - 1) as i:
                    for k in range(2):
                        tile(2 * i + k, k, i + 1)
                tile(NT - 2, 0, NT // 2)
                tile(NT - 1, 1, NT // 2, last=True)


def stage_mla_heads(nc, d):
    HQ = MH // 2
    with ExitStack() as stack:
        st = Stage(nc, "E", stack)
        ident = st.sb("ident", [P, P])
        eps = st.sb("eps", [P, 1])
        wq = st.sb("wq", [P, QL // P, MH * QD])
        wkv = st.sb("wkv", [P, MH * (ND + VD)])
        qg = st.sb("qg", [P, QL // P])
        kg = st.sb("kg", [P, 1])
        lat = st.sb("lat", [P, 2, LAT])
        cs = st.sb("cs", [P, 2, 2, RD // 2])
        sq = st.sb("sq", [P, QL])
        stat = st.sb("stat", [P, 2, 6])
        cn = st.sb("cn", [P, 2, QL + KVL])
        cT = st.sb("cT", [P, 2, 3, P])
        hq = st.sb("hq", [P, MH, QD])
        hk = st.sb("hk", [P, MH, QD])
        kr = st.sb("kr", [P, RD])
        rq = st.sb("rq", [P, 4, MH, RD // 2])
        rk = st.sb("rk", [P, 4, RD // 2])
        v = st.sb("v", [P, 2, MH, VD])
        qT = st.sb("qT", [QD, 2, MH, P])
        kT = st.sb("kT", [QD, 2, MH, P])
        psT = st.ps("psT", [P, 512])
        psQ = st.ps("psQ", [P, 2, 512])
        psK = st.ps("psK", [P, 2, 512])
        psX = st.ps("psX", [P, MH, P])
        loaded = [st.sem(f"loaded{k}") for k in range(2)]
        c_loaded = st.sem("c_loaded")
        w_loaded = st.sem("w_loaded")
        w_ready = st.sem("w_ready")
        eps_set = st.sem("eps_set")
        in_free = st.sem("in_free")
        act_step = st.sem("act_step")
        r_ready = st.sem("r_ready")
        cn_ready = st.sem("cn_ready")
        t_done = st.sem("t_done")
        cT_ready = st.sem("cT_ready")
        p_done = st.sem("p_done")
        hq_ready = st.sem("hq_ready")
        hk_ready = st.sem("hk_ready")
        dve_step = st.sem("dve_step")
        rot_q = st.sem("rot_q")
        rot_k = st.sem("rot_k")
        x_done = st.sem("x_done")
        qT_ready = st.sem("qT_ready")
        kT_ready = st.sem("kT_ready")
        stored = [st.sem(f"stored{k}") for k in range(2)]
        with nc.Block() as block:

            @block.sync
            def _(sp):
                def load(n, k):
                    count, = ahead(sp, n + 1)
                    sp.wait_ge(in_free, count)
                    sp.dma_start(lat[:, k], d["lat"][rows_of(n)]).then_inc(loaded[k], 16)
                    sp.dma_start(cs[:, k].rearrange("p a c -> p (a c)"), d["cs2"][rows_of(n)]).then_inc(loaded[k], 16)

                def store(n, k):
                    count, = ahead(sp, n + 1)
                    sp.wait_ge(qT_ready, count)
                    sp.wait_ge(kT_ready, count)
                    sp.dma_start(d["v2"][rows_of(n)], v[:, k].rearrange("p h c -> p (h c)")).then_inc(stored[k], 16)
                    sp.dma_start(d["qT2"][:, bass.ds(n * P, P)].rearrange("(h c) s -> c h s", c=QD), qT[:, k]).then_inc(stored[k], 16)
                    sp.dma_start(d["kT2"][:, bass.ds(n * P, P)].rearrange("(h c) s -> c h s", c=QD), kT[:, k]).then_inc(stored[k], 16)

                sp.dma_start(ident[:], d["ident"]).then_inc(c_loaded, 16)
                sp.dma_start(qg[:], d["q_norm_g_2"].rearrange("a (k p) -> p (a k)", p=P), allow_slow_non_contiguous=True).then_inc(c_loaded, 16)
                sp.dma_start(kg[:], d["kv_norm_g_2"].rearrange("a p -> p a"), allow_slow_non_contiguous=True).then_inc(c_loaded, 16)
                for k in range(2):
                    load(k, k)
                sp.dma_start(wq[:], d["w_uq_2"].rearrange("a (k p) n -> p (a k) n", p=P)).then_inc(w_loaded, 16)
                sp.dma_start(wkv[:], d["w_ukv_2"][0]).then_inc(w_loaded, 16)
                with sp.Fori(0, NT // 2 - 1) as i:
                    for k in range(2):
                        load(2 * i + k + 2, k)
                        store(2 * i + k, k)
                for k in range(2):
                    store(NT - 2 + k, k)
                for k in range(2):
                    sp.wait_ge(stored[k], 48 * (NT // 2 + 1))

            @block.scalar
            def _(act):
                nc.scalar.preload_act_table_set("natural_log_exp_and_others")
                chain = Chain(act, act_step)
                for k in range(2):
                    act.sem_inc(stored[k], 48)
                act.wait_ge(eps_set, 1)

                def stats(k, m):
                    act.wait_ge(loaded[k], 32 * m)
                    chain.link(nc.scalar.activation(sq[:], lat[:, k, 0:QL], ACT.Square, accum_out=stat[:, k, 0:1]))
                    chain.link(nc.scalar.activation(sq[:, 0:KVL], lat[:, k, QL:QL + KVL], ACT.Square, accum_out=stat[:, k, 1:2]))
                    nc.scalar.activation(stat[:, k, 2:3], stat[:, k, 0:1], ACT.Ln, scale=1.0 / QL, bias=eps[:, 0:1])
                    chain.link(nc.scalar.activation(stat[:, k, 3:4], stat[:, k, 1:2], ACT.Ln, scale=1.0 / KVL, bias=eps[:, 0:1]))
                    nc.scalar.activation(stat[:, k, 4:6], stat[:, k, 2:4], ACT.Exp, scale=-0.5).then_inc(r_ready, 1)

                def tile(n, k, m):
                    act.wait_ge(p_done, n + 1)
                    act.wait_ge(x_done, 2 * n + 1)
                    for b in range(2):
                        copy = nc.scalar.copy(hq[:, b * HQ:(b + 1) * HQ].rearrange("p h c -> p (h c)"), psQ[:, b, 0:HQ * QD])
                    copy.then_inc(hq_ready, 1)
                    act.wait_ge(stored[k], 48 * m)
                    for b in range(2):
                        kv = psK[:, b].rearrange("p (h c) -> p h c", c=ND + VD)
                        nc.scalar.copy(hk[:, b * HQ:(b + 1) * HQ, 0:ND], kv[:, :, 0:ND])
                        copy = nc.scalar.copy(v[:, k, b * HQ:(b + 1) * HQ], kv[:, :, ND:ND + VD])
                    copy.then_inc(hk_ready, 1)
                    act.wait_ge(x_done, 2 * n + 2)
                    chain.link(nc.scalar.copy(qT[:, k], psX[0:QD]))
                    act.sem_inc(qT_ready, 1)

                stats(0, 1)
                with act.Fori(0, NT // 2 - 1) as i:
                    chain.at(8 * i + 3)
                    stats(1, i + 1)
                    tile(2 * i, 0, i + 1)
                    stats(0, i + 2)
                    tile(2 * i + 1, 1, i + 1)
                    assert chain.n == 8
                chain.at(8 * (NT // 2 - 1) + 3)
                stats(1, NT // 2)
                tile(NT - 2, 0, NT // 2)
                tile(NT - 1, 1, NT // 2)

            @block.vector
            def _(dve):
                chain = Chain(dve, dve_step)
                nc.vector.memset(eps[:], EPS).then_inc(eps_set, 1)
                dve.sem_inc(in_free, 2)
                dve.wait_ge(c_loaded, 48)
                dve.wait_ge(w_loaded, 32)
                for j in range(QL // P):
                    nc.vector.tensor_scalar(wq[:, j], wq[:, j], qg[:, j:j + 1], QD ** -0.5, ALU.mult, ALU.mult)
                nc.vector.tensor_scalar(wkv[:], wkv[:], kg[:, 0:1], None, ALU.mult).then_inc(w_ready, 1)
                half = RD // 2

                def normed(n, k):
                    dve.wait_ge(r_ready, n + 1)
                    dve.wait_ge(t_done, n + 1)
                    nc.vector.tensor_scalar(cn[:, k, 0:QL], lat[:, k, 0:QL], stat[:, k, 4:5], None, ALU.mult)
                    nc.vector.tensor_scalar(cn[:, k, QL:QL + KVL], lat[:, k, QL:QL + KVL], stat[:, k, 5:6], None,
                                            ALU.mult).then_inc(cn_ready, 1)

                def turned(n, k):
                    dve.wait_ge(t_done, n + 3)
                    nc.vector.tensor_copy(cT[:, k].rearrange("p a c -> p (a c)"), psT[:, 0:3 * P]).then_inc(cT_ready, 1)

                def tile(n, k, m, last=False):
                    cos, sin = cs[:, k, 0], cs[:, k, 1]
                    x1, x2 = lat[:, k, QL + KVL:QL + KVL + half], lat[:, k, QL + KVL + half:LAT]
                    nc.vector.tensor_tensor(rk[:, 0], x1, cos, ALU.mult)
                    nc.vector.tensor_tensor(rk[:, 1], x2, sin, ALU.mult)
                    nc.vector.tensor_tensor(rk[:, 2], x1, sin, ALU.mult)
                    chain.link(nc.vector.tensor_tensor(rk[:, 3], x2, cos, ALU.mult))
                    nc.vector.tensor_tensor(kr[:, 0:half], rk[:, 0], rk[:, 1], ALU.subtract)
                    chain.link(nc.vector.tensor_tensor(kr[:, half:RD], rk[:, 2], rk[:, 3], ALU.add))
                    dve.wait_ge(hq_ready, n + 1)
                    cosb, sinb = (a.unsqueeze(1).to_broadcast([P, MH, half]) for a in (cos, sin))
                    x1, x2 = hq[:, :, ND:ND + half], hq[:, :, ND + half:QD]
                    nc.vector.tensor_tensor(rq[:, 0], x1, cosb, ALU.mult)
                    nc.vector.tensor_tensor(rq[:, 1], x2, sinb, ALU.mult)
                    nc.vector.tensor_tensor(rq[:, 2], x1, sinb, ALU.mult)
                    chain.link(nc.vector.tensor_tensor(rq[:, 3], x2, cosb, ALU.mult))
                    dve.sem_inc(in_free, 1)
                    nc.vector.tensor_tensor(x1, rq[:, 0], rq[:, 1], ALU.subtract)
                    nc.vector.tensor_tensor(x2, rq[:, 2], rq[:, 3], ALU.add).then_inc(rot_q, 1)
                    if not last:
                        normed(n + 1, 1 - k)
                    dve.wait_ge(hk_ready, n + 1)
                    nc.vector.tensor_copy(hk[:, :, ND:QD], kr[:].unsqueeze(1).to_broadcast([P, MH, RD])).then_inc(rot_k, 1)
                    if not last:
                        turned(n + 1, 1 - k)
                    dve.wait_ge(x_done, 2 * n + 3)
                    dve.wait_ge(stored[k], 48 * m)
                    nc.vector.tensor_copy(kT[:, k], psX[0:QD]).then_inc(kT_ready, 1)

                normed(0, 0)
                turned(0, 0)
                with dve.Fori(0, NT // 2 - 1) as i:
                    chain.at(6 * i)
                    tile(2 * i, 0, i + 1)
                    tile(2 * i + 1, 1, i + 1)
                    assert chain.n == 6
                chain.at(6 * (NT // 2 - 1))
                tile(NT - 2, 0, NT // 2)
                tile(NT - 1, 1, NT // 2, last=True)

            @block.tensor
            def _(pe):
                pe.sem_inc(t_done, 2)
                pe.sem_inc(x_done, 1)
                pe.wait_ge(c_loaded, 48)
                pe.wait_ge(w_ready, 1)

                def turn(n, k):
                    pe.wait_ge(cn_ready, n + 1)
                    for j in range(3):
                        t = nc.tensor.transpose(psT[:, j * P:(j + 1) * P], cn[:, k, j * P:(j + 1) * P], ident[:])
                    t.then_inc(t_done, 1)

                def tile(n, k, last=False):
                    pe.wait_ge(cT_ready, n + 1)
                    for b in range(2):
                        for j in range(QL // P):
                            nc.tensor.matmul(psQ[:, b, 0:HQ * QD], cT[:, k, j], wq[:, j, b * HQ * QD:(b + 1) * HQ * QD],
                                             start=(j == 0), stop=(j == QL // P - 1))
                    for b in range(2):
                        mm = nc.tensor.matmul(psK[:, b], cT[:, k, 2], wkv[:, b * 512:(b + 1) * 512], start=True, stop=True)
                    mm.then_inc(p_done, 1)
                    pe.wait_ge(rot_q, n + 1)
                    pe.wait_ge(hk_ready, n + 1)
                    for h in range(MH):
                        t = nc.tensor.transpose(psX[0:QD, h], hq[:, h], ident[:])
                    t.then_inc(x_done, 1)
                    if not last:
                        turn(n + 1, 1 - k)
                    pe.wait_ge(rot_k, n + 1)
                    pe.wait_ge(qT_ready, n + 1)
                    for h in range(MH):
                        t = nc.tensor.transpose(psX[0:QD, h], hk[:, h], ident[:])
                    t.then_inc(x_done, 1)

                turn(0, 0)
                with pe.Fori(0, NT // 2 - 1) as i:
                    for k in range(2):
                        tile(2 * i + k, k)
                tile(NT - 2, 0)
                tile(NT - 1, 1, last=True)


def stage_attention2(nc, d):
    QC = 512
    CH = S // QC
    PAIRS = [(c, kt) for c in range(CH) for kt in range((c + 1) * QC // P)]
    J = len(PAIRS)
    with ExitStack() as stack:
        st = Stage(nc, "F", stack)
        ident = st.sb("ident", [P, P])
        kT = st.sb("kT", [QD + 1, 2, S])
        qa = st.sb("qa", [QD + 1, 2, S])
        v1 = st.sb("v1", [P, 2, NT, VD + 1])
        kh, kl, qh, ql = (st.sb(name, [QD + 1, 2, S], F32R) for name in ("kh", "kl", "qh", "ql"))
        vh, vl = (st.sb(name, [P, 2, NT, VD + 1], F32R) for name in ("vh", "vl"))
        e = st.sb("e", [P, 4, QC])
        eh = st.sb("eh", [P, 4, QC], F32R)
        el = st.sb("el", [P, 4, QC], F32R)
        oT = st.sb("oT", [VD + 1, 2, QC])
        rs = st.sb("rs", [P, QC // P])
        ao = st.sb("ao", [P, 2, QC // P, VD])
        psS = [st.ps(f"psS{s}", [P, QC]) for s in range(4)]
        psO = [st.ps(f"psO{g}", [P, QC]) for g in range(2)]
        psR = st.ps("psR", [P, QC // P, VD + 1])
        set_done = st.sem("set_done")
        c_loaded = st.sem("c_loaded")
        loaded = [st.sem(f"loaded{k}") for k in range(2)]
        h_free = st.sem("h_free")
        s_done = st.sem("s_done")
        e_done = st.sem("e_done")
        el_done = st.sem("el_done")
        high_done = st.sem("high_done")
        low_done = st.sem("low_done")
        pv_done = st.sem("pv_done")
        oT_ready = st.sem("oT_ready")
        t_done = st.sem("t_done")
        r_ready = st.sem("r_ready")
        ao_ready = st.sem("ao_ready")
        stored = [st.sem(f"stored{k}") for k in range(2)]

        def shape(j):
            c, kt = PAIRS[j]
            first = max(0, kt * P - c * QC)
            return c, kt, first, QC - first, kt * P >= c * QC

        with nc.Block() as block:

            @block.sync
            def _(sp):
                sp.dma_start(ident[:], d["ident"]).then_inc(c_loaded, 16)
                sp.wait_ge(set_done, 1)
                with sp.Fori(0, MH // 2) as i:
                    for k in range(2):
                        h = 2 * i + k
                        count, row, col = ahead(sp, h + 1, h * QD, h * VD)
                        sp.wait_ge(low_done, count)
                        sp.dma_start(kT[0:QD, k], d["kT2"][bass.ds(row, QD)]).then_inc(loaded[k], 16)
                        sp.dma_start(qa[0:QD, k], d["qT2"][bass.ds(row, QD)]).then_inc(loaded[k], 16)
                        sp.dma_start(qa[QD:QD + 1, k], d["negm2"][bass.ds(h, 1)]).then_inc(loaded[k], 16)
                        sp.dma_start(v1[:, k, :, 0:VD], d["v2"][:, bass.ds(col, VD)].rearrange("(t p) c -> p t c", p=P)).then_inc(loaded[k], 16)

            @block.gpsimd
            def _(pool):
                pool.sem_inc(low_done, 2)

                def low(h, k):
                    pool.wait_ge(high_done, h + 1)
                    nc.gpsimd.tensor_tensor(kl[:, k], kT[:, k], kh[:, k], ALU.subtract)
                    nc.gpsimd.tensor_tensor(ql[:, k], qa[:, k], qh[:, k], ALU.subtract)
                    nc.gpsimd.tensor_tensor(vl[:, k], v1[:, k], vh[:, k], ALU.subtract).then_inc(low_done, 1)

                def store(h, c):
                    pool.wait_ge(ao_ready, h * CH + c + 1)
                    at = d["attn2"][c * QC:(c + 1) * QC, bass.ds(h * VD, VD)].rearrange("(t p) v -> p t v", p=P)
                    pool.dma_start(at, ao[:, c % 2]).then_inc(stored[c % 2], 16)

                def head(h, k, last=False):
                    store(h, 0)
                    store(h, 1)
                    if not last:
                        low(h + 1, 1 - k)
                    store(h, 2)
                    store(h, 3)

                low(0, 0)
                with pool.Fori(0, MH // 2 - 1) as i:
                    for k in range(2):
                        head(2 * i + k, k)
                head(MH - 2, 0)
                head(MH - 1, 1, last=True)
                for k in range(2):
                    pool.wait_ge(stored[k], 16 * MH * CH // 2)

            @block.vector
            def _(dve):
                nc.vector.memset(v1[:], 1.0)
                nc.vector.memset(kT[QD:QD + 1], 1.0).then_inc(set_done, 1)

                END = [max(j for j in range(J) if PAIRS[j][0] == c) for c in range(CH)]

                def high(h, k, m):
                    dve.wait_ge(loaded[k], 64 * m)
                    dve.wait_ge(h_free, h + 1)
                    nc.vector.tensor_copy(kh[:, k], kT[:, k])
                    nc.vector.tensor_copy(qh[:, k], qa[:, k])
                    nc.vector.tensor_copy(vh[:, k], v1[:, k]).then_inc(high_done, 1)

                def take(h, c):
                    dve.wait_ge(pv_done, h * J + END[c] + 5)
                    nc.vector.tensor_copy(oT[:, c % 2], psO[c % 2][0:VD + 1]).then_inc(oT_ready, 1)

                def divide(h, c):
                    dve.wait_ge(t_done, h * CH + c + 1)
                    nc.vector.reciprocal(rs[:], psR[:, :, VD]).then_inc(r_ready, 1)
                    dve.wait_ge(r_ready, h * CH + c + 1)
                    if not (isinstance(h, int) and h == 0 and c < 2):
                        dve.wait_ge(stored[c % 2], h * 32 + 16 * (c // 2))
                    nc.vector.tensor_tensor(ao[:, c % 2], psR[:, :, 0:VD], rs[:].unsqueeze(2).to_broadcast([P, QC // P, VD]),
                                            ALU.mult).then_inc(ao_ready, 1)

                def head(h, k, m, last=False):
                    for j in range(J):
                        c, kt, first, w, diagonal = shape(j)
                        slot = j % 4
                        dve.wait_ge(e_done, h * J + j + 1)
                        if diagonal:
                            nc.vector.tensor_tensor(el[0:64, slot, 0:64], e[0:64, slot, 0:64], eh[0:64, slot, 0:64], ALU.subtract)
                            nc.vector.tensor_tensor(el[:, slot, 64:w], e[:, slot, 64:w], eh[:, slot, 64:w], ALU.subtract).then_inc(el_done, 1)
                        else:
                            nc.vector.tensor_tensor(el[:, slot], e[:, slot], eh[:, slot], ALU.subtract).then_inc(el_done, 1)
                        for c in range(CH - 1):
                            if j == END[c] + 2:
                                take(h, c)
                            if j == END[c] + 6:
                                divide(h, c)
                        if j == END[1] + 8 and not last:
                            high(h + 1, 1 - k, m + k)
                    take(h, CH - 1)
                    divide(h, CH - 1)

                high(0, 0, 1)
                for k in range(2):
                    head(k, k, 1)
                with dve.Fori(1, MH // 2 - 1) as i:
                    for k in range(2):
                        head(2 * i + k, k, i + 1)
                head(MH - 2, 0, MH // 2)
                head(MH - 1, 1, MH // 2, last=True)

            @block.scalar
            def _(act):
                nc.scalar.preload_act_table_set("natural_log_exp_and_others")
                with act.Fori(0, MH // 2) as i:
                    for k in range(2):
                        for j in range(J):
                            c, kt, first, w, diagonal = shape(j)
                            slot = j % 4
                            act.wait_ge(s_done, (2 * i + k) * J + j + 1)
                            act.wait_ge(pv_done, (2 * i + k) * J + j + 1)
                            if diagonal:
                                nc.scalar.activation(e[0:64, slot, 0:64], psS[slot][0:64, 0:64], ACT.Exp)
                                nc.scalar.activation(eh[0:64, slot, 0:64], psS[slot][0:64, 0:64], ACT.Exp)
                                nc.scalar.activation(e[:, slot, 64:w], psS[slot][:, 64:w], ACT.Exp)
                                nc.scalar.activation(eh[:, slot, 64:w], psS[slot][:, 64:w], ACT.Exp).then_inc(e_done, 1)
                            else:
                                nc.scalar.activation(e[:, slot], psS[slot][:], ACT.Exp)
                                nc.scalar.activation(eh[:, slot], psS[slot][:], ACT.Exp).then_inc(e_done, 1)

            @block.tensor
            def _(pe):
                pe.sem_inc(pv_done, 4)
                pe.sem_inc(h_free, 2)
                pe.wait_ge(set_done, 1)
                pe.wait_ge(c_loaded, 16)
                with pe.Fori(0, MH // 2) as i:
                    for k in range(2):
                        h = 2 * i + k

                        def scores(j):
                            c, kt, first, w, diagonal = shape(j)
                            keys, queries = slice(kt * P, (kt + 1) * P), slice(c * QC + first, (c + 1) * QC)
                            s = psS[j % 4][:, 0:w]
                            nc.tensor.matmul(s, kh[:, k, keys], qh[:, k, queries], start=True, stop=False)
                            nc.tensor.matmul(s, kh[:, k, keys], ql[:, k, queries], start=False, stop=False)
                            nc.tensor.matmul(s, kl[:, k, keys], qh[:, k, queries], start=False, stop=True).then_inc(s_done, 1)

                        def turn(c):
                            pe.wait_ge(oT_ready, h * CH + c + 1)
                            for t in range(QC // P):
                                mm = nc.tensor.transpose(psR[:, t], oT[:, c % 2, t * P:(t + 1) * P], ident[0:VD + 1, 0:VD + 1])
                            mm.then_inc(t_done, 1)

                        pe.wait_ge(low_done, h + 3)
                        scores(0)
                        scores(1)
                        for j in range(J):
                            c, kt, first, w, diagonal = shape(j)
                            if j + 2 < J:
                                scores(j + 2)
                            if c and kt == 3:
                                turn(c - 1)
                            pe.wait_ge(e_done, h * J + j + 1)
                            o = psO[c % 2][0:VD + 1]
                            last = kt == (c + 1) * QC // P - 1
                            passes = ((vh, eh), (vl, eh), (vh, el))
                            for q, (v, a) in enumerate(passes):
                                if q == 2:
                                    pe.wait_ge(el_done, h * J + j + 1)
                                opens, closes = kt == 0 and q == 0, last and q == 2
                                if diagonal:
                                    nc.tensor.matmul(o[:, first:first + 64], v[0:64, k, kt], a[0:64, j % 4, 0:64],
                                                     start=opens, stop=closes, skip_group_check=True)
                                    mm = nc.tensor.matmul(o[:, first + 64:QC], v[:, k, kt], a[:, j % 4, 64:w], start=False,
                                                          stop=closes, skip_group_check=True)
                                else:
                                    mm = nc.tensor.matmul(o[:], v[:, k, kt], a[:, j % 4], start=opens, stop=closes,
                                                          skip_group_check=True)
                            mm.then_inc(pv_done, 1)
                        turn(CH - 1)
                        pe.sem_inc(h_free, 1)


NG = 5
def stage_gates(nc, d):
    with ExitStack() as stack:
        st = Stage(nc, "G", stack)
        ident = st.sb("ident", [P, P])
        gi = st.sb("gi", [P, NT, 2 * MLH])
        ir = st.sb("ir", [MLH, S])
        fr = st.sb("fr", [MLH, S])
        t0 = st.sb("t0", [MLH, S])
        one = st.sb("one", [MLH, S])
        b = st.sb("b", [MLH, S])
        g = st.sb("g", [MLH, S])
        ends = st.sb("ends", [MLH, NT + 1, P])
        col = st.sb("col", [P, 3, NT, MLH])
        ge = st.sb("ge", [P, NT + 1, MLH])
        out = st.sb("out", [P, NT, NG, MLH])
        ps = st.ps("ps", [P, 2, 2048])
        loaded = st.sem("loaded")
        t_done = st.sem("t_done")
        step = st.sem("step")
        act_step = st.sem("act_step")
        rows_ready = st.sem("rows_ready")
        c_done = st.sem("c_done")
        args_ready = st.sem("args_ready")
        done = st.sem("done")
        stored = st.sem("stored")
        with nc.Block() as block:

            @block.sync
            def _(sp):
                sp.dma_start(ident[:], d["ident"]).then_inc(loaded, 16)
                sp.dma_start(gi[:], d["gi"].rearrange("(t p) c -> p t c", p=P)).then_inc(loaded, 16)
                sp.wait_ge(rows_ready, 1)
                sp.dma_start(d["G"], g[:]).then_inc(stored, 16)
                sp.wait_ge(done, 1)
                sp.dma_start(d["gcols"].rearrange("(t p) c -> p t c", p=P), out[:].rearrange("p t a h -> p t (a h)")).then_inc(stored, 16)
                sp.wait_ge(stored, 32)

            @block.tensor
            def _(pe):
                pe.wait_ge(loaded, 32)
                for a in range(2):
                    for t in range(NT):
                        mm = nc.tensor.transpose(ps[0:MLH, a, t * P:(t + 1) * P], gi[:, t, a * MLH:(a + 1) * MLH], ident[:])
                mm.then_inc(t_done, 1)
                pe.wait_ge(rows_ready, 1)
                for a, src in enumerate((ir, b, g)):
                    for t in range(NT):
                        nc.tensor.transpose(ps[:, 0, (a * NT + t) * MLH:(a * NT + t + 1) * MLH], src[:, t * P:(t + 1) * P],
                                            ident[0:MLH, 0:MLH])
                for t in range(NT + 1):
                    mm = nc.tensor.matmul(ps[:, 1, t * MLH:(t + 1) * MLH], ends[:, t], ident[0:MLH, 0:MLH], start=True, stop=True)
                mm.then_inc(c_done, 1)

            @block.scalar
            def _(act):
                nc.scalar.preload_act_table_set("natural_log_exp_and_others")
                chain = Chain(act, act_step)
                act.wait_ge(step, 4)
                chain.link(nc.scalar.activation(t0[:], t0[:], ACT.Exp, scale=-1.0))
                chain.link(nc.scalar.activation(t0[:], t0[:], ACT.Ln, bias=1.0))
                act.wait_ge(args_ready, 1)
                nc.scalar.activation(out[:, :, 1:NG].rearrange("p t a h -> p t (a h)"),
                                     out[:, :, 1:NG].rearrange("p t a h -> p t (a h)"), ACT.Exp).then_inc(done, 1)

            @block.vector
            def _(dve):
                chain = Chain(dve, step)
                nc.vector.memset(one[:], 1.0)
                chain.link(nc.vector.memset(ends[:], 0.0))
                dve.wait_ge(t_done, 1)
                chain.link(nc.vector.tensor_copy(ir[:], ps[0:MLH, 0]))
                chain.link(nc.vector.tensor_copy(fr[:], ps[0:MLH, 1]))
                chain.link(nc.vector.scalar_tensor_tensor(t0[:], fr[:], -1.0, fr[:], ALU.mult, ALU.max))
                chain.link(nc.vector.tensor_scalar(fr[:], fr[:], 0.0, None, ALU.min))
                dve.wait_ge(act_step, 2)
                chain.link(nc.vector.tensor_tensor(fr[:], fr[:], t0[:], ALU.subtract))
                chain.link(nc.vector.tensor_tensor_scan(b[:], one[:], fr[:], 0.0, ALU.mult, ALU.add))
                chain.link(nc.vector.tensor_tensor(ir[:], ir[:], b[:], ALU.subtract))
                chain.link(nc.vector.tensor_tensor_scan(g[:], ir[:], ir[:], 0.0, ALU.max, ALU.max))
                nc.vector.tensor_copy(ends[:, 1:NT + 1], g[:].rearrange("h (t p) -> h t p", p=P)[:, :, P - 1:P].to_broadcast([MLH, NT, P])).then_inc(rows_ready, 1)
                dve.wait_ge(c_done, 1)
                nc.vector.tensor_copy(col[:].rearrange("p a t h -> p (a t h)"), ps[:, 0, 0:3 * NT * MLH])
                chain.link(nc.vector.tensor_copy(ge[:].rearrange("p t h -> p (t h)"), ps[:, 1, 0:(NT + 1) * MLH]))
                a_, b_, g_ = (col[:, q] for q in range(3))
                nc.vector.tensor_copy(out[:, :, 0], a_)
                nc.vector.tensor_tensor(out[:, :, 1], ge[:, 0:NT], g_, ALU.subtract)
                nc.vector.tensor_tensor(out[:, :, 2], a_, ge[:, 1:NT + 1], ALU.subtract)
                nc.vector.tensor_tensor(out[:, :, 3], ge[:, 0:NT], ge[:, 1:NT + 1], ALU.subtract)
                chain.link(nc.vector.scalar_tensor_tensor(out[:, :, 4], b_, -1.0, g_, ALU.mult, ALU.subtract))
                nc.vector.tensor_scalar(out[:, :, 4], out[:, :, 4], 88.0, None, ALU.min).then_inc(args_ready, 1)


def stage_mlstm(nc, d):
    V1 = MLD + 1
    with ExitStack() as stack:
        st = Stage(nc, "L", stack)
        ident = st.sb("ident", [P, P])
        mask = st.sb("mask", [P, P])
        eps = st.sb("eps", [P, 1])
        wts = st.sb("wts", [P, 3, MLH, MLD])
        cw = st.sb("cw", [P, CONV, ML])
        cb = st.sb("cb", [P, ML])
        hg = st.sb("hg", [P, ML])
        sk = st.sb("sk", [P, ML])
        xs = st.sb("xs", [P, 2, CONV, ML])
        gb = st.sb("gb", [P, 2, MLH, P])
        z = st.sb("z", [P, 2, ML])
        gc = st.sb("gc", [P, NT, NG * MLH])
        ct = st.sb("ct", [P, CONV, ML])
        cx = st.sb("cx", [P, ML])
        xe = st.sb("xe", [P, ML])
        xc = st.sb("xc", [P, 2, ML])
        xcT = st.sb("xcT", [P, MLH, P])
        xmT = st.sb("xmT", [P, MLH, P])
        mq = st.sb("mq", [P, MLH, P])
        mk = st.sb("mk", [P, MLH, P])
        kw = st.sb("kw", [P, MLH, MLD])
        v1 = st.sb("v1", [P, MLH, V1])
        w = st.sb("w", [P, 2, MLH, P])
        pr = st.sb("pr", [P, MLH, P])
        cst = st.sb("cst", [P, MLH, V1])
        ni = st.sb("ni", [P, MLH, V1])
        den = st.sb("den", [P, MLH])
        hh = st.sb("hh", [P, 2, MLH, MLD])
        hs = st.sb("hs", [P, MLH, MLD])
        hst = st.sb("hst", [P, 4, MLH])
        xk = st.sb("xk", [P, ML])
        o = st.sb("o", [P, 2, ML])
        psA, psB, psC, psD = (st.ps(f"ps{q}", [P, MLH, P]) for q in "ABCD")
        psI = st.ps("psI", [P, 2, 512])
        psU = st.ps("psU", [P, 2, 512])
        psN = [psC, psD]

        def pair(ps, b):
            return ps[:, b, 0:2 * V1].rearrange("p (h c) -> p h c", c=V1)

        def pair_n(b):
            return psN[b][:].rearrange("p h c -> p (h c)")[:, 0:2 * V1].rearrange("p (h c) -> p h c", c=V1)

        c_loaded = st.sem("c_loaded")
        set_done = st.sem("set_done")
        w_ready = st.sem("w_ready")
        loaded = [st.sem(f"loaded{k}") for k in range(2)]
        z_loaded = [st.sem(f"z_loaded{k}") for k in range(2)]
        in_free = st.sem("in_free")
        cx_ready = st.sem("cx_ready")
        pool_step = st.sem("pool_step")
        act_step = st.sem("act_step")
        xe_ready = st.sem("xe_ready")
        xc_ready = st.sem("xc_ready")
        dm_ready = st.sem("dm_ready")
        w_exp = st.sem("w_exp")
        t_done = st.sem("t_done")
        xT_ready = st.sem("xT_ready")
        qkv_done = st.sem("qkv_done")
        mq_ready = st.sem("mq_ready")
        mk_ready = st.sem("mk_ready")
        kw_ready = st.sem("kw_ready")
        v_ready = st.sem("v_ready")
        qk_done = st.sem("qk_done")
        pr_ready = st.sem("pr_ready")
        n_done = st.sem("n_done")
        u_done = st.sem("u_done")
        c_ready = st.sem("c_ready")
        dve_step = st.sem("dve_step")
        hc_ready = st.sem("hc_ready")
        hv_ready = st.sem("hv_ready")
        hr_ready = st.sem("hr_ready")
        hn_ready = st.sem("hn_ready")
        o_ready = st.sem("o_ready")
        stored = [st.sem(f"stored{k}") for k in range(2)]

        with nc.Block() as block:

            @block.sync
            def _(sp):
                sp.dma_start(ident[:], d["ident"]).then_inc(c_loaded, 16)
                sp.dma_start(mask[:], d["mask_st"]).then_inc(c_loaded, 16)
                for j, name in enumerate(("w_mq_2", "w_mk_2", "w_mv_2")):
                    sp.dma_start(wts[:, j], d[name].rearrange("a h d e -> d (a h) e")).then_inc(c_loaded, 16)
                for j in range(CONV):
                    sp.dma_start(cw[:, j], to_all(d["conv_w_2"][0, j:j + 1])).then_inc(c_loaded, 16)
                sp.dma_start(cb[:], to_all(d["conv_b_2"])).then_inc(c_loaded, 16)
                sp.dma_start(hg[:], to_all(d["mh_norm_g_2"])).then_inc(c_loaded, 16)
                sp.dma_start(sk[:], to_all(d["ml_skip_2"])).then_inc(c_loaded, 16)

                sp.dma_start(gc[:], d["gcols"].rearrange("(t p) c -> p t c", p=P)).then_inc(c_loaded, 16)

                def load(n, k):
                    count, at = ahead(sp, n + 1, n * P)
                    sp.wait_ge(t_done, count)
                    for j in range(CONV):
                        sp.dma_start(xs[:, k, j], d["xm"][bass.ds(n * P + j, P)]).then_inc(loaded[k], 16)
                    g = bass.AP(tensor=d["G"].tensor, offset=0, ap=[[0, P], [S, MLH], [1, S]])[:, :, bass.ds(at, P)]
                    sp.dma_start(gb[:, k], g).then_inc(loaded[k], 16)

                def load_z(n, k):
                    count, = ahead(sp, n + 1)
                    sp.wait_ge(in_free, count)
                    sp.dma_start(z[:, k], d["z"][rows_of(n)]).then_inc(z_loaded[k], 16)

                def store(n, k):
                    count, = ahead(sp, n + 1)
                    sp.wait_ge(o_ready, count)
                    sp.dma_start(d["mlo"][rows_of(n)], o[:, k]).then_inc(stored[k], 16)

                for k in range(2):
                    load(k, k)
                    load_z(k, k)
                with sp.Fori(0, NT // 2 - 1) as i:
                    for k in range(2):
                        load(2 * i + k + 2, k)
                        store(2 * i + k, k)
                        load_z(2 * i + k + 2, k)
                for k in range(2):
                    store(NT - 2 + k, k)
                for k in range(2):
                    sp.wait_ge(stored[k], 16 * (NT // 2 + 1))

            @block.gpsimd
            def _(pool):
                chain = Chain(pool, pool_step)
                for k in range(2):
                    pool.sem_inc(stored[k], 16)
                pool.wait_ge(c_loaded, 208)

                def front(n, k, m, first=False):
                    if not first:
                        pool.wait_ge(cx_ready, n)
                    pool.wait_ge(loaded[k], 80 * m)
                    for j in range(CONV):
                        step = nc.gpsimd.tensor_tensor(ct[:, j], xs[:, k, j], cw[:, j], ALU.mult)
                    chain.link(step)
                    nc.gpsimd.tensor_tensor(ct[:, 0], ct[:, 0], ct[:, 1], ALU.add)
                    chain.link(nc.gpsimd.tensor_tensor(ct[:, 2], ct[:, 2], ct[:, 3], ALU.add))
                    chain.link(nc.gpsimd.tensor_tensor(ct[:, 0], ct[:, 0], ct[:, 2], ALU.add))
                    pool.wait_ge(xc_ready, n + 1)
                    nc.gpsimd.tensor_tensor(cx[:], ct[:, 0], cb[:], ALU.add).then_inc(cx_ready, 1)

                def tail(n, k, m):
                    pool.wait_ge(xc_ready, n + 2)
                    chain.link(nc.gpsimd.tensor_tensor(xk[:], xc[:, k], sk[:], ALU.mult))
                    pool.wait_ge(hn_ready, n + 1)
                    pool.wait_ge(stored[k], 16 * m)
                    flat = hh[:, k].rearrange("p h c -> p (h c)")
                    chain.link(nc.gpsimd.tensor_tensor(o[:, k], flat, hg[:], ALU.mult))
                    chain.link(nc.gpsimd.tensor_tensor(o[:, k], o[:, k], xk[:], ALU.add))
                    pool.wait_ge(z_loaded[k], 16 * m)
                    nc.gpsimd.tensor_tensor(o[:, k], o[:, k], z[:, k], ALU.mult).then_inc(o_ready, 1)
                    pool.wait_ge(o_ready, n + 1)
                    pool.sem_inc(in_free, 1)

                front(0, 0, 1, first=True)
                with pool.Fori(0, NT // 2 - 1) as i:
                    chain.at(12 * i + 3)
                    front(2 * i + 1, 1, i + 1)
                    tail(2 * i, 0, i + 1)
                    front(2 * i + 2, 0, i + 2)
                    tail(2 * i + 1, 1, i + 1)
                    assert chain.n == 12
                chain.at(6 * NT - 12 + 3)
                front(NT - 1, 1, NT // 2)
                tail(NT - 2, 0, NT // 2)
                tail(NT - 1, 1, NT // 2)

            @block.scalar
            def _(act):
                nc.scalar.preload_act_table_set("natural_log_exp_and_others")
                chain = Chain(act, act_step)
                act.wait_ge(set_done, 1)

                def front(n, k):
                    act.wait_ge(dm_ready, n + 1)
                    nc.scalar.activation(w[:, k], w[:, k], ACT.Exp).then_inc(w_exp, 1)
                    act.wait_ge(cx_ready, n + 1)
                    chain.link(nc.scalar.activation(xe[:], cx[:], ACT.Exp, scale=-1.0))
                    chain.link(nc.scalar.activation(xe[:], xe[:], ACT.Ln, bias=1.0))
                    nc.scalar.activation(xe[:], xe[:], ACT.Exp, scale=-1.0).then_inc(xe_ready, 1)

                def turned(n):
                    act.wait_ge(t_done, n + 3)
                    nc.scalar.copy(xmT[:], psB[:])
                    nc.scalar.copy(xcT[:], psA[:]).then_inc(xT_ready, 1)

                def copies(n):
                    act.wait_ge(qkv_done, n + 1)
                    nc.scalar.copy(mq[:], psC[:]).then_inc(mq_ready, 1)
                    nc.scalar.copy(v1[:, :, 0:MLD], psI[:, 1].rearrange("p (h c) -> p h c", c=MLD)).then_inc(v_ready, 1)

                def norm(n, k):
                    act.wait_ge(hc_ready, n + 1)
                    nc.scalar.activation(hs[:], hh[:, k], ACT.Square).then_inc(hv_ready, 1)
                    act.wait_ge(hv_ready, 2 * n + 2)
                    chain.link(nc.scalar.activation(hst[:, 2], hst[:, 1], ACT.Ln, scale=1.0 / MLD, bias=eps[:, 0:1]))
                    nc.scalar.activation(hst[:, 3], hst[:, 2], ACT.Exp, scale=-0.5).then_inc(hr_ready, 1)

                def step(n, k):
                    copies(n)
                    front(n + 1, 1 - k)
                    turned(n + 1)
                    norm(n, k)

                front(0, 0)
                turned(0)
                with act.Fori(0, NT // 2 - 1) as i:
                    chain.at(6 * i + 2)
                    for k in range(2):
                        step(2 * i + k, k)
                    assert chain.n == 6
                chain.at(3 * NT - 6 + 2)
                step(NT - 2, 0)
                copies(NT - 1)
                norm(NT - 1, 1)

            @block.vector
            def _(dve):
                chain = Chain(dve, dve_step)
                nc.vector.memset(v1[:], 1.0)
                nc.vector.memset(cst[:], 0.0)
                nc.vector.memset(eps[:], EPS).then_inc(set_done, 1)
                dve.sem_inc(in_free, 2)
                dve.sem_inc(xc_ready, 1)
                dve.sem_inc(c_ready, 1)
                dve.wait_ge(c_loaded, 208)
                nc.vector.tensor_scalar(wts[:, 1], wts[:, 1], MLD ** -0.5, None, ALU.mult).then_inc(w_ready, 1)

                def head(n, q):
                    return gc[:, bass.ds(n, 1), q * MLH:(q + 1) * MLH].rearrange("p a h -> p h a")

                def exponents(n, k, m):
                    dve.wait_ge(loaded[k], 80 * m)
                    chain.link(nc.vector.tensor_tensor(w[:, k], head(n, 0).to_broadcast([P, MLH, P]), gb[:, k], ALU.subtract))
                    nc.vector.scalar_tensor_tensor(w[:, k], w[:, k], 0.0, mask[:].unsqueeze(1).to_broadcast([P, MLH, P]),
                                                   ALU.min, ALU.add).then_inc(dm_ready, 1)

                def convolved(n, k):
                    dve.wait_ge(xe_ready, n + 1)
                    nc.vector.tensor_tensor(xc[:, k], cx[:], xe[:], ALU.mult).then_inc(xc_ready, 1)

                def copies(n, k):
                    dve.wait_ge(qkv_done, n + 1)
                    nc.vector.tensor_copy(mk[:], psD[:]).then_inc(mk_ready, 1)
                    nc.vector.tensor_tensor(kw[:], psI[:, 0].rearrange("p (h c) -> p h c", c=MLD),
                                            head(n, 2).to_broadcast([P, MLH, MLD]), ALU.mult).then_inc(kw_ready, 1)

                def within(n, k):
                    dve.wait_ge(qk_done, n + 1)
                    dve.wait_ge(w_exp, n + 1)
                    nc.vector.tensor_tensor(pr[:], psA[:], w[:, k], ALU.mult).then_inc(pr_ready, 1)

                def state(n, k):
                    dve.wait_ge(n_done, n + 1)
                    for b in range(2):
                        step = nc.vector.tensor_tensor(ni[:, 2 * b:2 * b + 2], pair(psI, b),
                                                       head(n, 1)[:, 2 * b:2 * b + 2].to_broadcast([P, 2, V1]), ALU.mult)
                    chain.link(step)
                    for b in range(2):
                        step = nc.vector.tensor_tensor(ni[:, 2 * b:2 * b + 2], pair_n(b), ni[:, 2 * b:2 * b + 2], ALU.add)
                    chain.link(step)
                    dve.wait_ge(u_done, n + 1)
                    chain.link(nc.vector.tensor_tensor(cst[:], cst[:], head(n, 3).to_broadcast([P, MLH, V1]), ALU.mult))
                    for b in range(2):
                        step = nc.vector.tensor_tensor(cst[:, 2 * b:2 * b + 2], pair(psU, b), cst[:, 2 * b:2 * b + 2], ALU.add)
                    step.then_inc(c_ready, 1)

                def norm(n, k):
                    chain.link(nc.vector.scalar_tensor_tensor(den[:], ni[:, :, MLD], -1.0, ni[:, :, MLD], ALU.mult, ALU.max))
                    chain.link(nc.vector.tensor_tensor(den[:].unsqueeze(2), den[:].unsqueeze(2), head(n, 4), ALU.max))
                    chain.link(nc.vector.reciprocal(den[:], den[:]))
                    dve.wait_ge(in_free, n + 1)
                    chain.link(nc.vector.tensor_tensor(hh[:, k], ni[:, :, 0:MLD], den[:].unsqueeze(2).to_broadcast([P, MLH, MLD]), ALU.mult))
                    chain.link(nc.vector.reduce_sum(hst[:, 0], hh[:, k], AX_X))
                    chain.link(nc.vector.tensor_scalar(hst[:, 0], hst[:, 0], 1.0 / MLD, None, ALU.mult))
                    chain.link(nc.vector.tensor_tensor(hh[:, k], hh[:, k], hst[:, 0].unsqueeze(2).to_broadcast([P, MLH, MLD]), ALU.subtract))
                    dve.sem_inc(hc_ready, 1)

                def normed(n, k):
                    dve.wait_ge(hv_ready, 2 * n + 1)
                    nc.vector.reduce_sum(hst[:, 1], hs[:], AX_X).then_inc(hv_ready, 1)
                    dve.wait_ge(hr_ready, n + 1)
                    nc.vector.tensor_tensor(hh[:, k], hh[:, k], hst[:, 3].unsqueeze(2).to_broadcast([P, MLH, MLD]), ALU.mult).then_inc(hn_ready, 1)

                def step_of(n, k, m_next):
                    copies(n, k)
                    exponents(n + 1, 1 - k, m_next)
                    within(n, k)
                    state(n, k)
                    convolved(n + 1, 1 - k)
                    norm(n, k)
                    normed(n, k)

                exponents(0, 0, 1)
                convolved(0, 0)
                with dve.Fori(0, NT // 2 - 1) as i:
                    chain.at(22 * i + 1)
                    step_of(2 * i, 0, i + 1)
                    step_of(2 * i + 1, 1, i + 2)
                    assert chain.n == 22, chain.n
                chain.at(11 * NT - 22 + 1)
                step_of(NT - 2, 0, NT // 2)
                copies(NT - 1, 1)
                within(NT - 1, 1)
                state(NT - 1, 1)
                norm(NT - 1, 1)
                normed(NT - 1, 1)

            @block.tensor
            def _(pe):
                pe.wait_ge(c_loaded, 208)
                pe.wait_ge(w_ready, 1)
                pe.sem_inc(t_done, 2)
                with pe.Fori(0, NT // 2) as i:
                    for k in range(2):
                        n = 2 * i + k
                        pe.wait_ge(xc_ready, n + 2)
                        for h in range(MLH):
                            nc.tensor.transpose(psB[:, h], xs[:, k, CONV - 1, h * P:(h + 1) * P], ident[:])
                        for h in range(MLH):
                            t = nc.tensor.transpose(psA[:, h], xc[:, k, h * P:(h + 1) * P], ident[:])
                        t.then_inc(t_done, 1)
                        pe.wait_ge(xT_ready, n + 1)
                        pe.wait_ge(c_ready, n + 1)
                        for h in range(MLH):
                            nc.tensor.matmul(psC[:, h], wts[:, 0, h], xcT[:, h], start=True, stop=True)
                            nc.tensor.matmul(psD[:, h], wts[:, 1, h], xcT[:, h], start=True, stop=True)
                            nc.tensor.matmul(psI[:, 0, h * P:(h + 1) * P], xcT[:, h], wts[:, 1, h], start=True, stop=True)
                            mm = nc.tensor.matmul(psI[:, 1, h * P:(h + 1) * P], xmT[:, h], wts[:, 2, h], start=True, stop=True)
                        mm.then_inc(qkv_done, 1)
                        pe.wait_ge(mq_ready, n + 1)
                        pe.wait_ge(mk_ready, n + 1)
                        for h in range(MLH):
                            mm = nc.tensor.matmul(psA[:, h], mk[:, h], mq[:, h], start=True, stop=True)
                        mm.then_inc(qk_done, 1)
                        pe.wait_ge(kw_ready, n + 1)
                        pe.wait_ge(v_ready, n + 1)
                        for h in range(MLH):
                            nc.tensor.matmul(pair(psI, h // 2)[:, h % 2], mq[:, h], cst[:, h], start=True, stop=True)
                        for h in range(MLH):
                            mm = nc.tensor.matmul(pair(psU, h // 2)[:, h % 2], kw[:, h], v1[:, h], start=True, stop=True)
                        mm.then_inc(u_done, 1)
                        pe.wait_ge(pr_ready, n + 1)
                        for h in range(MLH):
                            mm = nc.tensor.matmul(pair_n(h // 2)[:, h % 2], pr[:, h], v1[:, h], start=True, stop=True)
                        mm.then_inc(n_done, 1)


def stage_route(nc, d):
    NL = GRP + NE
    BIG = 1e30
    ROUND = 1.5 * 2 ** 23
    with ExitStack() as stack:
        st = Stage(nc, "T", stack)
        ident = st.sb("ident", [P, P])
        tri = st.sb("tri", [P, P])
        ones = st.sb("ones", [P, P])
        wr = st.sb("wr", [P, KD, NL])
        br = st.sb("br", [P, NL])
        io = st.sb("io", [P, 2, NE])
        iob = st.sb("iob", [P, NBLK])
        pcol = st.sb("pcol", [P, 1])
        tok = st.sb("tok", [P, NT], I32)
        x = st.sb("x", [P, 2, D])
        xT = st.sb("xT", [P, 2, KD, P])
        lg = st.sb("lg", [P, NE])
        g8 = st.sb("g8", [P, 8])
        gm = st.sb("gm", [P, 8])
        gidx = st.sb("gidx", [P, 8], U32)
        gf = st.sb("gf", [P, 8])
        gneg = st.sb("gneg", [P, 1])
        ge = st.sb("ge", [P, GRP])
        gs = st.sb("gs", [P, 4])
        sel = st.sb("sel", [P, NE])
        pen = st.sb("pen", [P, NE])
        em = st.sb("em", [P, NE])
        spare = st.sb("spare", [P, 1])
        e8 = st.sb("e8", [P, 8])
        eidx = st.sb("eidx", [P, 8], U32)
        ef = st.sb("ef", [P, 8])
        tw = st.sb("tw", [P, 4])
        oh = st.sb("oh", [P, NT, 2, NE])
        both = st.sb("both", [P, NE])
        acc = st.sb("acc", [P, NE])
        prod = st.sb("prod", [P, 2, NE])
        rank = st.sb("rank", [P, NT, 2])
        wts = st.sb("wts", [P, NT, 2])
        nb = st.sb("nb", [P, NE])
        one = st.sb("one", [P, NE])
        ends = st.sb("ends", [P, NE])
        cmp = st.sb("cmp", [P, NBLK, NE])
        be = st.sb("be", [P, NBLK])
        wi = st.sb("wi", [P, NBLK], I32)
        big = st.sb("big", [P, NT, 2, NE])
        dest = st.sb("dest", [P, NT, 2])
        desti = st.sb("desti", [P, NT, 2], I32)
        db = st.sb("db", [P, NT, 2])
        addr = st.sb("addr", [P, NT, 2], I32)
        zero = st.sb("zero", [P, NBLK], I32)
        psT = st.ps("psT", [P, KD, P])
        psL = [st.ps(f"psL{k}", [P, 512]) for k in range(2)]
        psR = st.ps("psR", [P, 512])
        c_loaded = st.sem("c_loaded")
        loaded = [st.sem(f"loaded{k}") for k in range(2)]
        in_free = st.sem("in_free")
        t_done = st.sem("t_done")
        xT_ready = st.sem("xT_ready")
        l_done = st.sem("l_done")
        set_done = st.sem("set_done")
        step = st.sem("step")
        act_in = st.sem("act_in")
        act_out = st.sem("act_out")
        both_ready = st.sem("both_ready")
        r_done = st.sem("r_done")
        acc_ready = st.sem("acc_ready")
        addr_ready = st.sem("addr_ready")
        zero_stored = st.sem("zero_stored")
        scattered = st.sem("scattered")
        stored = st.sem("stored")
        with nc.Block() as block:

            @block.sync
            def _(sp):
                for name, t in (("ident", ident), ("tri", tri), ("ones", ones), ("iota_e", io), ("iota_b", iob), ("iota_p", pcol), ("tokens", tok)):
                    sp.dma_start(t[:], d[name]).then_inc(c_loaded, 16)
                sp.dma_start(wr[:, :, 0:GRP], d["w_router_group_2"].rearrange("a (k p) n -> p (a k) n", p=P)).then_inc(c_loaded, 16)
                sp.dma_start(wr[:, :, GRP:NL], d["w_router_expert_2"].rearrange("a (k p) n -> p (a k) n", p=P)).then_inc(c_loaded, 16)
                sp.dma_start(br[:, 0:GRP], to_all(d["b_router_group_2"])).then_inc(c_loaded, 16)
                sp.dma_start(br[:, GRP:NL], to_all(d["b_router_expert_2"])).then_inc(c_loaded, 16)
                sp.wait_ge(set_done, 1)
                sp.dma_start(d["rowtok"], zero[:]).then_inc(zero_stored, 16)
                with sp.Fori(0, NT // 2) as i:
                    for k in range(2):
                        count, at = ahead(sp, 2 * i + k + 1, (2 * i + k) * P)
                        sp.wait_ge(in_free, count)
                        sp.dma_start(x[:, k], d["hf"][bass.ds(at, P)]).then_inc(loaded[k], 16)
                sp.wait_ge(addr_ready, 1)
                sp.dma_start(d["widx"], wi[:]).then_inc(stored, 16)
                sp.dma_start(d["dest"], desti[:].rearrange("p t k -> p (t k)")).then_inc(stored, 16)
                sp.dma_start(d["wts"], wts[:].rearrange("p t k -> p (t k)")).then_inc(stored, 16)
                sp.wait_ge(stored, 48)

            @block.gpsimd
            def _(pool):
                pool.wait_ge(zero_stored, 16)
                pool.wait_ge(addr_ready, 1)
                table = d["rowtok"].rearrange("p (b a) -> (p b) a", a=1)
                for t in range(NT):
                    for k in range(2):
                        pool.indirect_dma_start(table, bass.IndirectOffsetOnAxis(addr[:, t, k:k + 1], 0), tok[:, t:t + 1], None).then_inc(scattered, 16)
                pool.wait_ge(scattered, 16 * 2 * NT)

            @block.tensor
            def _(pe):
                pe.sem_inc(in_free, 2)
                pe.wait_ge(c_loaded, 176)
                pe.wait_ge(set_done, 1)

                def logits(n, k, m):
                    pe.wait_ge(loaded[k], 16 * m)
                    for kd in range(KD):
                        t = nc.tensor.transpose(psT[:, kd], x[:, k, kd * P:(kd + 1) * P], ident[:])
                    t.then_inc(t_done, 1)
                    pe.wait_ge(t_done, n + 1)
                    pe.sem_inc(in_free, 1)
                    pe.wait_ge(xT_ready, n + 1)
                    for kd in range(KD):
                        mm = nc.tensor.matmul(psL[k][:, 0:NL], xT[:, k, kd], wr[:, kd], start=(kd == 0), stop=(kd == KD - 1))
                    mm.then_inc(l_done, 1)

                def ranks(n):
                    pe.wait_ge(both_ready, n + 1)
                    nc.tensor.matmul(psR[:, 0:NE], tri[:], both[:], start=True, stop=False)
                    nc.tensor.matmul(psR[:, 0:NE], ones[:], acc[:], start=False, stop=True).then_inc(r_done, 1)

                logits(0, 0, 1)
                with pe.Fori(0, NT // 2 - 1) as i:
                    logits(2 * i + 1, 1, i + 1)
                    ranks(2 * i)
                    logits(2 * i + 2, 0, i + 2)
                    ranks(2 * i + 1)
                logits(NT - 1, 1, NT // 2)
                ranks(NT - 2)
                ranks(NT - 1)
                pe.wait_ge(acc_ready, NT)
                nc.tensor.matmul(psR[:, 0:NE], ones[:], acc[:], start=True, stop=True).then_inc(r_done, 1)

            @block.scalar
            def _(act):
                nc.scalar.preload_act_table_set("natural_log_exp_and_others")

                def turned(n, k):
                    act.wait_ge(t_done, n + 1)
                    nc.scalar.copy(xT[:, k], psT[:]).then_inc(xT_ready, 1)

                def exps(n):
                    act.wait_ge(act_in, n + 1)
                    nc.scalar.activation(ge[:], g8[:, 0:GRP], ACT.Exp, bias=gneg[:, 0:1], accum_out=gs[:, 0:1])
                    nc.scalar.activation(tw[:, 1:2], tw[:, 0:1], ACT.Exp).then_inc(act_out, 1)

                turned(0, 0)
                with act.Fori(0, NT // 2 - 1) as i:
                    for k in range(2):
                        turned(2 * i + k + 1, 1 - k)
                        exps(2 * i + k)
                turned(NT - 1, 1)
                exps(NT - 2)
                exps(NT - 1)

            @block.vector
            def _(dve):
                chain = Chain(dve, step)
                nc.vector.memset(zero[:], 0)
                nc.vector.memset(one[:], 1.0)
                nc.vector.memset(acc[:], 0.0)
                nc.vector.memset(g8[:], -BIG).then_inc(set_done, 1)
                dve.wait_ge(c_loaded, 176)
                LINKS = 19
                with dve.Fori(0, NT // 2) as i:
                    for k in range(2):
                        n = 2 * i + k
                        if k == 0:
                            chain.at(2 * LINKS * i)
                        dve.wait_ge(l_done, n + 1)
                        chain.link(nc.vector.tensor_tensor(g8[:, 0:GRP], psL[k][:, 0:GRP], br[:, 0:GRP], ALU.add))
                        nc.vector.tensor_tensor(lg[:], psL[k][:, GRP:NL], br[:, GRP:NL], ALU.add)
                        chain.link(nc.vector.max(gm[:], g8[:]))
                        nc.vector.tensor_scalar(gneg[:], gm[:, 0:1], -1.0, None, ALU.mult)
                        chain.link(nc.vector.max_index(gidx[:], gm[:], g8[:]))
                        chain.link(nc.vector.tensor_copy(gf[:], gidx[:]))
                        chain.link(nc.vector.tensor_scalar(sel[:], io[:, 1], gf[:, 0:1], None, ALU.is_equal))
                        chain.link(nc.vector.tensor_scalar(pen[:], sel[:], BIG, -BIG, ALU.mult, ALU.add))
                        chain.link(nc.vector.tensor_tensor(em[:], lg[:], sel[:], ALU.mult))
                        chain.link(nc.vector.tensor_tensor(em[:], em[:], pen[:], ALU.add))
                        nc.vector.tensor_copy(spare[:], one[:, 0:1])
                        chain.link(nc.vector.max(e8[:], em[:]))
                        nc.vector.tensor_tensor(tw[:, 0:1], e8[:, 1:2], e8[:, 0:1], ALU.subtract).then_inc(act_in, 1)
                        chain.link(nc.vector.max_index(eidx[:], e8[:], em[:]))
                        chain.link(nc.vector.tensor_copy(ef[:], eidx[:]))
                        for q in range(2):
                            step_ = nc.vector.tensor_scalar(oh[:, bass.ds(n, 1), q], io[:, 0:1], ef[:, q:q + 1], None, ALU.is_equal)
                        chain.link(step_)
                        nc.vector.tensor_tensor(both[:].unsqueeze(1), oh[:, bass.ds(n, 1), 0], oh[:, bass.ds(n, 1), 1], ALU.add).then_inc(both_ready, 1)
                        dve.wait_ge(act_out, n + 1)
                        chain.link(nc.vector.tensor_scalar(tw[:, 2:3], tw[:, 1:2], 1.0, None, ALU.add))
                        chain.link(nc.vector.tensor_tensor(tw[:, 2:3], tw[:, 2:3], gs[:, 0:1], ALU.mult))
                        chain.link(nc.vector.reciprocal(tw[:, 2:3], tw[:, 2:3]))
                        chain.link(nc.vector.tensor_tensor(tw[:, 3:4], tw[:, 2:3], tw[:, 1:2], ALU.mult))
                        nc.vector.tensor_copy(wts[:, bass.ds(n, 1)], tw[:, 2:4].unsqueeze(1))
                        dve.wait_ge(r_done, n + 1)
                        chain.link(nc.vector.tensor_tensor(prod[:].unsqueeze(1), oh[:, bass.ds(n, 1)],
                                                           psR[:, 0:NE].unsqueeze(1).unsqueeze(1).to_broadcast([P, 1, 2, NE]), ALU.mult))
                        chain.link(nc.vector.reduce_sum(rank[:, bass.ds(n, 1)], prod[:].unsqueeze(1), AX_X))
                        chain.link(nc.vector.tensor_tensor(acc[:], acc[:], both[:], ALU.add))
                        dve.sem_inc(acc_ready, 1)
                    assert chain.n == 2 * LINKS, chain.n
                chain.at(LINKS * NT)
                dve.wait_ge(r_done, NT + 1)
                chain.link(nc.vector.tensor_scalar(nb[:], psR[:, 0:NE], 63.5, 1.0 / P, ALU.add, ALU.mult))
                chain.link(nc.vector.tensor_scalar(nb[:], nb[:], ROUND, -ROUND, ALU.add, ALU.add))
                chain.link(nc.vector.tensor_tensor_scan(ends[:], one[:], nb[:], 0.0, ALU.mult, ALU.add))
                chain.link(nc.vector.tensor_tensor(cmp[:], ends[:].unsqueeze(1).to_broadcast([P, NBLK, NE]),
                                                   iob[:].unsqueeze(2).to_broadcast([P, NBLK, NE]), ALU.is_le))
                chain.link(nc.vector.reduce_sum(be[:], cmp[:], AX_X))
                chain.link(nc.vector.tensor_scalar(be[:], be[:], float(NE - 1), float(P), ALU.min, ALU.mult))
                chain.link(nc.vector.tensor_scalar(be[:], be[:], pcol[:, 0:1], None, ALU.add))
                chain.link(nc.vector.tensor_copy(wi[:], be[:]))
                chain.link(nc.vector.tensor_tensor(nb[:], ends[:], nb[:], ALU.subtract))
                chain.link(nc.vector.tensor_scalar(nb[:], nb[:], float(P), None, ALU.mult))
                for q in range(2):
                    step_ = nc.vector.tensor_tensor(big[:, :, q], oh[:, :, q], nb[:].unsqueeze(1).to_broadcast([P, NT, NE]), ALU.mult)
                chain.link(step_)
                chain.link(nc.vector.reduce_sum(dest[:], big[:], AX_X))
                chain.link(nc.vector.tensor_tensor(dest[:], dest[:], rank[:], ALU.add))
                chain.link(nc.vector.tensor_copy(desti[:], dest[:]))
                chain.link(nc.vector.tensor_scalar(db[:], dest[:], -63.5, 1.0 / P, ALU.add, ALU.mult))
                chain.link(nc.vector.tensor_scalar(db[:], db[:], ROUND, -ROUND, ALU.add, ALU.add))
                chain.link(nc.vector.tensor_scalar(dest[:], dest[:], float(NBLK), None, ALU.mult))
                chain.link(nc.vector.scalar_tensor_tensor(dest[:], db[:], -float(P * NBLK - 1), dest[:], ALU.mult, ALU.add))
                nc.vector.tensor_copy(addr[:], dest[:]).then_inc(addr_ready, 1)


def stage_experts(nc, d):
    KE = DE // P
    NB = 4
    with ExitStack() as stack:
        st = Stage(nc, "X", stack)
        ident = st.sb("ident", [P, P])
        rt = st.sb("rt", [P, NBLK], I32)
        none = st.sb("none", [P, 2], I32)
        wi = st.sb("wi", [P, NBLK], I32)
        ix = st.sb("ix", [P, NB, 2], I32)
        x = st.sb("x", [P, NB, D])
        wg = st.sb("wg", [P, NB, KD * DE])
        wu = st.sb("wu", [P, NB, KD * DE])
        wd = st.sb("wd", [P, NB, KE * D])
        xT = st.sb("xT", [P, 2, KD, P])
        se = st.sb("se", [P, DE])
        sg = st.sb("sg", [P, DE])
        a = st.sb("a", [P, DE])
        aT = st.sb("aT", [P, KE, P])
        y = st.sb("y", [P, 2, D])
        psT = st.ps("psT", [P, KD, P])
        psG = [st.ps(f"psG{k}", [P, 2, DE]) for k in range(2)]
        psA = st.ps("psA", [P, KE, P])
        psY = st.ps("psY", [P, D])
        c_loaded = st.sem("c_loaded")
        ix_ready = st.sem("ix_ready")
        none_set = st.sem("none_set")
        x_loaded = [st.sem(f"x_loaded{k}") for k in range(NB)]
        gu_loaded = [st.sem(f"gu_loaded{k}") for k in range(NB)]
        wd_loaded = [st.sem(f"wd_loaded{k}") for k in range(NB)]
        t_done = st.sem("t_done")
        xT_a = st.sem("xT_a")
        xT_v = st.sem("xT_v")
        g_done = st.sem("g_done")
        act_step = st.sem("act_step")
        se_ready = st.sem("se_ready")
        dve_step = st.sem("dve_step")
        a_ready = st.sem("a_ready")
        at_done = st.sem("at_done")
        aT_ready = st.sem("aT_ready")
        y_done = st.sem("y_done")
        y_a = st.sem("y_a")
        y_v = st.sem("y_v")
        stored = [st.sem(f"stored{k}") for k in range(2)]
        views = {
            "wg": d["w_gate_e_2"].rearrange("a e (p k) f -> (a e p) (k f)", p=P),
            "wu": d["w_up_e_2"].rearrange("a e (p k) f -> (a e p) (k f)", p=P),
            "wd": d["w_down_e_2"].rearrange("a e (p k) f -> (a e p) (k f)", p=P),
        }
        with nc.Block() as block:

            @block.gpsimd
            def _(pool):
                nc.gpsimd.memset(none[:], 0).then_inc(none_set, 1)
                pool.wait_ge(none_set, 1)
                pool.wait_ge(c_loaded, 48)

                def load(n, k, free):
                    if free:
                        pool.wait_ge(y_done, n - (NB - 1))
                    nc.gpsimd.tensor_tensor(ix[:, k, 0:1], rt[:, bass.ds(n, 1)], none[:, 0:1], ALU.add)
                    nc.gpsimd.tensor_tensor(ix[:, k, 1:2], wi[:, bass.ds(n, 1)], none[:, 0:1], ALU.add).then_inc(ix_ready, 1)
                    pool.wait_ge(ix_ready, n + 1)
                    nc.gpsimd.tensor_tensor(none[:, 1:2], none[:, 0:1], none[:, 0:1], ALU.add)
                    rows = bass.IndirectOffsetOnAxis(ix[:, k, 0:1], 0)
                    weights = bass.IndirectOffsetOnAxis(ix[:, k, 1:2], 0)
                    pool.indirect_dma_start(x[:, k], None, d["hf"], rows).then_inc(x_loaded[k], 16)
                    pool.indirect_dma_start(wg[:, k], None, views["wg"], weights).then_inc(gu_loaded[k], 16)
                    pool.indirect_dma_start(wu[:, k], None, views["wu"], weights).then_inc(gu_loaded[k], 16)
                    pool.indirect_dma_start(wd[:, k], None, views["wd"], weights).then_inc(wd_loaded[k], 16)

                for k in range(NB):
                    load(k, k, False)
                with pool.Fori(1, NBLK // NB) as i:
                    for k in range(NB):
                        load(NB * i + k, k, True)

            @block.sync
            def _(sp):
                sp.dma_start(ident[:], d["ident"]).then_inc(c_loaded, 16)
                sp.dma_start(rt[:], d["rowtok"]).then_inc(c_loaded, 16)
                sp.dma_start(wi[:], d["widx"]).then_inc(c_loaded, 16)
                with sp.Fori(0, NBLK // 2) as i:
                    for k in range(2):
                        n = 2 * i + k
                        count, at = ahead(sp, n + 2, n * P)
                        sp.wait_ge(y_a, count)
                        sp.wait_ge(y_v, count)
                        sp.dma_start(d["y"][bass.ds(at, P)], y[:, k]).then_inc(stored[k], 16)
                for k in range(2):
                    sp.wait_ge(stored[k], 16 * (NBLK // 2 + 1))

            @block.tensor
            def _(pe):
                pe.wait_ge(c_loaded, 48)

                def turn(n, b, m):
                    pe.wait_ge(x_loaded[b], 16 * m)
                    cols = x[:, b].rearrange("p (c k) -> p k c", k=KD)
                    for kd in range(KD):
                        t = nc.tensor.transpose(psT[:, kd], cols[:, kd], ident[:])
                    t.then_inc(t_done, 1)

                def gate_up(n, b, m):
                    k = b % 2
                    pe.wait_ge(gu_loaded[b], 32 * m)
                    pe.wait_ge(xT_a, n + 1)
                    pe.wait_ge(xT_v, n + 1)
                    for q, w in enumerate((wg, wu)):
                        for kd in range(KD):
                            mm = nc.tensor.matmul(psG[k][:, q], xT[:, k, kd], w[:, b, kd * DE:(kd + 1) * DE],
                                                  start=(kd == 0), stop=(kd == KD - 1))
                    mm.then_inc(g_done, 1)

                def turn_a(n):
                    pe.wait_ge(a_ready, n + 2)
                    cols = a[:].rearrange("p (c j) -> p j c", j=KE)
                    for j in range(KE):
                        t = nc.tensor.transpose(psA[:, j], cols[:, j], ident[:])
                    t.then_inc(at_done, 1)

                def down(n, b, m):
                    pe.wait_ge(wd_loaded[b], 16 * m)
                    pe.wait_ge(y_a, n + 1)
                    pe.wait_ge(y_v, n + 1)
                    pe.wait_ge(aT_ready, n + 1)
                    for half in range(2):
                        for j in range(KE):
                            mm = nc.tensor.matmul(psY[:, half * 512:(half + 1) * 512], aT[:, j],
                                                  wd[:, b, j * D + half * 512:j * D + (half + 1) * 512],
                                                  start=(j == 0), stop=(j == KE - 1))
                    mm.then_inc(y_done, 1)

                def step(n, k, i):
                    left = NBLK - n if isinstance(n, int) else NB
                    turn_a(n)
                    if left > 1:
                        gate_up(n + 1, (k + 1) % NB, i + 1 + (k + 1) // NB)
                    if left > 2:
                        turn(n + 2, (k + 2) % NB, i + 1 + (k + 2) // NB)
                    down(n, k, i + 1)

                turn(0, 0, 1)
                gate_up(0, 0, 1)
                turn(1, 1, 1)
                with pe.Fori(0, NBLK // NB - 1) as i:
                    for k in range(NB):
                        step(NB * i + k, k, i)
                for k in range(NB):
                    step(NBLK - NB + k, k, NBLK // NB - 1)

            @block.scalar
            def _(act):
                nc.scalar.preload_act_table_set("natural_log_exp_and_others")
                chain = Chain(act, act_step)
                for k in range(2):
                    act.sem_inc(stored[k], 16)
                act.sem_inc(y_a, 1)

                def turned(n, k):
                    act.wait_ge(t_done, n + 1)
                    nc.scalar.copy(xT[:, k, KD // 2:KD], psT[:, KD // 2:KD]).then_inc(xT_a, 1)

                def exps(n, k):
                    act.wait_ge(g_done, n + 1)
                    act.wait_ge(a_ready, n + 1)
                    chain.link(nc.scalar.activation(se[:], psG[k][:, 0], ACT.Exp, scale=-1.0))
                    chain.link(nc.scalar.activation(se[:], se[:], ACT.Ln, bias=1.0))
                    nc.scalar.activation(se[:], se[:], ACT.Exp, scale=-1.0).then_inc(se_ready, 1)

                def back(n, k, m):
                    act.wait_ge(y_done, n + 1)
                    act.wait_ge(stored[k], 16 * m)
                    nc.scalar.copy(y[:, k, 0:512], psY[:, 0:512]).then_inc(y_a, 1)

                def step(n, k, m, turns=True):
                    exps(n + 1, 1 - k)
                    if turns:
                        turned(n + 2, k)
                    back(n, k, m)

                turned(0, 0)
                exps(0, 0)
                turned(1, 1)
                with act.Fori(0, NBLK // 2 - 1) as i:
                    chain.at(4 * i + 2)
                    step(2 * i, 0, i + 1)
                    step(2 * i + 1, 1, i + 1)
                chain.at(4 * (NBLK // 2 - 1) + 2)
                step(NBLK - 2, 0, NBLK // 2, turns=False)
                back(NBLK - 1, 1, NBLK // 2)

            @block.vector
            def _(dve):
                chain = Chain(dve, dve_step)
                dve.sem_inc(y_v, 1)
                dve.sem_inc(a_ready, 1)

                def turned(n, k):
                    dve.wait_ge(t_done, n + 1)
                    nc.vector.tensor_copy(xT[:, k, 0:KD // 2], psT[:, 0:KD // 2]).then_inc(xT_v, 1)

                def gated(n, k):
                    dve.wait_ge(se_ready, n + 1)
                    chain.link(nc.vector.tensor_tensor(sg[:], psG[k][:, 0], se[:], ALU.mult))
                    nc.vector.tensor_tensor(a[:], psG[k][:, 1], sg[:], ALU.mult).then_inc(a_ready, 1)

                def a_turned(n):
                    dve.wait_ge(at_done, n + 1)
                    nc.vector.tensor_copy(aT[:], psA[:]).then_inc(aT_ready, 1)

                def evacuate(n, k, m):
                    dve.wait_ge(y_done, n + 1)
                    dve.wait_ge(stored[k], 16 * m)
                    nc.vector.tensor_copy(y[:, k, 512:D], psY[:, 512:D]).then_inc(y_v, 1)

                def step(n, k, m, turns=True):
                    a_turned(n)
                    if turns:
                        turned(n + 2, k)
                    gated(n + 1, 1 - k)
                    evacuate(n, k, m)

                turned(0, 0)
                gated(0, 0)
                turned(1, 1)
                with dve.Fori(0, NBLK // 2 - 1) as i:
                    chain.at(2 * i + 1)
                    step(2 * i, 0, i + 1)
                    step(2 * i + 1, 1, i + 1)
                chain.at(2 * (NBLK // 2 - 1) + 1)
                step(NBLK - 2, 0, NBLK // 2, turns=False)
                a_turned(NBLK - 1)
                evacuate(NBLK - 1, 1, NBLK // 2)


def stage_final(nc, d, out):
    KP = PD // P
    KW = KD + KP
    with ExitStack() as stack:
        st = Stage(nc, "Z", stack)
        ident = st.sb("ident", [P, P])
        eps = st.sb("eps", [P, 1])
        gain = st.sb("gain", [P, KD])
        fg = st.sb("fg", [P, D])
        ws = st.sb("ws", [P, 2, D])
        wh = st.sb("wh", [P, KW, D], F32R)
        wl = st.sb("wl", [P, KW, D], F32R)
        dest = st.sb("dest", [P, 2 * NT], I32)
        none = st.sb("none", [P, 2], I32)
        wts = st.sb("wts", [P, 2 * NT])
        ix = st.sb("ix", [P, 2, 2], I32)
        wc = st.sb("wc", [P, 2, 2])
        x = st.sb("x", [P, 2, D])
        pt = st.sb("pt", [P, 2, PD])
        y = st.sb("y", [P, 2, 2, D])
        x3 = st.sb("x3", [P, 2, D])
        sq = st.sb("sq", [P, D])
        stat = st.sb("stat", [P, 2, 8])
        u = st.sb("u", [P, D])
        uh = st.sb("uh", [P, KD, P], F32R)
        ul = st.sb("ul", [P, KD, P], F32R)
        ph = st.sb("ph", [P, 2, KP, P], F32R)
        pl = st.sb("pl", [P, 2, KP, P], F32R)
        sg = st.sb("sg", [P, D])
        x4 = st.sb("x4", [P, D])
        o = st.sb("o", [P, 2, D])
        psT = st.ps("psT", [P, KD, P])
        psP = st.ps("psP", [P, KP, P])
        psG = [st.ps(f"psG{half}", [P, 512]) for half in range(2)]
        psE = st.ps("psE", [P, D])
        c_loaded = st.sem("c_loaded")
        w_loaded = [st.sem(f"w_loaded{k}") for k in range(2)]
        wh_ready = st.sem("wh_ready")
        wl_ready = st.sem("wl_ready")
        eps_set = st.sem("eps_set")
        loaded = [st.sem(f"loaded{k}") for k in range(2)]
        ix_ready = st.sem("ix_ready")
        none_set = st.sem("none_set")
        y_loaded = [st.sem(f"y_loaded{k}") for k in range(2)]
        dve_step = st.sem("dve_step")
        act_step = st.sem("act_step")
        x3_ready = st.sem("x3_ready")
        u_ready = st.sem("u_ready")
        t_done = st.sem("t_done")
        uh_ready = st.sem("uh_ready")
        ul_ready = st.sem("ul_ready")
        p_ready = st.sem("p_ready")
        g_done = st.sem("g_done")
        e_done = st.sem("e_done")
        l_ready = st.sem("l_ready")
        m_ready = st.sem("m_ready")
        s_ready = st.sem("s_ready")
        x4_ready = st.sem("x4_ready")
        r4_ready = st.sem("r4_ready")
        o_ready = st.sem("o_ready")
        stored = [st.sem(f"stored{k}") for k in range(2)]
        out_rows = out.rearrange("a s m -> (a s) m")
        with nc.Block() as block:

            @block.sync
            def _(sp):
                sp.dma_start(ident[:], d["ident"]).then_inc(c_loaded, 16)
                sp.dma_start(dest[:], d["dest"]).then_inc(c_loaded, 16)
                sp.dma_start(wts[:], d["wts"]).then_inc(c_loaded, 16)
                sp.dma_start(gain[:], d["norm_ple_g_2"].rearrange("a (k p) -> p (a k)", p=P), allow_slow_non_contiguous=True).then_inc(c_loaded, 16)
                sp.dma_start(fg[:], to_all(d["final_g2_row"])).then_inc(c_loaded, 16)

                def load(n, k):
                    count, = ahead(sp, n + 1)
                    sp.wait_ge(t_done, count)
                    sp.dma_start(x[:, k], d["x2"][rows_of(n)]).then_inc(loaded[k], 16)
                    sp.dma_start(pt[:, k], d["p_rows"][rows_of(n)]).then_inc(loaded[k], 16)

                def store(n, k):
                    count, at = ahead(sp, n + 1, n * P)
                    sp.wait_ge(o_ready, count)
                    sp.dma_start(out_rows[bass.ds(at, P)], o[:, k]).then_inc(stored[k], 16)

                for k in range(2):
                    load(k, k)
                for kd in range(KW):
                    if kd >= 2:
                        sp.wait_ge(wl_ready, kd - 1)
                    rows = d["w_ple_gate_2"][0, kd * P:(kd + 1) * P] if kd < KD else d["w_ple_2"][0, (kd - KD) * P:(kd - KD + 1) * P]
                    sp.dma_start(ws[:, kd % 2], rows).then_inc(w_loaded[kd % 2], 16)
                with sp.Fori(0, NT // 2 - 1) as i:
                    for k in range(2):
                        load(2 * i + k + 2, k)
                        store(2 * i + k, k)
                for k in range(2):
                    store(NT - 2 + k, k)
                for k in range(2):
                    sp.wait_ge(stored[k], 16 * (NT // 2 + 1))

            @block.gpsimd
            def _(pool):
                nc.gpsimd.memset(none[:], 0).then_inc(none_set, 1)
                pool.wait_ge(none_set, 1)
                pool.wait_ge(c_loaded, 80)

                def gather(n, k, free):
                    if free:
                        pool.wait_ge(x3_ready, n - 1)
                    nc.gpsimd.tensor_tensor(ix[:, k], dest[:, bass.ds(n * 2, 2)], none[:, 0:1].to_broadcast([P, 2]), ALU.add)
                    nc.gpsimd.tensor_copy(wc[:, k], wts[:, bass.ds(n * 2, 2)]).then_inc(ix_ready, 1)
                    pool.wait_ge(ix_ready, n + 1)
                    nc.gpsimd.tensor_tensor(none[:, 1:2], none[:, 0:1], none[:, 0:1], ALU.add)
                    for q in range(2):
                        pool.indirect_dma_start(y[:, k, q], None, d["y"], bass.IndirectOffsetOnAxis(ix[:, k, q:q + 1], 0)).then_inc(y_loaded[k], 16)

                for k in range(2):
                    gather(k, k, False)
                with pool.Fori(1, NT // 2) as i:
                    for k in range(2):
                        gather(2 * i + k, k, True)

            @block.scalar
            def _(act):
                nc.scalar.preload_act_table_set("natural_log_exp_and_others")
                chain = Chain(act, act_step)
                act.wait_ge(eps_set, 1)
                act.wait_ge(c_loaded, 80)
                for kd in range(KW):
                    act.wait_ge(w_loaded[kd % 2], 16 * (kd // 2) + 16)
                    if kd < KD:
                        nc.scalar.mul(wh[:, kd], ws[:, kd % 2], gain[:, kd:kd + 1]).then_inc(wh_ready, 1)
                    else:
                        nc.scalar.copy(wh[:, kd], ws[:, kd % 2]).then_inc(wh_ready, 1)

                def normed(n, k):
                    act.wait_ge(x3_ready, n + 1)
                    chain.link(nc.scalar.activation(sq[:], x3[:, k], ACT.Square, accum_out=stat[:, k, 0:1]))
                    chain.link(nc.scalar.activation(stat[:, k, 1:2], stat[:, k, 0:1], ACT.Ln, scale=1.0 / D, bias=eps[:, 0:1]))
                    chain.link(nc.scalar.activation(stat[:, k, 2:3], stat[:, k, 1:2], ACT.Exp, scale=-0.5))
                    act.wait_ge(t_done, n + 2)
                    nc.scalar.mul(u[:], x3[:, k], stat[:, k, 2:3]).then_inc(u_ready, 1)

                def turned(n):
                    act.wait_ge(t_done, n + 3)
                    nc.scalar.copy(uh[:], psT[:]).then_inc(uh_ready, 1)

                def sigmoid(n, last=False):
                    for half in range(2):
                        part = sg[:, half * 512:(half + 1) * 512]
                        act.wait_ge(g_done, 2 * n + half + 1)
                        chain.link(nc.scalar.activation(part, psG[half][:], ACT.Abs))
                        if half == 1 and not last:
                            turned(n + 1)
                        chain.link(nc.scalar.activation(part, part, ACT.Exp, scale=-1.0))
                        nc.scalar.activation(part, part, ACT.Ln, bias=1.0).then_inc(l_ready, 1)
                    act.wait_ge(m_ready, 2 * n + 4)
                    nc.scalar.activation(sg[:], sg[:], ACT.Exp).then_inc(s_ready, 1)

                def final(n, k):
                    act.wait_ge(x4_ready, n + 2)
                    chain.link(nc.scalar.activation(sq[:], x4[:], ACT.Square, accum_out=stat[:, k, 4:5]))
                    chain.link(nc.scalar.activation(stat[:, k, 5:6], stat[:, k, 4:5], ACT.Ln, scale=1.0 / D, bias=eps[:, 0:1]))
                    nc.scalar.activation(stat[:, k, 6:7], stat[:, k, 5:6], ACT.Exp, scale=-0.5).then_inc(r4_ready, 1)

                def tile(n, k):
                    normed(n + 1, 1 - k)
                    sigmoid(n)
                    final(n, k)

                LINKS = 9
                normed(0, 0)
                turned(0)
                with act.Fori(0, NT // 2 - 1) as i:
                    chain.at(2 * LINKS * i + 3)
                    tile(2 * i, 0)
                    tile(2 * i + 1, 1)
                    assert chain.n == 2 * LINKS, chain.n
                chain.at(LINKS * (NT - 2) + 3)
                tile(NT - 2, 0)
                sigmoid(NT - 1, last=True)
                final(NT - 1, 1)

            @block.tensor
            def _(pe):
                pe.sem_inc(t_done, 2)
                pe.wait_ge(c_loaded, 80)

                def turn(n, k, m):
                    pe.wait_ge(u_ready, n + 1)
                    pe.wait_ge(loaded[k], 32 * m)
                    for kd in range(KP):
                        nc.tensor.transpose(psP[:, kd], pt[:, k, kd * P:(kd + 1) * P], ident[:])
                    for kd in range(KD):
                        t = nc.tensor.transpose(psT[:, kd], u[:, kd * P:(kd + 1) * P], ident[:])
                    t.then_inc(t_done, 1)

                def tile(n, k, m_next, last=False):
                    pe.wait_ge(uh_ready, n + 1)
                    pe.wait_ge(ul_ready, n + 1)
                    for half in range(2):
                        cols = slice(half * 512, (half + 1) * 512)
                        pe.wait_ge(m_ready, 2 * n + half + 1)
                        for kd in range(KD):
                            nc.tensor.matmul(psG[half][:], uh[:, kd], wh[:, kd, cols], start=(kd == 0), stop=False)
                            nc.tensor.matmul(psG[half][:], uh[:, kd], wl[:, kd, cols], start=False, stop=False)
                            mm = nc.tensor.matmul(psG[half][:], ul[:, kd], wh[:, kd, cols], start=False, stop=(kd == KD - 1))
                        mm.then_inc(g_done, 1)
                    if not last:
                        turn(n + 1, 1 - k, m_next)
                    pe.wait_ge(p_ready, n + 1)
                    pe.wait_ge(x4_ready, n + 1)
                    for half in range(2):
                        cols = slice(half * 512, (half + 1) * 512)
                        for kd in range(KP):
                            nc.tensor.matmul(psE[:, cols], ph[:, k, kd], wh[:, KD + kd, cols], start=(kd == 0), stop=False)
                            nc.tensor.matmul(psE[:, cols], ph[:, k, kd], wl[:, KD + kd, cols], start=False, stop=False)
                            mm = nc.tensor.matmul(psE[:, cols], pl[:, k, kd], wh[:, KD + kd, cols], start=False, stop=(kd == KP - 1))
                    mm.then_inc(e_done, 1)

                turn(0, 0, 1)
                pe.wait_ge(wh_ready, KW)
                pe.wait_ge(wl_ready, KW)
                with pe.Fori(0, NT // 2 - 1) as i:
                    tile(2 * i, 0, i + 1)
                    tile(2 * i + 1, 1, i + 2)
                tile(NT - 2, 0, NT // 2)
                tile(NT - 1, 1, 0, last=True)

            @block.vector
            def _(dve):
                chain = Chain(dve, dve_step)
                nc.vector.memset(eps[:], EPS).then_inc(eps_set, 1)
                dve.sem_inc(x4_ready, 1)
                dve.sem_inc(m_ready, 2)
                for k in range(2):
                    dve.sem_inc(stored[k], 16)
                dve.wait_ge(c_loaded, 80)
                for kd in range(KW):
                    dve.wait_ge(wh_ready, kd + 1)
                    if kd < KD:
                        nc.vector.scalar_tensor_tensor(wl[:, kd], ws[:, kd % 2], gain[:, kd:kd + 1], wh[:, kd],
                                                       ALU.mult, ALU.subtract).then_inc(wl_ready, 1)
                    else:
                        nc.vector.tensor_tensor(wl[:, kd], ws[:, kd % 2], wh[:, kd], ALU.subtract).then_inc(wl_ready, 1)

                def experts(k, m):
                    dve.wait_ge(loaded[k], 32 * m)
                    dve.wait_ge(y_loaded[k], 32 * m)
                    chain.link(nc.vector.scalar_tensor_tensor(x3[:, k], y[:, k, 0], wc[:, k, 0:1], x[:, k], ALU.mult, ALU.add))
                    nc.vector.scalar_tensor_tensor(x3[:, k], y[:, k, 1], wc[:, k, 1:2], x3[:, k], ALU.mult, ALU.add).then_inc(x3_ready, 1)

                def turned(n, k):
                    dve.wait_ge(t_done, n + 3)
                    chain.link(nc.vector.tensor_copy(ph[:, k], psP[:]))
                    nc.vector.tensor_tensor(pl[:, k], psP[:], ph[:, k], ALU.subtract).then_inc(p_ready, 1)
                    dve.wait_ge(uh_ready, n + 1)
                    nc.vector.tensor_tensor(ul[:], psT[:], uh[:], ALU.subtract).then_inc(ul_ready, 1)

                def exponent(n, half):
                    part = sg[:, half * 512:(half + 1) * 512]
                    dve.wait_ge(l_ready, 2 * n + half + 1)
                    nc.vector.scalar_tensor_tensor(part, psG[half][:], 0.0, part, ALU.min, ALU.subtract).then_inc(m_ready, 1)

                def final(n, k, m):
                    dve.wait_ge(e_done, n + 1)
                    dve.wait_ge(s_ready, n + 1)
                    chain.link(nc.vector.tensor_tensor(x4[:], psE[:], sg[:], ALU.mult))
                    nc.vector.tensor_tensor(x4[:], x4[:], x3[:, k], ALU.add).then_inc(x4_ready, 1)
                    dve.wait_ge(r4_ready, n + 1)
                    dve.wait_ge(stored[k], 16 * m)
                    nc.vector.scalar_tensor_tensor(o[:, k], x4[:], stat[:, k, 6:7], fg[:], ALU.mult, ALU.mult).then_inc(o_ready, 1)

                def tile(n, k, m, m_next):
                    experts(1 - k, m_next)
                    exponent(n, 0)
                    turned(n + 1, 1 - k)
                    exponent(n, 1)
                    final(n, k, m)

                experts(0, 1)
                turned(0, 0)
                with dve.Fori(0, NT // 2 - 1) as i:
                    chain.at(6 * i + 2)
                    tile(2 * i, 0, i + 1, i + 1)
                    tile(2 * i + 1, 1, i + 1, i + 2)
                    assert chain.n == 6, chain.n
                chain.at(3 * (NT - 2) + 2)
                tile(NT - 2, 0, NT // 2, NT // 2)
                for half in range(2):
                    exponent(NT - 1, half)
                final(NT - 1, 1, NT // 2)


def constants():
    c = {"ident": np.eye(P, dtype=np.float32)}
    rows = S // 64
    j = np.arange(S)
    freqs = (1.0 / (np.float32(10000.0) ** (np.arange(16, dtype=np.float32) * 2.0 / 32))).astype(np.float32)
    ang = np.concatenate([(j // 64 - rows // 2).astype(np.float32)[:, None] * freqs,
                          (j % 64 - 32).astype(np.float32)[:, None] * freqs], axis=-1)
    c["rope"] = np.stack([np.cos(ang), np.sin(ang)], axis=1).astype(np.float32)
    c["rope_meta"] = np.stack([np.ones((META, 32)), np.zeros((META, 32))], axis=1).astype(np.float32)
    l, k = np.arange(LF + 1)[:, None], np.arange(1, LF + 1)[None, :]
    turn = 2 * np.pi * ((l * k) % L) / L
    weight = np.where(l == LF, 0.5, 1.0) / np.sqrt(L * HD)
    c["dft_cos"] = (np.cos(turn) * weight).astype(np.float32)
    c["dft_sin"] = (np.sin(turn) * weight).astype(np.float32)
    turn = 2 * np.pi * np.outer(np.arange(HD), np.arange(HD)) / HD
    c["cdsd"] = np.stack([np.kron(np.eye(2), np.cos(turn)), np.kron(np.eye(2), np.sin(turn))], axis=1).astype(np.float32)
    p = np.arange(P)[:, None]
    c["fourier_back_in"] = np.minimum(L - 1, np.maximum(0, L - (P * np.arange(LF // P + 1)[None, :] + p))).astype(np.int32)
    c["fourier_back_out"] = np.maximum(0, L - META - (1 + p + np.array([[q * KC + s * P for q in range(NC) for s in range(3)]]))).astype(np.int32)
    c["mask_st"] = np.where(np.arange(P)[:, None] <= np.arange(P)[None, :], 0.0, -1e30).astype(np.float32)
    c["tri"] = (np.arange(P)[:, None] < np.arange(P)[None, :]).astype(np.float32)
    c["ones"] = np.ones((P, P), np.float32)
    e = np.arange(NE)
    c["iota_e"] = np.broadcast_to(np.stack([e, e // (NE // GRP)]).astype(np.float32), (P, 2, NE))
    c["iota_b"] = np.broadcast_to(np.arange(NBLK, dtype=np.float32), (P, NBLK))
    c["iota_p"] = np.arange(P, dtype=np.float32)[:, None]
    c["tokens"] = (P * np.arange(NT)[None, :] + np.arange(P)[:, None]).astype(np.int32)
    c["rope2_inv"] = (1.0 / (np.float32(10000.0) ** (np.arange(0, RD, 2, dtype=np.float32) / np.float32(RD)))).astype(np.float32)[None]
    return c


def scratch(nc, d):
    for name, shape in (("fin", (L, FW)), ("four", (S, FW)), ("negm1", (NQ, S)), ("attn", (S, FW)), ("x1", (S, D)), ("cs2", (S, 32)), ("xm", (S + CONV - 1, ML)), ("lat", (S, QL + KVL + RD)),
                        ("qT2", (MH * QD, S)), ("kT2", (MH * QD, S)), ("v2", (S, MH * VD)), ("negm2", (MH, S)), ("attn2", (S, MH * VD)),
                        ("G", (MLH, S)), ("gcols", (S, NG * MLH)), ("mlo", (S, ML)), ("x2", (S, D)), ("hf", (S, D)),
                        ("y", (NBLK * P, D)), ("wts", (P, 2 * NT)),
                        ("z", (S, ML)), ("gi", (S, 2 * MLH)), ("v", (L, NKV * HD)), ("hT", (NH * HD, L)), ("gates", (S, 2 * FW))):
        d[name] = nc.dram_tensor(name, shape, F32, kind="Internal").ap()
    for name, shape in (("rowtok", (P, NBLK)), ("widx", (P, NBLK)), ("dest", (P, 2 * NT))):
        d[name] = nc.dram_tensor(name, shape, I32, kind="Internal").ap()


def build(nc, d, out):
    scratch(nc, d)
    d["final_g_row"] = d["final_g"].rearrange("(a n) -> a n", a=1)
    stage_project1(nc, d)
    stage_fourier(nc, d)
    stage_max(nc, d, "M1", ("hT", "hT"), NQ, lambda h: NQ * HD + (h // (NQ // NKV)) * HD, HD, L, False, "negm1")
    stage_attention1(nc, d)
    d["x_rows"] = d["x"].rearrange("a s m -> (a s) m")
    stage_output(nc, d, "O1", "four", "attn", "gates", "w_out", "x_rows", "final_g_row", None, "x1")
    stage_rope2(nc, d)
    stage_project2(nc, d)
    stage_mla_heads(nc, d)
    stage_max(nc, d, "M2", ("qT2", "kT2"), MH, lambda h: h * QD, QD, S, True, "negm2")
    stage_attention2(nc, d)
    stage_gates(nc, d)
    stage_mlstm(nc, d)
    stage_output(nc, d, "O2", "attn2", "mlo", None, "w_o_2", "x1", "norm_ffn_g_2", "x2", "hf")
    stage_route(nc, d)
    stage_experts(nc, d)
    d["final_g2_row"] = d["final_norm_g_2"].rearrange("(a n) -> a n", a=1)
    d["p_rows"] = d["p_2"].rearrange("a b s n -> (a b s) n")
    stage_final(nc, d, out)


def kernel(**inputs):
    import numpy as _np
    import concourse.bacc as _bacc
    from concourse import mybir as _mybir
    from concourse.bass_utils import run_bass_kernel_spmd as _run

    nc = _bacc.Bacc("TRN2", target_bir_lowering=False, num_devices=1)
    arrays, d = {}, {}
    for name, a in list(inputs.items()) + list(constants().items()):
        a = _np.ascontiguousarray(a)
        arrays[f"in_{name}"] = a
        d[name] = nc.dram_tensor(f"in_{name}", a.shape, _mybir.dt.from_np(a.dtype), kind="ExternalInput").ap()
    out = nc.dram_tensor("out_0", (1, S, D), F32, kind="ExternalOutput").ap()
    build(nc, d, out)
    return _run(nc, [arrays], core_ids=[0]).results[0]["out_0"]
```
